# Optimizing a Trainium2 kernel written in Bass

```python
import math
import jax, jax.numpy as jnp
from jax import lax
import numpy as np

D_MODEL = 1024
BATCH = 1
SEQ = 512
DEPTH = 2

CHUNK = 64
HEAD_DIM = 64
N_RET = 6
N_SB = 5
N_FOX = 5
W_RET = N_RET * HEAD_DIM
W_SB = N_SB * HEAD_DIM
W_FOX = N_FOX * HEAD_DIM
MIX_WIDTH = W_RET + W_SB + W_FOX
IN_WIDTH = 4 * W_RET + 3 * W_SB + 3 * W_FOX + N_FOX
Q_BLOCK = 128
ROPE_BASE = 10000.0
EPS = 1e-6
N_GROUPS = 4
EXPERTS_PER_GROUP = 8
N_EXPERTS = N_GROUPS * EXPERTS_PER_GROUP
TOP_K = 2
D_EXPERT = 512
MOE_BLOCK = 128

kernel_name = "hybrid_retention_stickbreak_fox_hmoe"

def rmsnorm(x, g):
    xf = x.astype(jnp.float32)
    y = xf * lax.rsqrt(jnp.mean(xf * xf, axis=-1, keepdims=True) + EPS)
    return (y * g.astype(jnp.float32)).astype(x.dtype)

def to_heads(t, n):
    B, S, _ = t.shape
    return t.reshape(B, S, n, HEAD_DIM).transpose(0, 2, 1, 3)

def from_heads(t):
    B, H, S, d = t.shape
    return t.transpose(0, 2, 1, 3).reshape(B, S, H * d)

def rotary(x, pos):
    half = HEAD_DIM // 2
    inv = 1.0 / (ROPE_BASE ** (jnp.arange(half, dtype=jnp.float32) / half))
    ang = pos.astype(jnp.float32)[:, None] * inv[None, :]
    cos = jnp.cos(ang).astype(x.dtype)
    sin = jnp.sin(ang).astype(x.dtype)
    x1, x2 = x[..., :half], x[..., half:]
    return jnp.concatenate([x1 * cos - x2 * sin, x1 * sin + x2 * cos], axis=-1)

def head_group_norm(o, g):
    H, d = o.shape[1], o.shape[3]
    mu = jnp.mean(o, axis=-1, keepdims=True)
    c = o - mu
    var = jnp.mean(c * c, axis=-1, keepdims=True)
    return c * lax.rsqrt(var + EPS) * g.astype(jnp.float32).reshape(1, H, 1, d)

def head_rms_norm(o, g):
    H, d = o.shape[1], o.shape[3]
    return o * lax.rsqrt(jnp.mean(o * o, axis=-1, keepdims=True) + EPS) * g.astype(jnp.float32).reshape(1, H, 1, d)

def retention(q, k, v):
    B, H, S, d = q.shape
    N = S // CHUNK
    f32 = jnp.float32
    qc = q.astype(f32).reshape(B, H, N, CHUNK, d)
    kc = k.astype(f32).reshape(B, H, N, CHUNK, d)
    vc = v.astype(f32).reshape(B, H, N, CHUNK, d)
    log_gamma = jnp.log(1.0 - 2.0 ** (-5.0 - jnp.arange(H, dtype=f32)))
    idx = jnp.arange(CHUNK, dtype=f32)
    intra_decay = jnp.exp(log_gamma[:, None, None] * jnp.abs(idx[:, None] - idx[None, :]))
    q_decay = jnp.exp(log_gamma[:, None] * (idx + 1.0))
    k_decay = jnp.exp(log_gamma[:, None] * (CHUNK - 1.0 - idx))
    chunk_decay = jnp.exp(log_gamma * CHUNK)
    scores = jnp.einsum('bhncd,bhnkd->bhnck', qc, kc) * intra_decay[None, :, None]
    o_intra = jnp.einsum('bhnck,bhnke->bhnce', scores, vc)
    u = jnp.einsum('bhnkd,bhnke->bhnde', kc * k_decay[None, :, None, :, None], vc)

    def step(state, u_n):
        return state * chunk_decay[None, :, None, None] + u_n, state

    _, state_prev = lax.scan(step, jnp.zeros((B, H, d, d), f32), jnp.moveaxis(u, 2, 0))
    state_prev = jnp.moveaxis(state_prev, 0, 2)
    o_cross = jnp.einsum('bhncd,bhnde->bhnce', qc * q_decay[None, :, None, :, None], state_prev)
    return (o_intra + o_cross).reshape(B, H, S, d)

def causal_block_mixers(q_sb, k_sb, v_sb, q_fx, k_fx, v_fx, log_f):
    B, H, S, d = q_sb.shape
    nb = S // Q_BLOCK
    scale = d ** -0.5
    f32 = jnp.float32
    F = jnp.cumsum(log_f.astype(f32), axis=-1)
    key_pos = jnp.arange(S)

    def to_blocks(t):
        return jnp.moveaxis(t.reshape(t.shape[:2] + (nb, Q_BLOCK) + t.shape[3:]), 2, 0)

    def one_block(args):
        i, qs, qf, Fq = args
        q_pos = i * Q_BLOCK + jnp.arange(Q_BLOCK)
        z = jnp.einsum('bhqd,bhkd->bhqk', qs, k_sb).astype(f32) * scale
        strict = key_pos[None, :] < q_pos[:, None]
        log_beta = jax.nn.log_sigmoid(z)
        log_1m = jnp.where(strict, log_beta - z, 0.0)
        between = lax.cumsum(log_1m, axis=3, reverse=True) - log_1m
        a = jnp.where(strict, jnp.exp(log_beta + between), 0.0)
        o_sb = jnp.einsum('bhqk,bhkd->bhqd', a.astype(v_sb.dtype), v_sb).astype(f32)
        logits = jnp.einsum('bhqd,bhkd->bhqk', qf, k_fx).astype(f32) * scale
        logits = logits + Fq[..., :, None] - F[..., None, :]
        causal = key_pos[None, :] <= q_pos[:, None]
        p = jax.nn.softmax(jnp.where(causal, logits, -jnp.inf), axis=-1)
        o_fx = jnp.einsum('bhqk,bhkd->bhqd', p.astype(v_fx.dtype), v_fx).astype(f32)
        return o_sb, o_fx

    o_sb, o_fx = lax.map(one_block, (jnp.arange(nb), to_blocks(q_sb), to_blocks(q_fx), to_blocks(F)))
    o_sb = jnp.moveaxis(o_sb, 0, 2).reshape(B, H, S, d)
    o_fx = jnp.moveaxis(o_fx, 0, 2).reshape(B, H, S, d)
    return o_sb, o_fx

def mixer_block(h, w_in, b_forget, g_ret, g_sb, g_fox, w_out, pos):
    f32 = jnp.float32
    proj = h @ w_in
    sizes = [W_RET] * 4 + [W_SB] * 3 + [W_FOX] * 3 + [N_FOX]
    cuts, acc = [], 0
    for s in sizes[:-1]:
        acc += s
        cuts.append(acc)
    q_r, k_r, v_r, gate_r, q_s, k_s, v_s, q_f, k_f, v_f, f_logit = jnp.split(proj, cuts, axis=-1)
    qr = rotary(to_heads(q_r, N_RET), pos) * (HEAD_DIM ** -0.5)
    kr = rotary(to_heads(k_r, N_RET), pos)
    o_ret = head_group_norm(retention(qr, kr, to_heads(v_r, N_RET)), g_ret)
    o_ret = from_heads(o_ret) * jax.nn.silu(gate_r.astype(f32))
    log_f = jax.nn.log_sigmoid(f_logit.astype(f32) + b_forget.astype(f32)).transpose(0, 2, 1)
    o_sb, o_fx = causal_block_mixers(to_heads(q_s, N_SB), to_heads(k_s, N_SB), to_heads(v_s, N_SB),
                                     to_heads(q_f, N_FOX), to_heads(k_f, N_FOX), to_heads(v_f, N_FOX), log_f)
    o_sb = from_heads(head_rms_norm(o_sb, g_sb))
    o_fx = from_heads(head_rms_norm(o_fx, g_fox))
    merged = jnp.concatenate([o_ret, o_sb, o_fx], axis=-1).astype(h.dtype)
    return merged @ w_out

def hier_moe(h, w_group, b_group, w_router, b_router, w_gate, w_up, w_down):
    B, S, D = h.shape
    T = B * S
    f32 = jnp.float32
    xt = h.reshape(T, D)
    g_logits = (xt @ w_group).astype(f32) + b_group.astype(f32)
    g_prob = jax.nn.softmax(g_logits, axis=-1)
    grp = jnp.argmax(g_logits, axis=-1)
    p_grp = jnp.take_along_axis(g_prob, grp[:, None], axis=-1)
    e_logits = ((xt @ w_router).astype(f32) + b_router.astype(f32)).reshape(T, N_GROUPS, EXPERTS_PER_GROUP)
    e_logits = jnp.take_along_axis(e_logits, grp[:, None, None], axis=1)[:, 0]
    top_val, top_idx = lax.top_k(e_logits, TOP_K)
    gate = jax.nn.softmax(top_val, axis=-1) * p_grp
    expert_id = (grp[:, None] * EXPERTS_PER_GROUP + top_idx).reshape(-1)
    A = T * TOP_K
    order = jnp.argsort(expert_id)
    sorted_e = expert_id[order]
    token_of = order // TOP_K
    gate_sorted = gate.reshape(-1)[order]
    counts = jnp.bincount(expert_id, length=N_EXPERTS)
    start = jnp.cumsum(counts) - counts
    padded = ((counts + MOE_BLOCK - 1) // MOE_BLOCK) * MOE_BLOCK
    padded_end = jnp.cumsum(padded)
    padded_start = padded_end - padded
    dest = padded_start[sorted_e] + (jnp.arange(A) - start[sorted_e])
    P = ((A + MOE_BLOCK - 1) // MOE_BLOCK) * MOE_BLOCK + N_EXPERTS * MOE_BLOCK
    nblk = P // MOE_BLOCK
    buf = jnp.zeros((P, D), h.dtype).at[dest].set(xt[token_of])
    blk_start = jnp.arange(nblk) * MOE_BLOCK
    blk_expert = jnp.minimum(jnp.sum(padded_end[None, :] <= blk_start[:, None], axis=-1), N_EXPERTS - 1)

    def expert_block(args):
        xb, e = args
        hid = jax.nn.silu(xb @ w_gate[e]) * (xb @ w_up[e])
        return hid @ w_down[e]

    ybuf = lax.map(expert_block, (buf.reshape(nblk, MOE_BLOCK, D), blk_expert)).reshape(P, D)
    y = ybuf[dest] * gate_sorted[:, None].astype(ybuf.dtype)
    out = jax.ops.segment_sum(y, token_of, num_segments=T)
    return out.reshape(B, S, D)

def setup_inputs(seed: int = 0) -> dict:
    key = jax.random.key(seed)
    ks = jax.random.split(key, 18)
    L, D = DEPTH, D_MODEL

    def nrm(k, shape, scale):
        return jax.random.normal(k, shape, jnp.float32) * scale

    return {
        "x": nrm(ks[0], (BATCH, SEQ, D), 1.0),
        "norm_mix": 1.0 + nrm(ks[1], (L, D), 0.02),
        "w_in": nrm(ks[2], (L, D, IN_WIDTH), D ** -0.5),
        "b_forget": jax.random.uniform(ks[3], (L, N_FOX), jnp.float32, 1.0, 4.0),
        "g_ret": 1.0 + nrm(ks[4], (L, W_RET), 0.02),
        "g_sb": 1.0 + nrm(ks[5], (L, W_SB), 0.02),
        "g_fox": 1.0 + nrm(ks[6], (L, W_FOX), 0.02),
        "w_out": nrm(ks[7], (L, MIX_WIDTH, D), MIX_WIDTH ** -0.5),
        "norm_ffn": 1.0 + nrm(ks[8], (L, D), 0.02),
        "w_group": nrm(ks[9], (L, D, N_GROUPS), D ** -0.5),
        "b_group": nrm(ks[10], (L, N_GROUPS), 0.01),
        "w_router": nrm(ks[11], (L, D, N_EXPERTS), D ** -0.5),
        "b_router": nrm(ks[12], (L, N_EXPERTS), 0.01),
        "w_gate": nrm(ks[13], (L, N_EXPERTS, D, D_EXPERT), D ** -0.5),
        "w_up": nrm(ks[14], (L, N_EXPERTS, D, D_EXPERT), D ** -0.5),
        "w_down": nrm(ks[15], (L, N_EXPERTS, D_EXPERT, D), D_EXPERT ** -0.5),
        "norm_final": 1.0 + nrm(ks[16], (D,), 0.02),
    }

def reference(x, norm_mix, w_in, b_forget, g_ret, g_sb, g_fox, w_out, norm_ffn, w_group, b_group,
              w_router, b_router, w_gate, w_up, w_down, norm_final):
    S = x.shape[1]
    pos = jnp.arange(S)
    for l in range(DEPTH):
        mix = mixer_block(rmsnorm(x, norm_mix[l]), w_in[l], b_forget[l], g_ret[l], g_sb[l], g_fox[l],
                          w_out[l], pos)
        x = x + mix.astype(x.dtype)
        ffn = hier_moe(rmsnorm(x, norm_ffn[l]), w_group[l], b_group[l], w_router[l], b_router[l],
                       w_gate[l], w_up[l], w_down[l])
        x = x + ffn.astype(x.dtype)
    return rmsnorm(x, norm_final)


_drawn_inputs = setup_inputs


def setup_inputs(seed=0):
    import zlib

    import numpy as np

    out = dict(_drawn_inputs(seed))
    spreads = {}
    factors = {'g_ret': 2.743, 'b_group': 2.996, 'b_router': 3.081, 'norm_final': 2.856}
    for name, (base, spread) in spreads.items():
        noise = np.random.default_rng([zlib.crc32(name.encode()), seed]).standard_normal(out[name].shape)
        drawn = base * np.exp(spread * noise) if base else spread * noise
        out[name] = __import__('jax').numpy.asarray(drawn.astype(out[name].dtype))
    for name, factor in factors.items():
        out[name] = (out[name] * factor).astype(out[name].dtype)
    return out
```

```python
from contextlib import ExitStack

import concourse.bass as bass
from concourse import mybir
import numpy as np

F32 = mybir.dt.float32
U32 = mybir.dt.uint32
I32 = mybir.dt.int32
ALU = mybir.AluOpType
ACT = mybir.ActivationFunctionType
AXX = mybir.AxisListType.X

P = 128
D = 1024
S = 512
DEPTH = 2
KD = D // P
NT = S // P
HD = 64
N_RET, N_SB, N_FOX = 6, 5, 5
W_RET, W_SB, W_FOX = N_RET * HD, N_SB * HD, N_FOX * HD
CHUNK = 64
EPS = 1e-6
NG, EPG = 4, 8
NE = NG * EPG
DE = 512
CAP = 64
N_OVER = 15
ROWS = (NE + N_OVER) * CAP
BIG = 1e30

C_QR, C_KR, C_VR, C_GATE = 0, W_RET, 2 * W_RET, 3 * W_RET
C_QS = 4 * W_RET
C_KS, C_VS = C_QS + W_SB, C_QS + 2 * W_SB
C_QF = C_QS + 3 * W_SB
C_KF, C_VF = C_QF + W_FOX, C_QF + 2 * W_FOX

PIECES = [
    [(C_QR, 512)],
    [(C_QR + 512, 256), (C_QS, 256)],
    [(C_VR, W_RET)],
    [(C_GATE, W_RET)],
    [(C_QS + 256, 64), (C_QF, 320), (C_KS, 128)],
    [(C_KS + 128, 192), (C_KF, 320)],
    [(C_VF, W_FOX + N_FOX)],
    [(C_VS, W_SB)],
]
PQ0, PQ1, PVR, PGATE, PQ2, PQ3, PVF, PVS, PO0, PO1 = range(10)
N_FRONT = 10
RING = 6
PIECE = 8 * 512
UNROLL = RING // 3

KEY_AT = [0, 512, 896, 1152]
QUERY_AT = [0, 128, 384, 768]
BLOCKS = 1280


def mixer_jobs():
    work, plan, fills, frees = [4, 5, 6, 7], {}, [0] * 8, [0] * 8
    turn = [0]

    def job(*key, bank=None, releases=1):
        if bank is None:
            bank = work[turn[0] % len(work)]
            turn[0] += 1
        fills[bank] += 1
        plan[key] = (bank, fills[bank], frees[bank], frees[bank] + releases)
        frees[bank] += releases

    def turned(name):
        for t in range(NT):
            for hh in range(2):
                job(name, t, hh)

    turned("h")
    for j in range(8):
        job("T", j)
        if j >= 2:
            job("rot", j - 2)
    for t in range(NT):
        job("vr", t)
    for h in range(N_RET):
        for i in range(NT):
            job("rs", h, i, bank=i, releases=2 if i < NT - 1 else 1)
        if h:
            job("o", "ret", h - 1)
    job("o", "ret", N_RET - 1)
    for t in range(NT):
        job("gate", t, bank=t)
    for j in range(8, 16):
        job("T", j)
    for t in range(NT):
        job("vf", t, releases=2)
    for t in range(NT):
        job("vs", t)
    job("F")
    for h in range(N_SB):
        for i in range(NT):
            job("sz", h, i, bank=i, releases=0)
        for key in (("fs", h, 0), ("fs", h, 1), ("ft", h, 0), ("fs", h, 2), ("ft", h, 1), ("fs", h, 3)):
            job(*key)
        for i in range(NT):
            job("sacc", h, i, bank=i)
        job("ft", h, 2)
        job("ft", h, 3)
        job("o", "fox", h)
        job("o", "sb", h)
    turned("m")
    for t in range(NT):
        for half in range(2):
            job("out", t, half)
    turned("g")
    job("route")
    job("pos")
    return plan, fills, frees


JOBS, FILLS, FREES = mixer_jobs()
LAST_USE = [("T", 3), ("T", 7), ("vr", 3), ("gate", 3), ("T", 11), ("T", 15), ("vf", 3), ("vs", 3),
            ("out", 3, 0), ("out", 3, 1)]


def ring_plan():
    dmas = [0] * RING
    front = []
    for n in range(N_FRONT):
        s = n % RING
        k = len(PIECES[n]) if n < len(PIECES) else 1
        front.append((s, dmas[s], k))
        dmas[s] += k
    return front, dmas, [d + NE // UNROLL for d in dmas]


FRONT, DMAS0, DMAS = ring_plan()

HEADS = [("ret", h) for h in range(N_RET)] + [x for h in range(N_SB) for x in (("fox", h), ("sb", h))]
NUMBER = {kh: n for n, kh in enumerate(HEADS)}

V_STEPS = 114
ZERO_COLS = 2 * BLOCKS
RMS_STAGES = 4
CREDIT = 1


def qk_place(kind, h):
    if kind == "ret":
        return h // 2, 3 + h // 2, h % 2
    q, k, odd = (6 + h // 2, 11 + h // 2, h % 2) if kind == "sb" else \
        (8, 13, 1) if h == 0 else (9 + (h - 1) // 2, 14 + (h - 1) // 2, (h - 1) % 2)
    return tile_buffer(q), tile_buffer(k), odd


def tile_buffer(j):
    return j if j < 6 else j % 10 if j < 10 else j - 10


def columns(*sizes):
    at, out = 0, {}
    for name, n in sizes:
        out[name] = slice(at, at + n)
        at += n
    return out, at


CONST, N_CONST = columns(("perm", P), ("ident", P), ("neg_from", P), ("neg_upto", P), ("neg_ones", P),
                         ("strict_add", P), ("strict", P), ("causal_add", P), ("rank4", NG),
                         ("rank32", NE), ("e64", NE), ("over_base", NE), ("thresholds", 7),
                         ("block_no", N_OVER))
PARAM, N_PARAM = columns(("g_mix", KD), ("g_merged", KD), ("g_ffn", KD), ("g_expert", KD),
                         ("b_forget", N_FOX), ("b_group", NG), ("b_router", NE))
RETC, N_RETC = columns(("diag", N_RET * P), ("key_decay", N_RET * NT), ("query_decay", N_RET * NT))


def shape_constants():
    k, q = np.arange(P)[:, None], np.arange(P)[None, :]
    c = np.zeros((P, N_CONST), np.float64)
    perm = np.zeros((P, P))
    for r in range(P):
        half = r % HD
        perm[r + 32 if half < 32 else r - 32, r] = -1.0 if half < 32 else 1.0
    c[:, CONST["perm"]] = perm
    c[:, CONST["ident"]] = np.eye(P)
    c[:, CONST["neg_from"]] = -(k >= q).astype(float)
    c[:, CONST["neg_upto"]] = -(k <= q).astype(float)
    c[:, CONST["neg_ones"]] = -1.0
    c[:, CONST["strict_add"]] = -BIG * (k >= q)
    c[:, CONST["strict"]] = k < q
    c[:, CONST["causal_add"]] = -BIG * (k < q)
    c[:, CONST["rank4"]] = NG - np.arange(NG)
    c[:, CONST["rank32"]] = NE - np.arange(NE)
    c[:, CONST["e64"]] = CAP * np.arange(NE)
    c[:, CONST["over_base"]] = CAP * NE - CAP - CAP * np.arange(NE)
    c[:, CONST["thresholds"]] = CAP * (1 + np.arange(7))
    c[:, CONST["block_no"]] = np.arange(N_OVER)
    half = HD // 2
    inv = (1.0 / (np.float32(10000.0) ** (np.arange(half, dtype=np.float32) / np.float32(half)))).astype(np.float32)
    ang = (np.arange(S, dtype=np.float32)[None, :] * inv[:, None]).astype(np.float64)
    rope = np.concatenate([np.tile(np.cos(ang), (4, 1)), np.tile(np.sin(ang), (4, 1))], axis=1)
    log_g = np.log(1.0 - 2.0 ** (-5.0 - np.arange(N_RET)))
    ret = np.zeros((P, N_RETC), np.float64)
    for h in range(N_RET):
        same = (k // CHUNK) == (q // CHUNK)
        decay = np.exp(log_g[h] * (np.abs(q - k) - q)) * (same | (q > k))
        ret[:, h * P:(h + 1) * P] = decay
        for t in range(NT):
            pos = P * t + np.arange(P)
            ret[:, RETC["key_decay"].start + h * NT + t] = np.exp(-log_g[h] * pos)
            ret[:, RETC["query_decay"].start + h * NT + t] = np.exp(log_g[h] * pos)
    f = lambda a: np.ascontiguousarray(a.astype(np.float32))
    return f(c), f(rope), f(ret), [float(np.exp(-g * P)) for g in log_g]


def trunk(nc, x_in, w_in, w_out, w_route, w_gate, w_up, w_down, gains, b_forget, b_group, b_router,
          norm_final, const, rope, ret_tables, out, gamma_tile):
    xbuf = nc.dram_tensor("xbuf", (ROWS, D), F32, kind="Internal").ap()
    ybuf = nc.dram_tensor("ybuf", (ROWS, D), F32, kind="Internal").ap()
    zeroed = []
    for buf in (xbuf, ybuf[NE * CAP:, :]):
        flat = buf.rearrange("(p r) d -> p (r d)", p=CAP)
        zeroed += [flat[:, a:min(a + ZERO_COLS, flat.shape[1])] for a in range(0, flat.shape[1], ZERO_COLS)]

    with ExitStack() as ctx:
        def sb(name, shape, dt=F32):
            return ctx.enter_context(nc.sbuf_tensor(name, shape, dt))

        def sem(name):
            return ctx.enter_context(nc.semaphore(name))

        ring = sb("ring", [P, RING, PIECE])
        x = sb("x", [P, NT, D])
        nat = sb("nat", [P, NT, D])
        trn = sb("trn", [P, KD, S])
        region_qk = sb("region_qk", [P, 10, S])
        region_v = sb("region_v", [P, NT * (W_RET + W_FOX)])
        probs = sb("probs", [P, 2, BLOCKS])
        log1m = sb("log1m", [P, BLOCKS])
        pair = sb("pair", [P, 2, S])
        wide = sb("wide", [P, 2, S])
        cst = sb("cst", [P, N_CONST])
        par_all = sb("par_all", [P, DEPTH, N_PARAM])
        par = sb("par", [P, N_PARAM])
        wr = sb("wr", [P, KD, NG + NE])
        st = sb("st", [P, 3, 48])
        fox_stat = sb("fox_stat", [P, 2, N_FOX * NT])
        logf = sb("logf", [P, 2, NT * N_FOX])
        neg_f = sb("neg_f", [N_FOX, S])
        gates = sb("gates", [P, 2, NT])
        dest = sb("dest", [P, 2, NT], U32)
        over_tab = sb("over_tab", [1, 16], I32)
        bank = [ctx.enter_context(nc.psum_tensor(f"bank{i}", [P, S], F32)) for i in range(8)]

        c = {k: cst[:, v] for k, v in CONST.items()}
        g = {k: par[:, v] for k, v in PARAM.items()}
        qk = region_qk
        v_ret = region_v[:, 0:NT * W_RET].rearrange("p (t n) -> p t n", t=NT)
        v_sb = region_v[:, 0:NT * W_SB].rearrange("p (t n) -> p t n", t=NT)
        v_fox = region_v[:, NT * W_RET:NT * (W_RET + W_FOX)].rearrange("p (t n) -> p t n", t=NT)
        values = {"ret": v_ret, "sb": v_sb, "fox": v_fox}
        cos_t, sin_t = wide[:, 0, :], wide[:, 1, :]
        ret_t = log1m[:, 0:N_RETC]
        moe = region_qk[:, :, :].rearrange("p j s -> p (j s)")
        xs = [moe[:, b * 512:(b + 1) * 512] for b in range(2)]
        ys = [moe[:, 1024 + b * 512:1536 + b * 512] for b in range(2)]
        xt, sg, hid, hidt = moe[:, 2048:2560], moe[:, 2560:2816], moe[:, 2816:3072], moe[:, 3072:3328]
        got = trn[:, :, :].rearrange("p (b a m) s -> p b a (m s)", b=2, a=2)

        landed = [sem(f"landed{i}") for i in range(RING)]
        filled = [sem(f"filled{i}") for i in range(8)]
        emptied = [sem(f"emptied{i}") for i in range(8)]
        x_loaded, const_loaded, param_loaded = sem("x_loaded"), sem("const_loaded"), sem("param_loaded")
        rope_loaded, ret_loaded, route_loaded = sem("rope_loaded"), sem("ret_loaded"), sem("route_loaded")
        zero_set, zeros_written = sem("zero_set"), sem("zeros_written")
        v_step, s_step, par_ready = sem("v_step"), sem("s_step"), sem("par_ready")
        squared, rms_ready, log_ready, nat_ready = sem("squared"), sem("rms_ready"), sem("log_ready"), sem("nat_ready")
        gate_exp, gate_used, merged = sem("gate_exp"), sem("gate_used"), sem("merged")
        f_ready, f_done, logf_ready = sem("f_ready"), sem("f_done"), sem("logf_ready")
        abs_ready, log_done, log1m_ready = sem("abs_ready"), sem("log_done"), sem("log1m_ready")
        max_ready = sem("max_ready")
        route_arg, route_exp, assigned = sem("route_arg"), sem("route_exp"), sem("assigned")
        dest_ready, over_ready = sem("dest_ready"), sem("over_ready")
        scattered, gathered, combined = sem("scattered"), [sem("gathered0"), sem("gathered1")], sem("combined")
        gain_loaded, final_ready, stored = sem("gain_loaded"), sem("final_ready"), sem("stored")

        class Blocks:
            def __init__(self, tag):
                self.xs_turned = sem(f"{tag}_xs_turned")
                self.xt_ready = sem(f"{tag}_xt_ready")
                self.gate_done = sem(f"{tag}_gate_done")
                self.up_done = sem(f"{tag}_up_done")
                self.exp_done = sem(f"{tag}_exp_done")
                self.sig_step = sem(f"{tag}_sig_step")
                self.hid_ready = sem(f"{tag}_hid_ready")
                self.hid_turned = sem(f"{tag}_hid_turned")
                self.hidt_ready = sem(f"{tag}_hidt_ready")
                self.down_done = sem(f"{tag}_down_done")
                self.y_ready = sem(f"{tag}_y_ready")
                self.xs_loaded = [sem(f"{tag}_xs_loaded{b}") for b in range(2)]
                self.y_stored = [sem(f"{tag}_y_stored{b}") for b in range(2)]

        main, over = Blocks("main"), Blocks("over")
        over_landed, waits_passed = sem("over_landed"), sem("waits_passed")
        block = ctx.enter_context(nc.Block())

        def slot_of(u, kind):
            return (N_FRONT + 3 * u + kind) % RING

        def weights(expert, kind):
            return (w_gate, w_up, w_down)[kind][expert, :, :].rearrange("(h p c) n -> p h (c n)", h=2, p=P)

        def piece(s, width=512):
            return ring[:, s, 0:KD * width].rearrange("p (k n) -> p k n", n=width)

        def halves(s):
            return ring[:, s, :].rearrange("p (h m) -> p h m", h=2)

        def heads(ap):
            return ap.rearrange("p (h d) -> p h d", d=HD)

        def passed(eng):
            eng.sem_inc(waits_passed, 1)

        def over_count(eng):
            passed(eng)
            return eng.value_load(over_tab[0:1, N_OVER:N_OVER + 1], min_val=0, max_val=N_OVER)

        @block.sync
        def _(sp):
            for t in range(NT):
                sp.dma_start(x[:, t, :], x_in[0, t * P:(t + 1) * P, :]).then_inc(x_loaded, 16)
            sp.dma_start(cst[:, :], const).then_inc(const_loaded, 16)
            for l in range(DEPTH):
                sp.dma_start(par_all[:, l, 0:4 * KD], gains[l, :, :]).then_inc(param_loaded, 16)
                for name, src in (("b_forget", b_forget), ("b_group", b_group), ("b_router", b_router)):
                    sp.dma_start(par_all[:, l, PARAM[name]], src[l, :].partition_broadcast(P)).then_inc(param_loaded, 16)

            def load_expert(l, e, u, kind):
                s = slot_of(u, kind)
                sp.dma_start(halves(s), weights(l * NE + e, kind)).then_inc(landed[s], 16)

            def load_tokens(E, row, b):
                for h in range(2):
                    sp.dma_start(xs[b][h * CAP:(h + 1) * CAP, :],
                                 xbuf[bass.ds(row, CAP), h * 512:(h + 1) * 512]).then_inc(E.xs_loaded[b], 16)

            with sp.Fori(0, DEPTH) as l:
                sp.wait_ge(main.down_done, CREDIT + l * NE)
                passed(sp)
                sp.wait_ge(over.down_done, CREDIT + l * N_OVER)
                passed(sp)
                for n in range(N_FRONT):
                    s, _, _ = FRONT[n]
                    if n >= RING:
                        b, fill, _, _ = JOBS[LAST_USE[n - RING]]
                        sp.wait_ge(filled[b], l * FILLS[b] + fill)
                    if n < len(PIECES):
                        width, at = sum(w for _, w in PIECES[n]), 0
                        for col, w in PIECES[n]:
                            src = w_in[l, :, col:col + w].rearrange("(k p) n -> p k n", p=P)
                            sp.dma_start(piece(s, width)[:, :, at:at + w], src).then_inc(landed[s], 16)
                            at += w
                    else:
                        half = n - len(PIECES)
                        src = w_out[l, :, half * 512:(half + 1) * 512].rearrange("(k p) n -> p k n", p=P)
                        sp.dma_start(piece(s), src).then_inc(landed[s], 16)
                    if n == 1:
                        sp.wait_ge(combined, CREDIT + l * NT)
                        sp.dma_start(wide[:, :, :], rope.rearrange("p (a s) -> p a s", a=2)).then_inc(rope_loaded, 16)
                        sp.dma_start(ret_t, ret_tables).then_inc(ret_loaded, 16)
                        sp.dma_start(wr[:, :, :], w_route[l, :, :].rearrange("(k p) n -> p k n", p=P)).then_inc(route_loaded, 16)
                for u in range(UNROLL):
                    for kind in range(3):
                        s = slot_of(u, kind)
                        last = max(n for n in range(N_FRONT) if n % RING == s)
                        b, fill, _, _ = JOBS[LAST_USE[last]]
                        sp.wait_ge(filled[b], l * FILLS[b] + fill)
                        load_expert(l, u, u, kind)
                sp.wait_ge(scattered, (l + 1) * 2 * NT * 16)
                for u in range(UNROLL):
                    load_tokens(main, u * CAP, u)
                passed(sp)
                with sp.Fori(1, NE // UNROLL) as i:
                    for u in range(UNROLL):
                        before = l * NE + (i - 1) * UNROLL + u + 1
                        for kind, used in enumerate((main.gate_done, main.up_done, main.down_done)):
                            sp.wait_ge(used, CREDIT + before)
                            passed(sp)
                            load_expert(l, i * UNROLL + u, u, kind)
                        load_tokens(main, (i * UNROLL + u) * CAP, u)
                sp.wait_ge(over_ready, l + 1)
                n_over = over_count(sp)
                with sp.If(n_over > 0):
                    sp.wait_ge(main.down_done, CREDIT + (l + 1) * NE)
                    passed(sp)
                    with sp.Fori(0, N_OVER) as j:
                        sp.wait_ge(over.down_done, CREDIT + l * N_OVER + j)
                        passed(sp)
                        e = sp.value_load(over_tab[0:1, bass.ds(j, 1)], min_val=0, max_val=NE - 1)
                        for kind in range(3):
                            sp.dma_start(halves(slot_of(0, kind)), weights(l * NE + e, kind)).then_inc(over_landed, 16)
                        load_tokens(over, (NE + j) * CAP, 0)
                with sp.Else():
                    sp.sem_inc(over_landed, 16 * 3 * N_OVER)
                    sp.sem_inc(over.xs_loaded[0], 16 * 2 * N_OVER)
            sp.wait_ge(combined, CREDIT + DEPTH * NT)
            sp.dma_start(trn[:, 0:2, :].rearrange("p a s -> p (a s)"), norm_final.partition_broadcast(P)).then_inc(gain_loaded, 16)
            for t in range(NT):
                sp.wait_ge(final_ready, t + 1)
                sp.dma_start(out[0, t * P:(t + 1) * P, :], nat[:, t, :]).then_inc(stored, 16)
            sp.wait_ge(stored, 16 * NT)

        @block.gpsimd
        def _(pool):
            for count in (main.down_done, over.down_done, *emptied, combined, main.gate_done, over.gate_done,
                          main.up_done, over.up_done, main.y_ready, over.y_ready, *main.y_stored, *over.y_stored):
                pool.sem_inc(count, CREDIT)
            with pool.Fori(0, DEPTH) as l:
                pool.wait_ge(zeros_written, 16 * len(zeroed))
                pool.wait_ge(nat_ready, (l + 1) * 2 * NT)
                pool.wait_ge(dest_ready, l + 1)
                passed(pool)
                for t in range(NT):
                    for a in range(2):
                        pool.indirect_dma_start(
                            xbuf, bass.IndirectOffsetOnAxis(ap=dest[:, a, t:t + 1], axis=0),
                            nat[:, t, :], None, bounds_check=ROWS - 1).then_inc(scattered, 16)
                for b in range(2):
                    pool.wait_ge(main.y_stored[b], CREDIT + (l + 1) * 32 * (NE // 2))
                pool.wait_ge(over.y_stored[0], CREDIT + (l + 1) * 32 * N_OVER)
                passed(pool)
                for t in range(NT):
                    if t >= 2:
                        pool.wait_ge(combined, CREDIT + l * NT + t - 1)
                        passed(pool)
                    for a in range(2):
                        pool.indirect_dma_start(
                            got[:, t % 2, a, :], None, ybuf,
                            bass.IndirectOffsetOnAxis(ap=dest[:, a, t:t + 1], axis=0),
                            bounds_check=ROWS - 1).then_inc(gathered[t % 2], 16)

        @block.scalar
        def _(act):
            act.wait_ge(zero_set, 1)
            for rows in zeroed:
                act.dma_start(rows, probs[0:CAP, :, :].rearrange("p b n -> p (b n)")[:, 0:rows.shape[1]]).then_inc(zeros_written, 16)

            def rsqrt(l, stage, n):
                act.wait_ge(rms_ready, l * RMS_STAGES + stage)
                act.activation(st[:, 1, 0:n], st[:, 0, 0:n], ACT.Ln).then_inc(s_step, 1)
                act.wait_ge(s_step, l * RMS_STAGES + stage)
                act.activation(st[:, 1, 0:n], st[:, 1, 0:n], ACT.Exp, scale=-0.5).then_inc(log_ready, 1)

            def square(t):
                act.activation(nat[:, t, :], x[:, t, :], ACT.Square, accum_out=st[:, 2, t:t + 1]).then_inc(squared, 1)

            def wait_job(l, *key):
                b, fill, _, _ = JOBS[key]
                act.wait_ge(filled[b], l * FILLS[b] + fill)
                return b

            def turned(l, name, gain):
                for t in range(NT):
                    b = wait_job(l, name, t, 1)
                    for j in range(4):
                        ins = act.activation(trn[:, 4 + j, t * P:(t + 1) * P], bank[b][:, j * P:(j + 1) * P],
                                             ACT.Copy, scale=g[gain][:, 4 + j:5 + j])
                    ins.then_inc(emptied[b], 1)

            def projected(l, j):
                b = wait_job(l, "T", j)
                scale = HD ** -0.5 if j in (0, 1, 2, 6, 7, 8, 9, 10) else 1.0
                act.activation(qk[:, j % 10, :], bank[b][:, :], ACT.Copy, scale=scale).then_inc(emptied[b], 1)

            def block_steps(E, n, b, stored_before):
                act.wait_ge(E.gate_done, CREDIT + n + 1)
                act.activation(sg, bank[1][:, 0:256], ACT.Exp, scale=-1.0).then_inc(E.exp_done, 1)
                act.wait_ge(E.down_done, CREDIT + n + 1)
                act.wait_ge(E.y_stored[b], CREDIT + stored_before)
                act.activation(ys[b], bank[6][:, :], ACT.Copy).then_inc(E.y_ready, 1)
                act.wait_ge(E.y_ready, CREDIT + n + 1)

            def store(E, row, b):
                for h in range(2):
                    act.dma_start(ybuf[bass.ds(row, CAP), h * 512:(h + 1) * 512],
                                  ys[b][h * CAP:(h + 1) * CAP, :]).then_inc(E.y_stored[b], 16)

            act.wait_ge(x_loaded, 16 * NT)
            with act.Fori(0, DEPTH) as l:
                for t in range(NT):
                    act.wait_ge(combined, CREDIT + l * NT)
                    square(t)
                rsqrt(l, 1, NT)
                act.wait_ge(par_ready, l + 1)
                turned(l, "h", "g_mix")
                for j in range(8):
                    projected(l, j)
                for t in range(NT):
                    b = wait_job(l, "vr", t)
                    act.activation(v_ret[:, t, :], bank[b][:, 0:W_RET], ACT.Copy).then_inc(emptied[b], 1)
                act.wait_ge(ret_loaded, 16 * (l + 1))
                act.wait_ge(zeros_written, 16 * len(zeroed))
                for h in range(N_RET):
                    n = NUMBER["ret", h]
                    for i in range(NT - 1):
                        b, _, free, _ = JOBS["rs", h, i]
                        act.wait_ge(emptied[b], CREDIT + l * FREES[b] + free + 1)
                        key = RETC["key_decay"].start + h * NT + i
                        act.activation(probs[:, n % 2, KEY_AT[i] + P:KEY_AT[i] + S - i * P], bank[b][:, P:S - i * P],
                                       ACT.Copy, scale=ret_t[:, key:key + 1]).then_inc(emptied[b], 1)
                rsqrt(l, 2, NT * N_RET)
                for t in range(NT):
                    b = wait_job(l, "gate", t)
                    if t >= 2:
                        act.wait_ge(gate_used, l * NT + t - 1)
                    act.activation(pair[:, t % 2, 0:W_RET], bank[b][:, 0:W_RET], ACT.Exp, scale=-1.0).then_inc(gate_exp, 1)
                for j in range(8, 16):
                    projected(l, j)
                for t in range(NT):
                    b, _, free, _ = JOBS["vf", t]
                    act.wait_ge(emptied[b], CREDIT + l * FREES[b] + free + 1)
                    act.activation(v_fox[:, t, :], bank[b][:, 0:W_FOX], ACT.Copy).then_inc(emptied[b], 1)
                for t in range(NT):
                    b = wait_job(l, "vs", t)
                    act.activation(v_sb[:, t, :], bank[b][:, 0:W_SB], ACT.Copy).then_inc(emptied[b], 1)
                act.wait_ge(f_ready, l + 1)
                act.activation(logf[:, 1, :], logf[:, 1, :], ACT.Exp, scale=-1.0).then_inc(f_done, 1)
                act.wait_ge(f_done, l * 2 + 1)
                act.activation(logf[:, 1, :], logf[:, 1, :], ACT.Ln, bias=1.0).then_inc(f_done, 1)

                def log_part(h, i):
                    k = h * NT + i
                    zt = pair[:, i % 2, 0:S - i * P]
                    act.wait_ge(abs_ready, l * N_SB * NT + k + 1)
                    act.activation(zt, zt, ACT.Exp, scale=-1.0).then_inc(log_done, 1)
                    act.wait_ge(log_done, l * 2 * N_SB * NT + 2 * k + 1)
                    act.activation(zt, zt, ACT.Ln, bias=1.0).then_inc(log_done, 1)

                def softmax_row(h, t):
                    k = h * NT + t
                    b = wait_job(l, "fs", h, t)
                    act.wait_ge(max_ready, l * N_FOX * NT + k + 1)
                    act.activation(wide[:, t % 2, 0:(t + 1) * P], bank[b][:, 0:(t + 1) * P], ACT.Exp,
                                   bias=fox_stat[:, 0, k:k + 1], accum_out=fox_stat[:, 1, k:k + 1]).then_inc(emptied[b], 1)

                for h in range(N_SB):
                    log_part(h, 0)
                    log_part(h, 1)
                    softmax_row(h, 0)
                    softmax_row(h, 1)
                    log_part(h, 2)
                    log_part(h, 3)
                    softmax_row(h, 2)
                    softmax_row(h, 3)
                    n = NUMBER["sb", h]
                    for i in range(NT):
                        b = wait_job(l, "sacc", h, i)
                        act.activation(probs[:, n % 2, KEY_AT[i]:KEY_AT[i] + S - i * P], bank[b][:, 0:S - i * P],
                                       ACT.Exp).then_inc(emptied[b], 1)
                rsqrt(l, 3, NT * (N_SB + N_FOX))
                turned(l, "m", "g_merged")
                for t in range(NT):
                    b, _, _, free = JOBS["out", t, 1]
                    act.wait_ge(emptied[b], CREDIT + l * FREES[b] + free)
                    square(t)
                rsqrt(l, 4, NT)
                turned(l, "g", "g_ffn")
                for k in range(2):
                    act.wait_ge(route_arg, l * 2 + k + 1)
                    arg = probs[:, 0, 144 + 16 * k:144 + 16 * k + (NG * NT if k == 0 else NT)]
                    act.activation(arg, arg, ACT.Exp).then_inc(route_exp, 1)
                with act.Fori(0, NE // UNROLL) as i:
                    for u in range(UNROLL):
                        e = i * UNROLL + u
                        block_steps(main, l * NE + e, u, 32 * (l * (NE // UNROLL) + i))
                        store(main, e * CAP, u)
                act.wait_ge(over_ready, l + 1)
                n_over = over_count(act)
                with act.If(n_over > 0):
                    act.wait_ge(main.y_stored[0], CREDIT + 32 * (l + 1) * (NE // 2))
                    with act.Fori(0, N_OVER) as j:
                        block_steps(over, l * N_OVER + j, 0, 32 * (l * N_OVER + j))
                        store(over, (NE + j) * CAP, 0)
                with act.Else():
                    act.sem_inc(over.exp_done, N_OVER)
                    act.sem_inc(over.y_ready, N_OVER)
                    act.sem_inc(over.y_stored[0], 32 * N_OVER)
            for t in range(NT):
                act.wait_ge(combined, CREDIT + DEPTH * NT)
                square(t)
            rsqrt(DEPTH, 1, NT)

        @block.tensor
        def _(pe):
            def begin(l, *key):
                b, _, free, _ = JOBS[key]
                pe.wait_ge(emptied[b], CREDIT + l * FREES[b] + free)
                return b

            def after(l, *key):
                b, _, _, free = JOBS[key]
                pe.wait_ge(emptied[b], CREDIT + l * FREES[b] + free)

            def all_read(l, *keys, job=None):
                last = {}
                for key in keys:
                    b, _, _, free = JOBS[key]
                    last[b] = max(last.get(b, 0), free)
                if job:
                    b, _, free, _ = JOBS[job]
                    last[b] = max(last.get(b, 0), free)
                for b, free in last.items():
                    pe.wait_ge(emptied[b], CREDIT + l * FREES[b] + free)

            def arrived(l, n):
                s, before, k = FRONT[n]
                pe.wait_ge(landed[s], 16 * (l * DMAS[s] + before + k))
                return s

            def transposes(l, name):
                for t in range(NT):
                    for hh in range(2):
                        b = begin(l, name, t, hh)
                        for j in range(4):
                            k = 4 * hh + j
                            ins = pe.transpose(bank[b][:, j * P:(j + 1) * P], nat[:, t, k * P:(k + 1) * P], c["ident"])
                        ins.then_inc(filled[b], 1)

            def wait_turned(l, name):
                all_read(l, *((name, t, hh) for t in range(NT) for hh in range(2)))

            def tile_T(l, n, j, col):
                s = arrived(l, n)
                b = begin(l, "T", j)
                for k in range(KD):
                    ins = pe.matmul(bank[b][:, :], piece(s)[:, k, col:col + P], trn[:, k, :], start=k == 0, stop=k == KD - 1)
                ins.then_inc(filled[b], 1)

            def tile_N(l, n, name, width, bank_cols=0):
                s = arrived(l, n)
                for t in range(NT):
                    b = begin(l, name, t)
                    for k in range(KD):
                        ins = pe.matmul(bank[b][:, 0:width], trn[:, k, t * P:(t + 1) * P], piece(s, width)[:, k, :],
                                        start=k == 0, stop=k == KD - 1)
                    ins.then_inc(filled[b], 1)

            def rotate(l, j):
                after(l, "T", j)
                b = begin(l, "rot", j)
                pe.matmul(bank[b][:, :], c["perm"], qk[:, j, :], start=True, stop=True).then_inc(filled[b], 1)

            def scores_T(l, kind, h, job):
                q, k, odd = qk_place(kind, h)
                part = slice(odd * HD, (odd + 1) * HD)
                for i in range(NT):
                    b = begin(l, job, h, i)
                    pe.matmul(bank[b][:, 0:S - i * P], qk[part, k, i * P:(i + 1) * P], qk[part, q, i * P:S],
                              start=True, stop=True).then_inc(filled[b], 1)

            def sum_values(l, kind, h):
                n = NUMBER[kind, h]
                made_by = {"ret": "rs", "sb": "sacc", "fox": "ft"}[kind]
                all_read(l, *((made_by, h, i) for i in range(NT)), job=("o", kind, h))
                b = JOBS["o", kind, h][0]
                for t in range(NT):
                    dst = bank[b][:, t * HD:(t + 1) * HD]
                    for i in range(t + 1):
                        at = QUERY_AT[t] + i * P if kind == "fox" else KEY_AT[i] + (t - i) * P
                        ins = pe.matmul(dst, probs[:, n % 2, at:at + P], values[kind][:, i, h * HD:(h + 1) * HD],
                                        start=i == 0, stop=i == t)
                ins.then_inc(filled[b], 1)

            def fox_scores(l, h, t):
                q, k, odd = qk_place("fox", h)
                part = slice(odd * HD, (odd + 1) * HD)
                b = begin(l, "fs", h, t)
                keys = (t + 1) * P
                pe.matmul(bank[b][:, 0:keys], qk[part, q, t * P:(t + 1) * P], qk[part, k, 0:keys], start=True, stop=False)
                pe.matmul(bank[b][:, 0:keys], c["ident"][0:N_FOX, h:h + 1].to_broadcast([N_FOX, P]), neg_f[:, 0:keys],
                          start=False, stop=False)
                pe.matmul(bank[b][:, t * P:keys], c["ident"], c["causal_add"], start=False, stop=True).then_inc(filled[b], 1)

            def fox_turn(l, h, t):
                all_read(l, ("fs", h, t), job=("ft", h, t))
                b = JOBS["ft", h, t][0]
                for i in range(t + 1):
                    ins = pe.transpose(bank[b][:, i * P:(i + 1) * P], wide[:, t % 2, i * P:(i + 1) * P], c["ident"])
                ins.then_inc(filled[b], 1)

            def sb_sums(l, h):
                pe.wait_ge(log1m_ready, l * N_SB * NT + (h + 1) * NT)
                for i in range(NT):
                    b = JOBS["sacc", h, i][0]
                    for j in range(i, NT):
                        lhs = c["neg_from"] if j == i else c["neg_ones"]
                        pe.matmul(bank[b][:, (j - i) * P:S - i * P], lhs, log1m[:, KEY_AT[j]:KEY_AT[j] + S - j * P],
                                  start=False, stop=False, skip_group_check=True)
                    pe.matmul(bank[b][:, 0:P], c["ident"], c["strict_add"], start=False, stop=True,
                              skip_group_check=True).then_inc(filled[b], 1)

            def expert_block(E, n, b, loaded, gate_at, up_at, down_at):
                pe.wait_ge(E.xs_loaded[b], loaded)
                for j in range(4):
                    src = xs[b].rearrange("p (m c) -> p c m", c=4)[:, j, :]
                    ins = pe.transpose(bank[0][:, j * P:(j + 1) * P], src, c["ident"])
                ins.then_inc(E.xs_turned, 1)
                pe.wait_ge(E.xt_ready, n + 1)
                for (wait, s), dst, done in ((gate_at, bank[1], E.gate_done), (up_at, bank[3], E.up_done)):
                    pe.wait_ge(*wait)
                    w = ring[:, s, :].rearrange("p (h c n) -> p h c n", h=2, c=4)
                    for k in range(8):
                        h, j = divmod(k, 4)
                        for half in range(2):
                            ins = pe.matmul(dst[half * CAP:(half + 1) * CAP, 0:256],
                                            xt[:, j * P + h * CAP:j * P + (h + 1) * CAP],
                                            w[:, h, j, half * 256:(half + 1) * 256], start=k == 0, stop=k == 7)
                    ins.then_inc(done, 1)
                pe.wait_ge(E.hid_ready, n + 1)
                for j in range(2):
                    src = hid.rearrange("p (m c) -> p c m", c=2)[:, j, :]
                    ins = pe.transpose(bank[5][:, j * P:(j + 1) * P], src, c["ident"])
                ins.then_inc(E.hid_turned, 1)
                pe.wait_ge(E.hidt_ready, n + 1)
                pe.wait_ge(E.y_ready, CREDIT + n)
                wait, s = down_at
                pe.wait_ge(*wait)
                w = ring[:, s, :].rearrange("p (h c n) -> p h c n", h=2, c=2)
                for k in range(4):
                    h, j = divmod(k, 2)
                    for half in range(2):
                        ins = pe.matmul(bank[6][half * CAP:(half + 1) * CAP, :],
                                        hidt[:, j * P + h * CAP:j * P + (h + 1) * CAP],
                                        w[:, h, j, half * 512:(half + 1) * 512], start=k == 0, stop=k == 3)
                ins.then_inc(E.down_done, 1)

            pe.wait_ge(const_loaded, 16)
            with pe.Fori(0, DEPTH) as l:
                pe.wait_ge(nat_ready, l * 2 * NT + NT)
                transposes(l, "h")
                wait_turned(l, "h")
                for j in range(8):
                    tile_T(l, PQ0 if j < 4 else PQ1, j, (j % 4) * P)
                    if j >= 2:
                        rotate(l, j - 2)
                tile_N(l, PVR, "vr", W_RET)
                all_read(l, *(("rot", j) for j in range(6)), *(("vr", t) for t in range(NT)))
                for h in range(N_RET):
                    scores_T(l, "ret", h, "rs")
                    if h:
                        sum_values(l, "ret", h - 1)
                sum_values(l, "ret", N_RET - 1)
                tile_N(l, PGATE, "gate", W_RET)
                for j in range(8, 16):
                    tile_T(l, PQ2 if j < 12 else PQ3, j, (j % 4) * P)
                tile_N(l, PVF, "vf", W_FOX + N_FOX)
                tile_N(l, PVS, "vs", W_SB)
                pe.wait_ge(logf_ready, l + 1)
                b = begin(l, "F")
                for q in range(NT):
                    for t in range(q + 1):
                        ins = pe.matmul(bank[b][0:N_FOX, q * P:(q + 1) * P], logf[:, 0, t * N_FOX:(t + 1) * N_FOX],
                                        c["neg_upto"] if t == q else c["neg_ones"], start=t == 0, stop=t == q)
                ins.then_inc(filled[b], 1)
                all_read(l, *(("T", j) for j in range(6, 16)), *(("vf", t) for t in range(NT)),
                         *(("vs", t) for t in range(NT)), ("F",))
                for h in range(N_SB):
                    scores_T(l, "sb", h, "sz")
                    fox_scores(l, h, 0)
                    fox_scores(l, h, 1)
                    fox_turn(l, h, 0)
                    fox_scores(l, h, 2)
                    fox_turn(l, h, 1)
                    fox_scores(l, h, 3)
                    sb_sums(l, h)
                    fox_turn(l, h, 2)
                    fox_turn(l, h, 3)
                    sum_values(l, "fox", h)
                    sum_values(l, "sb", h)
                pe.wait_ge(merged, l + 1)
                transposes(l, "m")
                wait_turned(l, "m")
                slots = [arrived(l, PO0), arrived(l, PO1)]
                for t in range(NT):
                    for half in range(2):
                        b = begin(l, "out", t, half)
                        for k in range(KD):
                            ins = pe.matmul(bank[b][:, :], trn[:, k, t * P:(t + 1) * P], piece(slots[half])[:, k, :],
                                            start=k == 0, stop=k == KD - 1)
                        ins.then_inc(filled[b], 1)
                pe.wait_ge(nat_ready, l * 2 * NT + 2 * NT)
                transposes(l, "g")
                wait_turned(l, "g")
                pe.wait_ge(route_loaded, 16 * (l + 1))
                b = begin(l, "route")
                for t in range(NT):
                    for k in range(KD):
                        ins = pe.matmul(bank[b][:, t * 36:(t + 1) * 36], trn[:, k, t * P:(t + 1) * P], wr[:, k, :],
                                        start=k == 0, stop=k == KD - 1)
                ins.then_inc(filled[b], 1)
                pe.wait_ge(assigned, l + 1)
                b = begin(l, "pos")
                pos_in = probs[:, 1, 0:2 * NT * NE].rearrange("p (a t e) -> p a t e", a=2, t=NT)
                for q in range(NT + 1):
                    for t in range(min(q, NT - 1) + 1):
                        own = t == q
                        ins = pe.matmul(bank[b][:, q * NE:(q + 1) * NE], c["strict"] if own else c["neg_ones"],
                                        pos_in[:, 0 if own else 1, t, :], start=t == 0, stop=t == min(q, NT - 1))
                ins.then_inc(filled[b], 1)
                with pe.Fori(0, NE // UNROLL) as i:
                    for u in range(UNROLL):
                        e = i * UNROLL + u
                        at = []
                        for kind in range(3):
                            s = slot_of(u, kind)
                            at.append(((landed[s], 16 * (l * DMAS[s] + DMAS0[s] + i + 1)), s))
                        expert_block(main, l * NE + e, u, 32 * (l * (NE // UNROLL) + i + 1), *at)
                pe.wait_ge(over_ready, l + 1)
                n_over = over_count(pe)
                with pe.If(n_over > 0):
                    with pe.Fori(0, N_OVER) as j:
                        n = l * N_OVER + j
                        at = [((over_landed, 48 * (n + 1)), slot_of(0, kind)) for kind in range(3)]
                        pe.wait_ge(main.y_ready, CREDIT + (l + 1) * NE)
                        expert_block(over, n, 0, 32 * (n + 1), *at)
                with pe.Else():
                    for s in (over.xs_turned, over.gate_done, over.up_done, over.hid_turned, over.down_done):
                        pe.sem_inc(s, N_OVER)

        @block.vector
        def _(v):
            base, count = [0], [0]

            def step(ins):
                count[0] += 1
                ins.then_inc(v_step, 1)
                v.wait_ge(v_step, base[0] + count[0])

            def wait_job(l, *key):
                b, fill, _, _ = JOBS[key]
                v.wait_ge(filled[b], l * FILLS[b] + fill)
                return b

            def wait_read(l, *key):
                b, _, _, free = JOBS[key]
                v.wait_ge(emptied[b], CREDIT + l * FREES[b] + free)

            def tt(out, a, b, op):
                return v.tensor_tensor(out, a, b, op)

            def magnitude(out, a):
                return v.tensor_scalar(out.bitcast(I32), a.bitcast(I32), 0x7FFFFFFF, None, ALU.bitwise_and)

            def newton(n):
                m, y, a = st[:, 0, 0:n], st[:, 1, 0:n], st[:, 2, 0:n]
                step(tt(a, y, y, ALU.mult))
                step(tt(a, a, m, ALU.mult))
                step(v.tensor_scalar(a, a, -0.5, 1.5, ALU.mult, ALU.add))
                step(tt(y, y, a, ALU.mult))

            def mean_rsqrt(l, stage, n, width):
                v.tensor_scalar(st[:, 0, 0:n], st[:, 2, 0:n], 1.0 / width, EPS, ALU.mult, ALU.add).then_inc(rms_ready, 1)
                v.wait_ge(rms_ready, l * RMS_STAGES + stage)
                v.wait_ge(log_ready, l * RMS_STAGES + stage)
                newton(n)

            def normalise(l, stage, count_before):
                v.wait_ge(squared, count_before + NT)
                mean_rsqrt(l, stage, NT, D)
                for t in range(NT):
                    v.tensor_scalar(nat[:, t, :], x[:, t, :], st[:, 1, t:t + 1], None, ALU.mult).then_inc(nat_ready, 1)

            def turned(l, name, gain):
                for t in range(NT):
                    b = wait_job(l, name, t, 0)
                    tt(trn[:, 0:4, t * P:(t + 1) * P], bank[b][:, :].rearrange("p (j n) -> p j n", j=4),
                       g[gain][:, 0:4].unsqueeze(2).to_broadcast([P, 4, P]), ALU.mult).then_inc(emptied[b], 1)

            def head_out(l, kind, h):
                b = wait_job(l, "o", kind, h)
                src = bank[b][:, 0:NT * HD].rearrange("p (t d) -> p t d", d=HD)
                col = {"ret": 0, "sb": W_RET, "fox": W_RET + W_SB}[kind] + h * HD
                dst = nat[:, :, col:col + HD]
                if kind == "sb":
                    v.tensor_copy(dst, src).then_inc(emptied[b], 1)
                    return
                if kind == "ret":
                    q = RETC["query_decay"].start + h * NT
                    by = ret_t[:, q:q + NT]
                else:
                    by = fox_stat[:, 1, h * NT:(h + 1) * NT]
                    step(v.reciprocal(by, by))
                tt(dst, src, by.unsqueeze(2).to_broadcast([P, NT, HD]), ALU.mult).then_inc(emptied[b], 1)

            def group_norm_ret(l):
                wait_read(l, "o", "ret", N_RET - 1)
                for t in range(NT):
                    ins = v.tensor_reduce(st[:, 2, t * N_RET:(t + 1) * N_RET], heads(nat[:, t, 0:W_RET]), AXX, ALU.add)
                step(ins)
                step(v.tensor_scalar(st[:, 1, 0:NT * N_RET], st[:, 2, 0:NT * N_RET], 1.0 / HD, None, ALU.mult))
                for t in range(NT):
                    o = heads(nat[:, t, 0:W_RET])
                    ins = tt(o, o, st[:, 1, t * N_RET:(t + 1) * N_RET].unsqueeze(2).to_broadcast([P, N_RET, HD]), ALU.subtract)
                step(ins)
                flat = probs[:, :, :].rearrange("p b n -> p (b n)")
                for t in range(NT):
                    o = nat[:, t, 0:W_RET]
                    ins = tt(flat[:, t * W_RET:(t + 1) * W_RET], o, o, ALU.mult)
                step(ins)
                for t in range(NT):
                    ins = v.tensor_reduce(st[:, 2, t * N_RET:(t + 1) * N_RET], heads(flat[:, t * W_RET:(t + 1) * W_RET]), AXX, ALU.add)
                step(ins)
                mean_rsqrt(l, 2, NT * N_RET, HD)
                for t in range(NT):
                    o = heads(nat[:, t, 0:W_RET])
                    ins = tt(o, o, st[:, 1, t * N_RET:(t + 1) * N_RET].unsqueeze(2).to_broadcast([P, N_RET, HD]), ALU.mult)
                step(ins)

            def gate_ret(l):
                for t in range(NT):
                    e = pair[:, t % 2, 0:W_RET]
                    b = JOBS["gate", t][0]
                    v.wait_ge(gate_exp, l * NT + t + 1)
                    step(v.tensor_scalar(e, e, 1.0, None, ALU.add))
                    step(v.reciprocal(e, e))
                    tt(e, bank[b][:, 0:W_RET], e, ALU.mult).then_inc(emptied[b], 1)
                    v.wait_ge(emptied[b], CREDIT + l * FREES[b] + JOBS["gate", t][3])
                    o = nat[:, t, 0:W_RET]
                    tt(o, o, e, ALU.mult).then_inc(gate_used, 1)

            def rms_heads(l):
                wait_read(l, "o", "sb", N_SB - 1)
                wid, nh = W_SB + W_FOX, N_SB + N_FOX
                flat = probs[:, :, :].rearrange("p b n -> p (b n)")
                for t in range(NT):
                    o = nat[:, t, W_RET:D]
                    ins = tt(flat[:, t * wid:(t + 1) * wid], o, o, ALU.mult)
                step(ins)
                for t in range(NT):
                    ins = v.tensor_reduce(st[:, 2, t * nh:(t + 1) * nh], heads(flat[:, t * wid:(t + 1) * wid]), AXX, ALU.add)
                step(ins)
                mean_rsqrt(l, 3, NT * nh, HD)
                for t in range(NT):
                    o = heads(nat[:, t, W_RET:D])
                    ins = tt(o, o, st[:, 1, t * nh:(t + 1) * nh].unsqueeze(2).to_broadcast([P, nh, HD]), ALU.mult)
                ins.then_inc(merged, 1)

            def forget_gates(l):
                for t in range(NT):
                    b = wait_job(l, "vf", t)
                    tt(logf[:, 0, t * N_FOX:(t + 1) * N_FOX], bank[b][:, W_FOX:W_FOX + N_FOX], g["b_forget"],
                       ALU.add).then_inc(emptied[b], 1)
                for t in range(NT):
                    b, _, free, _ = JOBS["vf", t]
                    v.wait_ge(emptied[b], CREDIT + l * FREES[b] + free + 1)
                magnitude(logf[:, 1, :], logf[:, 0, :]).then_inc(f_ready, 1)
                v.wait_ge(f_done, l * 2 + 2)
                v.scalar_tensor_tensor(out=logf[:, 0, :], in0=logf[:, 0, :], scalar=0.0, in1=logf[:, 1, :],
                                       op0=ALU.min, op1=ALU.subtract).then_inc(logf_ready, 1)
                b = wait_job(l, "F")
                v.tensor_copy(neg_f[:, :], bank[b][0:N_FOX, :]).then_inc(emptied[b], 1)

            def sb_abs(l, h, i):
                b = wait_job(l, "sz", h, i)
                magnitude(pair[:, i % 2, 0:S - i * P], bank[b][:, 0:S - i * P]).then_inc(abs_ready, 1)

            def sb_log1m(l, h, i):
                k = l * N_SB * NT + h * NT + i
                v.wait_ge(log_done, 2 * k + 2)
                b = JOBS["sz", h, i][0]
                at = log1m[:, KEY_AT[i]:KEY_AT[i] + S - i * P]
                step(v.scalar_tensor_tensor(out=at, in0=bank[b][:, 0:S - i * P], scalar=0.0, in1=pair[:, i % 2, 0:S - i * P],
                                            op0=ALU.max, op1=ALU.add))
                tt(at[:, 0:P], at[:, 0:P], c["strict"], ALU.mult).then_inc(log1m_ready, 1)

            def fox_max(l, h, t):
                k = h * NT + t
                b = wait_job(l, "fs", h, t)
                v.tensor_reduce(fox_stat[:, 0, k:k + 1], bank[b][:, 0:(t + 1) * P], AXX, ALU.max, negate=True).then_inc(max_ready, 1)

            def fox_turned(l, h, t):
                n = NUMBER["fox", h]
                b = wait_job(l, "ft", h, t)
                v.tensor_copy(probs[:, n % 2, QUERY_AT[t]:QUERY_AT[t] + (t + 1) * P], bank[b][:, 0:(t + 1) * P]).then_inc(emptied[b], 1)

            def argmax(o, src, mx, ties, rank, n):
                wide_of = lambda a: a.unsqueeze(2).to_broadcast([P, NT, n])
                step(v.tensor_reduce(mx, src, AXX, ALU.max))
                step(tt(o, src, wide_of(mx), ALU.is_equal))
                step(tt(o, o, rank.unsqueeze(1).to_broadcast([P, NT, n]), ALU.mult))
                step(v.tensor_reduce(ties, o, AXX, ALU.max))
                step(tt(o, o, wide_of(ties), ALU.is_equal))

            def route(l):
                top, flat = [0], probs[:, :, :].rearrange("p b n -> p (b n)")

                def take(n, at=None):
                    if at is None:
                        at = top[0]
                        top[0] += n
                    return flat[:, at:at + n]
                logits = take(NT * (NG + NE)).rearrange("p (t n) -> p t n", t=NT)
                e_group = take(NT * NG).rearrange("p (t n) -> p t n", t=NT)
                e_top = take(NT)
                top[0] = 192
                small = [take(NT) for _ in range(8)]
                onehot_g = take(NT * NG).rearrange("p (t n) -> p t n", t=NT)
                three = lambda a: a.rearrange("p (t n) -> p t n", t=NT)
                el, o1, o2, tmp = (three(take(NT * NE)) for _ in range(4))
                pos_in = probs[:, 1, 0:2 * NT * NE].rearrange("p (a t e) -> p a t e", a=2, t=NT)
                top[0] = BLOCKS + 2 * NT * NE
                where = three(take(NT * NE))
                counts, nblocks, before, shift = (take(NE) for _ in range(4))
                cmp7 = take(NE * 7).rearrange("p (e m) -> p e m", m=7)
                cmp15 = take(N_OVER * NE).rearrange("p (j e) -> p j e", e=NE)
                owner = take(16)
                m_g, s_g, p_g, m_1, m_2, r, w_a, w_b = small
                bc = lambda a, n: a.unsqueeze(2).to_broadcast([P, NT, n])

                b = wait_job(l, "route")
                bias = par[:, PARAM["b_group"].start:PARAM["b_router"].stop]
                tt(logits, bank[b][:, 0:NT * 36].rearrange("p (t n) -> p t n", t=NT),
                   bias.unsqueeze(1).to_broadcast([P, NT, NG + NE]), ALU.add).then_inc(emptied[b], 1)
                v.wait_ge(emptied[b], CREDIT + l * FREES[b] + JOBS["route",][3])
                argmax(onehot_g, logits[:, :, 0:NG], m_g, r, c["rank4"], NG)
                tt(e_group, logits[:, :, 0:NG], bc(m_g, NG), ALU.subtract).then_inc(route_arg, 1)
                step(v.tensor_scalar(onehot_g, onehot_g, BIG, -BIG, ALU.mult, ALU.add))
                for q in range(NG):
                    part = slice(q * EPG, (q + 1) * EPG)
                    ins = tt(el[:, :, part], logits[:, :, NG + q * EPG:NG + (q + 1) * EPG],
                             onehot_g[:, :, q:q + 1].to_broadcast([P, NT, EPG]), ALU.add)
                step(ins)
                argmax(o1, el, m_1, r, c["rank32"], NE)
                step(v.scalar_tensor_tensor(out=el, in0=o1, scalar=-3.0 * BIG, in1=el, op0=ALU.mult, op1=ALU.add))
                argmax(o2, el, m_2, r, c["rank32"], NE)
                v.wait_ge(route_exp, 2 * l + 1)
                step(v.tensor_reduce(s_g, e_group, AXX, ALU.add))
                step(v.reciprocal(p_g, s_g))
                tt(e_top, m_2, m_1, ALU.subtract).then_inc(route_arg, 1)
                step(tt(pos_in[:, 0, :, :], o1, o2, ALU.add))
                v.tensor_scalar(pos_in[:, 1, :, :], pos_in[:, 0, :, :], -1.0, None, ALU.mult).then_inc(assigned, 1)
                v.wait_ge(route_exp, 2 * l + 2)
                step(v.tensor_scalar(r, e_top, 1.0, None, ALU.add))
                step(v.reciprocal(r, r))
                step(tt(gates[:, 0, :], r, p_g, ALU.mult))
                step(tt(gates[:, 1, :], e_top, gates[:, 0, :], ALU.mult))
                b = wait_job(l, "pos")
                v.tensor_copy(where, bank[b][:, 0:NT * NE].rearrange("p (t n) -> p t n", t=NT))
                v.tensor_copy(counts, bank[b][:, NT * NE:(NT + 1) * NE]).then_inc(emptied[b], 1)
                v.wait_ge(emptied[b], CREDIT + l * FREES[b] + JOBS["pos",][3])
                step(tt(cmp7, counts.unsqueeze(2).to_broadcast([P, NE, 7]),
                        c["thresholds"].unsqueeze(1).to_broadcast([P, NE, 7]), ALU.is_gt))
                step(v.tensor_reduce(nblocks, cmp7, AXX, ALU.add))
                step(v.tensor_copy(before, nblocks))
                a, z = before, shift
                for d in (1, 2, 4, 8, 16):
                    v.tensor_copy(z[:, 0:d], a[:, 0:d])
                    step(tt(z[:, d:NE], a[:, d:NE], a[:, 0:NE - d], ALU.add))
                    a, z = z, a
                step(tt(cmp15, a.unsqueeze(1).to_broadcast([P, N_OVER, NE]),
                        c["block_no"].unsqueeze(2).to_broadcast([P, N_OVER, NE]), ALU.is_le))
                step(v.tensor_reduce(owner[:, 0:N_OVER], cmp15, AXX, ALU.add))
                step(v.tensor_scalar(owner[:, 0:N_OVER], owner[:, 0:N_OVER], float(NE - 1), None, ALU.min))
                step(v.tensor_copy(owner[:, N_OVER:16], a[:, NE - 1:NE]))
                v.tensor_copy(over_tab[:, :], owner[0:1, :]).then_inc(over_ready, 1)
                step(tt(z, a, nblocks, ALU.subtract))
                step(v.scalar_tensor_tensor(out=z, in0=z, scalar=float(CAP), in1=c["over_base"], op0=ALU.mult, op1=ALU.add))
                step(v.tensor_scalar(tmp, where, float(CAP), None, ALU.is_ge))
                step(tt(tmp, tmp, z.unsqueeze(1).to_broadcast([P, NT, NE]), ALU.mult))
                step(tt(where, where, c["e64"].unsqueeze(1).to_broadcast([P, NT, NE]), ALU.add))
                step(tt(where, where, tmp, ALU.add))
                for o, at in ((o1, w_a), (o2, w_b)):
                    step(tt(o, o, where, ALU.mult))
                    step(v.tensor_reduce(at, o, AXX, ALU.add))
                v.tensor_copy(dest[:, 0, :], w_a)
                v.tensor_copy(dest[:, 1, :], w_b).then_inc(dest_ready, 1)

            def expert_block(E, n):
                v.wait_ge(E.xs_turned, n + 1)
                tt(xt.rearrange("p (f s) -> p f s", s=CAP), bank[0][:, :].rearrange("p (f s) -> p f s", s=CAP),
                   g["g_expert"].unsqueeze(2).to_broadcast([P, KD, CAP]), ALU.mult).then_inc(E.xt_ready, 1)
                v.wait_ge(E.exp_done, n + 1)
                v.tensor_scalar(sg, sg, 1.0, None, ALU.add).then_inc(E.sig_step, 1)
                v.wait_ge(E.sig_step, 4 * n + 1)
                v.reciprocal(sg, sg).then_inc(E.sig_step, 1)
                v.wait_ge(E.sig_step, 4 * n + 2)
                tt(sg, bank[1][:, 0:256], sg, ALU.mult).then_inc(E.sig_step, 1)
                v.wait_ge(E.sig_step, 4 * n + 3)
                v.wait_ge(E.up_done, CREDIT + n + 1)
                tt(hid, bank[3][:, 0:256], sg, ALU.mult).then_inc(E.hid_ready, 1)
                v.wait_ge(E.hid_turned, n + 1)
                v.tensor_copy(hidt, bank[5][:, 0:256]).then_inc(E.hidt_ready, 1)
                v.sem_inc(E.sig_step, 1)

            v.memset(probs[:, :, :], 0.0).then_inc(zero_set, 1)
            v.wait_ge(const_loaded, 16)
            v.wait_ge(param_loaded, 16 * 4 * DEPTH)
            v.wait_ge(x_loaded, 16 * NT)
            with v.Fori(0, DEPTH) as l:
                base[0], count[0] = l * V_STEPS, 0
                v.tensor_copy(par[:, :], par_all[:, bass.ds(l, 1), :].rearrange("p a n -> p (a n)")).then_inc(par_ready, 1)
                v.wait_ge(par_ready, l + 1)
                normalise(l, 1, l * 2 * NT)
                turned(l, "h", "g_mix")
                v.wait_ge(rope_loaded, 16 * (l + 1))
                for j in range(6):
                    b = wait_job(l, "rot", j)
                    v.tensor_tensor(pair[:, j % 2, :], bank[b][:, :], sin_t, ALU.mult)
                    step(v.tensor_tensor(qk[:, j, :], qk[:, j, :], cos_t, ALU.mult))
                    tt(qk[:, j, :], qk[:, j, :], pair[:, j % 2, :], ALU.add).then_inc(emptied[b], 1)
                v.wait_ge(ret_loaded, 16 * (l + 1))
                v.wait_ge(zeros_written, 16 * len(zeroed))
                for h in range(N_RET):
                    n = NUMBER["ret", h]
                    for i in range(NT):
                        b = wait_job(l, "rs", h, i)
                        v.scalar_tensor_tensor(out=probs[:, n % 2, KEY_AT[i]:KEY_AT[i] + P], in0=bank[b][:, 0:P],
                                               scalar=gamma_tile[h] ** i, in1=ret_t[:, h * P:(h + 1) * P],
                                               op0=ALU.mult, op1=ALU.mult).then_inc(emptied[b], 1)
                    if h:
                        head_out(l, "ret", h - 1)
                head_out(l, "ret", N_RET - 1)
                group_norm_ret(l)
                gate_ret(l)
                forget_gates(l)
                for h in range(N_SB):
                    sb_abs(l, h, 0)
                    sb_abs(l, h, 1)
                    fox_max(l, h, 0)
                    sb_log1m(l, h, 0)
                    sb_abs(l, h, 2)
                    fox_max(l, h, 1)
                    sb_log1m(l, h, 1)
                    sb_abs(l, h, 3)
                    fox_turned(l, h, 0)
                    fox_max(l, h, 2)
                    sb_log1m(l, h, 2)
                    fox_turned(l, h, 1)
                    fox_max(l, h, 3)
                    sb_log1m(l, h, 3)
                    fox_turned(l, h, 2)
                    fox_turned(l, h, 3)
                    head_out(l, "fox", h)
                    head_out(l, "sb", h)
                rms_heads(l)
                turned(l, "m", "g_merged")
                for t in range(NT):
                    for half in range(2):
                        b = wait_job(l, "out", t, half)
                        cols = x[:, t, half * 512:(half + 1) * 512]
                        tt(cols, bank[b][:, :], cols, ALU.add).then_inc(emptied[b], 1)
                normalise(l, 4, l * 2 * NT + NT)
                turned(l, "g", "g_ffn")
                route(l)
                with v.Fori(0, NE) as e:
                    expert_block(main, l * NE + e)
                v.wait_ge(over_ready, l + 1)
                n_over = over_count(v)
                with v.If(n_over > 0):
                    with v.Fori(0, N_OVER) as j:
                        expert_block(over, l * N_OVER + j)
                with v.Else():
                    for s in (over.xt_ready, over.hid_ready, over.hidt_ready):
                        v.sem_inc(s, N_OVER)
                    v.sem_inc(over.sig_step, 4 * N_OVER)
                for t in range(NT):
                    v.wait_ge(gathered[t % 2], 64 * l + 32 * (t // 2 + 1))
                    step(v.scalar_tensor_tensor(out=x[:, t, :], in0=got[:, t % 2, 0, :], scalar=gates[:, 0, t:t + 1],
                                                in1=x[:, t, :], op0=ALU.mult, op1=ALU.add))
                    v.scalar_tensor_tensor(out=x[:, t, :], in0=got[:, t % 2, 1, :], scalar=gates[:, 1, t:t + 1],
                                           in1=x[:, t, :], op0=ALU.mult, op1=ALU.add).then_inc(combined, 1)
            assert count[0] == V_STEPS
            base[0], count[0] = DEPTH * V_STEPS, 0
            v.wait_ge(combined, CREDIT + DEPTH * NT)
            v.wait_ge(squared, DEPTH * 2 * NT + NT)
            mean_rsqrt(DEPTH, 1, NT, D)
            v.wait_ge(gain_loaded, 16)
            for t in range(NT):
                step(v.tensor_scalar(nat[:, t, :], x[:, t, :], st[:, 1, t:t + 1], None, ALU.mult))
                tt(nat[:, t, :], nat[:, t, :], trn[:, 0:2, :].rearrange("p a s -> p (a s)"), ALU.mult).then_inc(final_ready, 1)


def kernel(x, norm_mix, w_in, b_forget, g_ret, g_sb, g_fox, w_out, norm_ffn, w_group, b_group, w_router,
           b_router, w_gate, w_up, w_down, norm_final):
    from concourse import bacc
    from concourse.bass_utils import run_bass_kernel_spmd

    by_chunk = lambda a: np.asarray(a).reshape(DEPTH, KD, P).transpose(0, 2, 1)
    merged = np.concatenate([np.asarray(g_ret), np.asarray(g_sb), np.asarray(g_fox)], axis=1)
    by_expert = np.asarray(norm_ffn).reshape(DEPTH, 2, P, 4).transpose(0, 2, 3, 1).reshape(DEPTH, P, KD)
    const, rope, ret, gamma_tile = shape_constants()
    arrays = {
        "x_in": x, "w_in": w_in, "w_out": w_out,
        "w_route": np.concatenate([np.asarray(w_group), np.asarray(w_router)], axis=2),
        "w_gate": np.asarray(w_gate).reshape(DEPTH * NE, D, DE), "w_up": np.asarray(w_up).reshape(DEPTH * NE, D, DE),
        "w_down": np.asarray(w_down).reshape(DEPTH * NE, DE, D),
        "gains": np.concatenate([by_chunk(norm_mix), by_chunk(merged), by_chunk(norm_ffn), by_expert], axis=2),
        "b_forget": b_forget, "b_group": b_group, "b_router": b_router, "norm_final": norm_final,
        "const": const, "rope": rope, "ret_tables": ret,
    }
    arrays = {k: np.ascontiguousarray(v) for k, v in arrays.items()}
    nc = bacc.Bacc("TRN2", target_bir_lowering=False, num_devices=1)
    args = {k: nc.dram_tensor(k, a.shape, mybir.dt.from_np(a.dtype), kind="ExternalInput").ap() for k, a in arrays.items()}
    out = nc.dram_tensor("out", (1, S, D), F32, kind="ExternalOutput").ap()
    trunk(nc, out=out, gamma_tile=gamma_tile, **args)
    result = run_bass_kernel_spmd(nc, [arrays], core_ids=[0])
    return result.results[0]["out"]
```

```python
from contextlib import ExitStack

import concourse.bass as bass
from concourse import mybir
import numpy as np

F32 = mybir.dt.float32
U32 = mybir.dt.uint32
I32 = mybir.dt.int32
ALU = mybir.AluOpType
ACT = mybir.ActivationFunctionType
AXX = mybir.AxisListType.X

P = 128
D = 1024
S = 512
DEPTH = 2
KD = D // P
NT = S // P
HD = 64
N_RET, N_SB, N_FOX = 6, 5, 5
W_RET, W_SB, W_FOX = N_RET * HD, N_SB * HD, N_FOX * HD
CHUNK = 64
EPS = 1e-6
NG, EPG = 4, 8
NE = NG * EPG
DE = 512
CAP = 64
N_OVER = 15
ROWS = (NE + N_OVER) * CAP
BIG = 1e30

C_QR, C_KR, C_VR, C_GATE = 0, W_RET, 2 * W_RET, 3 * W_RET
C_QS = 4 * W_RET
C_KS, C_VS = C_QS + W_SB, C_QS + 2 * W_SB
C_QF = C_QS + 3 * W_SB
C_KF, C_VF = C_QF + W_FOX, C_QF + 2 * W_FOX

PIECES = [
    [(C_QR, 512)],
    [(C_QR + 512, 256), (C_QS, 256)],
    [(C_VR, W_RET)],
    [(C_GATE, W_RET)],
    [(C_QS + 256, 64), (C_QF, 320), (C_KS, 128)],
    [(C_KS + 128, 192), (C_KF, 320)],
    [(C_VF, W_FOX + N_FOX)],
    [(C_VS, W_SB)],
]
PQ0, PQ1, PVR, PGATE, PQ2, PQ3, PVF, PVS, PO0, PO1 = range(10)
N_FRONT = 10
RING = 6
PIECE = 8 * 512
UNROLL = RING // 3

KEY_AT = [0, 512, 896, 1152]
QUERY_AT = [0, 128, 384, 768]
BLOCKS = 1280


def mixer_jobs():
    work, plan, fills, frees = [4, 5, 6, 7], {}, [0] * 8, [0] * 8
    turn = [0]

    def job(*key, bank=None, releases=1):
        if bank is None:
            bank = work[turn[0] % len(work)]
            turn[0] += 1
        fills[bank] += 1
        plan[key] = (bank, fills[bank], frees[bank], frees[bank] + releases)
        frees[bank] += releases

    def turned(name):
        for t in range(NT):
            for hh in range(2):
                job(name, t, hh)

    turned("h")
    for j in range(8):
        job("T", j)
        if j >= 2:
            job("rot", j - 2)
    for t in range(NT):
        job("vr", t)
    for h in range(N_RET):
        for i in range(NT):
            job("rs", h, i, bank=i, releases=2 if i < NT - 1 else 1)
        if h:
            job("o", "ret", h - 1)
    job("o", "ret", N_RET - 1)
    for t in range(NT):
        job("gate", t, bank=t)
    for j in range(8, 16):
        job("T", j)
    for t in range(NT):
        job("vf", t, releases=2)
    for t in range(NT):
        job("vs", t)
    job("F")
    for h in range(N_SB):
        for i in range(NT):
            job("sz", h, i, bank=i, releases=0)
        for n in range(3):
            job("fs", h, n, bank=4 + n)
        if h:
            job("o", "sb", h - 1, bank=7)
        for n in range(3):
            job("ft", h, n, bank=4 + n)
        for i in range(NT):
            job("sacc", h, i, bank=i)
        job("o", "fox", h, bank=7)
    job("o", "sb", N_SB - 1, bank=7)
    turned("m")
    for t in range(NT):
        for half in range(2):
            job("out", t, half)
    turned("g")
    job("route")
    job("pos")
    return plan, fills, frees


JOBS, FILLS, FREES = mixer_jobs()
LAST_USE = [("T", 3), ("T", 7), ("vr", 3), ("gate", 3), ("T", 11), ("T", 15), ("vf", 3), ("vs", 3),
            ("out", 3, 0), ("out", 3, 1)]


def ring_plan():
    dmas = [0] * RING
    front = []
    for n in range(N_FRONT):
        s = n % RING
        k = len(PIECES[n]) if n < len(PIECES) else 1
        front.append((s, dmas[s], k))
        dmas[s] += k
    return front, dmas, [d + NE // UNROLL for d in dmas]


FRONT, DMAS0, DMAS = ring_plan()

HEADS = [("ret", h) for h in range(N_RET)] + [x for h in range(N_SB) for x in (("sb", h), ("fox", h))]
NUMBER = {kh: n for n, kh in enumerate(HEADS)}

FOX_JOBS = [[(0, 0), (1, P)], [(2, 0)], [(3, 0)]]

V_STEPS = 111
ZERO_COLS, ZERO_RUNS = 256, 47
RMS_STAGES = 4
CREDIT = 1


def qk_place(kind, h):
    if kind == "ret":
        return h // 2, 3 + h // 2, h % 2
    q, k, odd = (6 + h // 2, 11 + h // 2, h % 2) if kind == "sb" else \
        (8, 13, 1) if h == 0 else (9 + (h - 1) // 2, 14 + (h - 1) // 2, (h - 1) % 2)
    return tile_buffer(q), tile_buffer(k), odd


def tile_buffer(j):
    return j if j < 6 else j % 10 if j < 10 else j - 10


def columns(*sizes):
    at, out = 0, {}
    for name, n in sizes:
        out[name] = slice(at, at + n)
        at += n
    return out, at


CONST, N_CONST = columns(("perm", P), ("ident", P), ("neg_from", P), ("neg_upto", P), ("neg_ones", P),
                         ("strict_add", P), ("strict", P), ("causal_add", P), ("rank4", NG),
                         ("rank32", NE), ("e64", NE), ("over_base", NE), ("thresholds", 7),
                         ("block_no", N_OVER), ("row_no", CAP))
PARAM, N_PARAM = columns(("g_mix", KD), ("g_merged", KD), ("g_ffn", KD), ("g_expert", KD),
                         ("b_forget", N_FOX), ("b_group", NG), ("b_router", NE))
RETC, N_RETC = columns(("diag", N_RET * P), ("key_decay", N_RET * NT), ("query_decay", N_RET * NT))


def shape_constants():
    k, q = np.arange(P)[:, None], np.arange(P)[None, :]
    c = np.zeros((P, N_CONST), np.float64)
    perm = np.zeros((P, P))
    for r in range(P):
        half = r % HD
        perm[r + 32 if half < 32 else r - 32, r] = -1.0 if half < 32 else 1.0
    c[:, CONST["perm"]] = perm
    c[:, CONST["ident"]] = np.eye(P)
    c[:, CONST["neg_from"]] = -(k >= q).astype(float)
    c[:, CONST["neg_upto"]] = -(k <= q).astype(float)
    c[:, CONST["neg_ones"]] = -1.0
    c[:, CONST["strict_add"]] = -BIG * (k >= q)
    c[:, CONST["strict"]] = k < q
    c[:, CONST["causal_add"]] = -BIG * (k < q)
    c[:, CONST["rank4"]] = NG - np.arange(NG)
    c[:, CONST["rank32"]] = NE - np.arange(NE)
    c[:, CONST["e64"]] = CAP * (1 + np.arange(NE))
    c[:, CONST["over_base"]] = CAP * NE - CAP - CAP * np.arange(NE)
    c[:, CONST["thresholds"]] = CAP * (1 + np.arange(7))
    c[:, CONST["block_no"]] = np.arange(N_OVER)
    c[:, CONST["row_no"]] = np.arange(CAP)
    half = HD // 2
    inv = (1.0 / (np.float32(10000.0) ** (np.arange(half, dtype=np.float32) / np.float32(half)))).astype(np.float32)
    ang = (np.arange(S, dtype=np.float32)[None, :] * inv[:, None]).astype(np.float64)
    rope = np.concatenate([np.tile(np.cos(ang), (4, 1)), np.tile(np.sin(ang), (4, 1))], axis=1)
    log_g = np.log(1.0 - 2.0 ** (-5.0 - np.arange(N_RET)))
    ret = np.zeros((P, N_RETC), np.float64)
    for h in range(N_RET):
        same = (k // CHUNK) == (q // CHUNK)
        decay = np.exp(log_g[h] * (np.abs(q - k) - q)) * (same | (q > k))
        ret[:, h * P:(h + 1) * P] = decay
        for t in range(NT):
            pos = P * t + np.arange(P)
            ret[:, RETC["key_decay"].start + h * NT + t] = np.exp(-log_g[h] * pos)
            ret[:, RETC["query_decay"].start + h * NT + t] = np.exp(log_g[h] * pos)
    f = lambda a: np.ascontiguousarray(a.astype(np.float32))
    return f(c), f(rope), f(ret), [float(np.exp(-g * P)) for g in log_g]


def trunk(nc, x_in, w_in, w_out, w_route, w_gate, w_up, w_down, gains, b_forget, b_group, b_router,
          norm_final, const, rope, ret_tables, out, gamma_tile):
    ybuf = nc.dram_tensor("ybuf", (ROWS, D), F32, kind="Internal").ap()
    over_rows = ybuf[NE * CAP:, :].rearrange("(p r) (a n) -> p (r a) n", p=CAP, n=ZERO_COLS)

    with ExitStack() as ctx:
        def sb(name, shape, dt=F32):
            return ctx.enter_context(nc.sbuf_tensor(name, shape, dt))

        def sem(name):
            return ctx.enter_context(nc.semaphore(name))

        ring = sb("ring", [P, RING, PIECE])
        x = sb("x", [P, NT, D])
        nat = sb("nat", [P, NT, D])
        trn = sb("trn", [P, KD, S])
        region_qk = sb("region_qk", [P, 10, S])
        region_v = sb("region_v", [P, NT * (W_RET + W_FOX)])
        probs = sb("probs", [P, 2, BLOCKS])
        log1m = sb("log1m", [P, BLOCKS])
        pair = sb("pair", [P, 2, S])
        cos_sin = sb("cos_sin", [P, 2 * S])
        zeros = sb("zeros", [P, ZERO_COLS])
        cst = sb("cst", [P, N_CONST])
        par_all = sb("par_all", [P, DEPTH, N_PARAM])
        par = sb("par", [P, N_PARAM])
        wr = sb("wr", [P, KD, NG + NE])
        st = sb("st", [P, 3, 48])
        fox_stat = sb("fox_stat", [P, 2, N_FOX * NT])
        logf = sb("logf", [P, 2, NT * N_FOX])
        gates = sb("gates", [P, 2, NT])
        rel = sb("rel", [P, 2 * NT])[:, :]
        dest = sb("dest", [P, 2, NT], U32)
        over_tab = sb("over_tab", [1, 16], I32)
        bank = [ctx.enter_context(nc.psum_tensor(f"bank{i}", [P, S], F32)) for i in range(8)]

        c = {k: cst[:, v] for k, v in CONST.items()}
        g = {k: par[:, v] for k, v in PARAM.items()}
        qk = region_qk
        v_ret = region_v[:, 0:NT * W_RET].rearrange("p (t n) -> p t n", t=NT)
        v_sb = region_v[:, 0:NT * W_SB].rearrange("p (t n) -> p t n", t=NT)
        v_fox = region_v[:, NT * W_RET:NT * (W_RET + W_FOX)].rearrange("p (t n) -> p t n", t=NT)
        values = {"ret": v_ret, "sb": v_sb, "fox": v_fox}
        cos_t, sin_t = cos_sin[:, 0:S], cos_sin[:, S:2 * S]
        trn_flat = trn[:, :, :].rearrange("p j s -> p (j s)")
        absz, wide, neg_f = trn_flat[:, 0:BLOCKS], trn_flat[:, BLOCKS:2 * BLOCKS], trn_flat[0:N_FOX, 2 * BLOCKS:2 * BLOCKS + S]
        ret_t = log1m[:, 0:N_RETC]
        moe = region_qk[:, :, :].rearrange("p j s -> p (j s)")
        xs, hot = moe[:, 0:512], moe[:, 512:1024].rearrange("p (a t s) -> p a t s", a=2, t=NT)
        ys = [moe[:, 1024 + b * 512:1536 + b * 512] for b in range(2)]
        xt, sg, hid, hidt = moe[:, 2048:2560], moe[:, 2560:2816], moe[:, 2816:3072], moe[:, 3072:3328]
        got = trn[:, :, :].rearrange("p (b a m) s -> p b a (m s)", b=2, a=2)

        landed = [sem(f"landed{i}") for i in range(RING)]
        filled = [sem(f"filled{i}") for i in range(8)]
        emptied = [sem(f"emptied{i}") for i in range(8)]
        x_loaded, const_loaded, param_loaded = sem("x_loaded"), sem("const_loaded"), sem("param_loaded")
        rope_loaded, ret_loaded, route_loaded = sem("rope_loaded"), sem("ret_loaded"), sem("route_loaded")
        zero_set, zeros_written = sem("zero_set"), sem("zeros_written")
        v_step, s_step, par_ready = sem("v_step"), sem("s_step"), sem("par_ready")
        squared, rms_ready, log_ready, nat_ready = sem("squared"), sem("rms_ready"), sem("log_ready"), sem("nat_ready")
        gate_exp, gate_used, merged = sem("gate_exp"), sem("gate_used"), sem("merged")
        f_ready, f_done, logf_ready = sem("f_ready"), sem("f_done"), sem("logf_ready")
        abs_ready, exp_done, log_done, log1m_ready = sem("abs_ready"), sem("exp_done"), sem("log_done"), sem("log1m_ready")
        max_ready = sem("max_ready")
        route_arg, route_exp, assigned = sem("route_arg"), sem("route_exp"), sem("assigned")
        dest_ready, over_ready = sem("dest_ready"), sem("over_ready")
        gathered, combined = [sem("gathered0"), sem("gathered1")], sem("combined")
        gain_loaded, final_ready, stored = sem("gain_loaded"), sem("final_ready"), sem("stored")

        class Blocks:
            def __init__(self, tag):
                self.hot_step = sem(f"{tag}_hot_step")
                self.hot_ready = sem(f"{tag}_hot_ready")
                self.xs_summed = sem(f"{tag}_xs_summed")
                self.xs_ready = sem(f"{tag}_xs_ready")
                self.xs_turned = sem(f"{tag}_xs_turned")
                self.xt_ready = sem(f"{tag}_xt_ready")
                self.gate_done = sem(f"{tag}_gate_done")
                self.up_done = sem(f"{tag}_up_done")
                self.exp_done = sem(f"{tag}_exp_done")
                self.sig_step = sem(f"{tag}_sig_step")
                self.hid_ready = sem(f"{tag}_hid_ready")
                self.hid_turned = sem(f"{tag}_hid_turned")
                self.hidt_ready = sem(f"{tag}_hidt_ready")
                self.down_done = sem(f"{tag}_down_done")
                self.y_ready = sem(f"{tag}_y_ready")
                self.y_stored = [sem(f"{tag}_y_stored{b}") for b in range(2)]

        main, over = Blocks("main"), Blocks("over")
        over_landed, waits_passed = sem("over_landed"), sem("waits_passed")
        block = ctx.enter_context(nc.Block())

        def slot_of(u, kind):
            return (N_FRONT + 3 * u + kind) % RING

        def weights(expert, kind):
            return (w_gate, w_up, w_down)[kind][expert, :, :].rearrange("(h p c) n -> p h (c n)", h=2, p=P)

        def piece(s, width=512):
            return ring[:, s, 0:KD * width].rearrange("p (k n) -> p k n", n=width)

        def halves(s):
            return ring[:, s, :].rearrange("p (h m) -> p h m", h=2)

        def heads(ap):
            return ap.rearrange("p (h d) -> p h d", d=HD)

        def passed(eng):
            eng.sem_inc(waits_passed, 1)

        def over_count(eng):
            passed(eng)
            return eng.value_load(over_tab[0:1, N_OVER:N_OVER + 1], min_val=0, max_val=N_OVER)

        @block.sync
        def _(sp):
            for t in range(NT):
                sp.dma_start(x[:, t, :], x_in[0, t * P:(t + 1) * P, :]).then_inc(x_loaded, 16)
            sp.dma_start(cst[:, :], const).then_inc(const_loaded, 16)
            for l in range(DEPTH):
                sp.dma_start(par_all[:, l, 0:4 * KD], gains[l, :, :]).then_inc(param_loaded, 16)
                for name, src in (("b_forget", b_forget), ("b_group", b_group), ("b_router", b_router)):
                    sp.dma_start(par_all[:, l, PARAM[name]], src[l, :].partition_broadcast(P)).then_inc(param_loaded, 16)

            def load_expert(l, e, u, kind):
                s = slot_of(u, kind)
                sp.dma_start(halves(s), weights(l * NE + e, kind)).then_inc(landed[s], 16)

            with sp.Fori(0, DEPTH) as l:
                sp.wait_ge(main.down_done, CREDIT + l * NE)
                passed(sp)
                sp.wait_ge(over.down_done, CREDIT + l * N_OVER)
                passed(sp)
                for n in range(N_FRONT):
                    s, _, _ = FRONT[n]
                    if n >= RING:
                        b, fill, _, _ = JOBS[LAST_USE[n - RING]]
                        sp.wait_ge(filled[b], l * FILLS[b] + fill)
                    if n < len(PIECES):
                        width, at = sum(w for _, w in PIECES[n]), 0
                        for col, w in PIECES[n]:
                            src = w_in[l, :, col:col + w].rearrange("(k p) n -> p k n", p=P)
                            sp.dma_start(piece(s, width)[:, :, at:at + w], src).then_inc(landed[s], 16)
                            at += w
                    else:
                        half = n - len(PIECES)
                        src = w_out[l, :, half * 512:(half + 1) * 512].rearrange("(k p) n -> p k n", p=P)
                        sp.dma_start(piece(s), src).then_inc(landed[s], 16)
                    if n == 1:
                        sp.wait_ge(combined, CREDIT + l * NT)
                        sp.dma_start(cos_sin[:, :], rope).then_inc(rope_loaded, 16)
                        sp.dma_start(ret_t, ret_tables).then_inc(ret_loaded, 16)
                        sp.dma_start(wr[:, :, :], w_route[l, :, :].rearrange("(k p) n -> p k n", p=P)).then_inc(route_loaded, 16)
                for u in range(UNROLL):
                    for kind in range(3):
                        s = slot_of(u, kind)
                        last = max(n for n in range(N_FRONT) if n % RING == s)
                        b, fill, _, _ = JOBS[LAST_USE[last]]
                        sp.wait_ge(filled[b], l * FILLS[b] + fill)
                        load_expert(l, u, u, kind)
                passed(sp)
                with sp.Fori(1, NE // UNROLL) as i:
                    for u in range(UNROLL):
                        before = l * NE + (i - 1) * UNROLL + u + 1
                        for kind, used in enumerate((main.gate_done, main.up_done, main.down_done)):
                            sp.wait_ge(used, CREDIT + before)
                            passed(sp)
                            load_expert(l, i * UNROLL + u, u, kind)
                sp.wait_ge(over_ready, l + 1)
                n_over = over_count(sp)
                with sp.If(n_over > 0):
                    sp.wait_ge(main.down_done, CREDIT + (l + 1) * NE)
                    passed(sp)
                    with sp.Fori(0, N_OVER) as j:
                        sp.wait_ge(over.down_done, CREDIT + l * N_OVER + j)
                        passed(sp)
                        e = sp.value_load(over_tab[0:1, bass.ds(j, 1)], min_val=0, max_val=NE - 1)
                        for kind in range(3):
                            sp.dma_start(halves(slot_of(0, kind)), weights(l * NE + e, kind)).then_inc(over_landed, 16)
                with sp.Else():
                    sp.sem_inc(over_landed, 16 * 3 * N_OVER)
            sp.wait_ge(combined, CREDIT + DEPTH * NT)
            sp.dma_start(trn[:, 0:2, :].rearrange("p a s -> p (a s)"), norm_final.partition_broadcast(P)).then_inc(gain_loaded, 16)
            for t in range(NT):
                sp.wait_ge(final_ready, t + 1)
                sp.dma_start(out[0, t * P:(t + 1) * P, :], nat[:, t, :]).then_inc(stored, 16)
            sp.wait_ge(stored, 16 * NT)

        @block.gpsimd
        def _(pool):
            for count in (main.down_done, over.down_done, *emptied, combined, main.gate_done, over.gate_done,
                          main.up_done, over.up_done, main.xs_summed, over.xs_summed, main.y_ready, over.y_ready, *main.y_stored, *over.y_stored):
                pool.sem_inc(count, CREDIT)
            pool.wait_ge(zero_set, 1)
            for n in range(RING):
                pool.wait_ge(landed[n], 16 * FRONT[n][2])
            pool.dma_start(over_rows, zeros[0:CAP, :].unsqueeze(1).to_broadcast([CAP, over_rows.shape[1], ZERO_COLS])).then_inc(zeros_written, 16)
            pool.wait_ge(zeros_written, 16)
            with pool.Fori(0, DEPTH) as l:
                pool.wait_ge(dest_ready, l + 1)
                passed(pool)
                for b in range(2):
                    pool.wait_ge(main.y_stored[b], CREDIT + (l + 1) * 32 * (NE // 2))
                pool.wait_ge(over.y_stored[0], CREDIT + (l + 1) * 32 * N_OVER)
                passed(pool)
                for t in range(NT):
                    if t >= 2:
                        pool.wait_ge(combined, CREDIT + l * NT + t - 1)
                        passed(pool)
                    for a in range(2):
                        pool.indirect_dma_start(
                            got[:, t % 2, a, :], None, ybuf,
                            bass.IndirectOffsetOnAxis(ap=dest[:, a, t:t + 1], axis=0),
                            bounds_check=ROWS - 1).then_inc(gathered[t % 2], 16)

        @block.scalar
        def _(act):
            def rsqrt(l, stage, n):
                act.wait_ge(rms_ready, l * RMS_STAGES + stage)
                act.activation(st[:, 1, 0:n], st[:, 0, 0:n], ACT.Ln).then_inc(s_step, 1)
                act.wait_ge(s_step, l * RMS_STAGES + stage)
                act.activation(st[:, 1, 0:n], st[:, 1, 0:n], ACT.Exp, scale=-0.5).then_inc(log_ready, 1)

            def square(t):
                act.activation(nat[:, t, :], x[:, t, :], ACT.Square, accum_out=st[:, 2, t:t + 1]).then_inc(squared, 1)

            def wait_job(l, *key):
                b, fill, _, _ = JOBS[key]
                act.wait_ge(filled[b], l * FILLS[b] + fill)
                return b

            def turned(l, name, gain):
                for t in range(NT):
                    b = wait_job(l, name, t, 1)
                    for j in range(4):
                        ins = act.activation(trn[:, 4 + j, t * P:(t + 1) * P], bank[b][:, j * P:(j + 1) * P],
                                             ACT.Copy, scale=g[gain][:, 4 + j:5 + j])
                    ins.then_inc(emptied[b], 1)

            def projected(l, j):
                b = wait_job(l, "T", j)
                scale = HD ** -0.5 if j in (0, 1, 2, 6, 7, 8, 9, 10) else 1.0
                act.activation(qk[:, j % 10, :], bank[b][:, :], ACT.Copy, scale=scale).then_inc(emptied[b], 1)

            def rows_out(E, n):
                act.wait_ge(E.xs_summed, CREDIT + n + 1)
                act.activation(xs, bank[2][:, :], ACT.Copy).then_inc(E.xs_ready, 1)

            def block_steps(E, n, b, stored_before, ahead=False):
                act.wait_ge(E.gate_done, CREDIT + n + 1)
                act.activation(sg, bank[1][:, 0:256], ACT.Exp, scale=-1.0).then_inc(E.exp_done, 1)
                if ahead:
                    rows_out(E, n + 1)
                act.wait_ge(E.down_done, CREDIT + n + 1)
                act.wait_ge(E.y_stored[b], CREDIT + stored_before)
                act.activation(ys[b], bank[6][:, :], ACT.Copy).then_inc(E.y_ready, 1)
                act.wait_ge(E.y_ready, CREDIT + n + 1)

            def store(E, row, b):
                for h in range(2):
                    act.dma_start(ybuf[bass.ds(row, CAP), h * 512:(h + 1) * 512],
                                  ys[b][h * CAP:(h + 1) * CAP, :]).then_inc(E.y_stored[b], 16)

            act.wait_ge(x_loaded, 16 * NT)
            with act.Fori(0, DEPTH) as l:
                for t in range(NT):
                    act.wait_ge(combined, CREDIT + l * NT)
                    square(t)
                rsqrt(l, 1, NT)
                act.wait_ge(par_ready, l + 1)
                turned(l, "h", "g_mix")
                for j in range(8):
                    projected(l, j)
                for t in range(NT):
                    b = wait_job(l, "vr", t)
                    act.activation(v_ret[:, t, :], bank[b][:, 0:W_RET], ACT.Copy).then_inc(emptied[b], 1)
                act.wait_ge(ret_loaded, 16 * (l + 1))
                for h in range(N_RET):
                    n = NUMBER["ret", h]
                    for i in range(NT - 1):
                        b, _, free, _ = JOBS["rs", h, i]
                        act.wait_ge(emptied[b], CREDIT + l * FREES[b] + free + 1)
                        key = RETC["key_decay"].start + h * NT + i
                        act.activation(probs[:, n % 2, KEY_AT[i] + P:KEY_AT[i] + S - i * P], bank[b][:, P:S - i * P],
                                       ACT.Copy, scale=ret_t[:, key:key + 1]).then_inc(emptied[b], 1)
                rsqrt(l, 2, NT * N_RET)
                for t in range(NT):
                    b = wait_job(l, "gate", t)
                    if t >= 2:
                        act.wait_ge(gate_used, l * NT + t - 1)
                    act.activation(pair[:, t % 2, 0:W_RET], bank[b][:, 0:W_RET], ACT.Exp, scale=-1.0).then_inc(gate_exp, 1)
                for j in range(8, 16):
                    projected(l, j)
                for t in range(NT):
                    b, _, free, _ = JOBS["vf", t]
                    act.wait_ge(emptied[b], CREDIT + l * FREES[b] + free + 1)
                    act.activation(v_fox[:, t, :], bank[b][:, 0:W_FOX], ACT.Copy).then_inc(emptied[b], 1)
                for t in range(NT):
                    b = wait_job(l, "vs", t)
                    act.activation(v_sb[:, t, :], bank[b][:, 0:W_SB], ACT.Copy).then_inc(emptied[b], 1)
                act.wait_ge(f_ready, l + 1)
                act.activation(logf[:, 1, :], logf[:, 1, :], ACT.Exp, scale=-1.0).then_inc(f_done, 1)
                act.wait_ge(f_done, l * 2 + 1)
                act.activation(logf[:, 1, :], logf[:, 1, :], ACT.Ln, bias=1.0).then_inc(f_done, 1)

                def logs(h):
                    k = l * N_SB + h
                    for n, (tiles, at, end) in enumerate(((1, 0, S), (NT, S, BLOCKS))):
                        act.wait_ge(abs_ready, k * NT + tiles)
                        act.activation(absz[:, at:end], absz[:, at:end], ACT.Exp, scale=-1.0).then_inc(exp_done, 1)
                    for n, (at, end) in enumerate(((0, S), (S, BLOCKS))):
                        act.wait_ge(exp_done, 2 * k + n + 1)
                        act.activation(absz[:, at:end], absz[:, at:end], ACT.Ln, bias=1.0).then_inc(log_done, 1)

                def softmax_rows(h):
                    for n, tiles in enumerate(FOX_JOBS):
                        b = JOBS["fs", h, n][0]
                        act.wait_ge(max_ready, (l * N_FOX + h) * len(FOX_JOBS) + n + 1)
                        for t, at in tiles:
                            k = h * NT + t
                            ins = act.activation(wide[:, QUERY_AT[t]:QUERY_AT[t] + (t + 1) * P], bank[b][:, at:at + (t + 1) * P],
                                                 ACT.Exp, bias=fox_stat[:, 0, k:k + 1], accum_out=fox_stat[:, 1, k:k + 1])
                        ins.then_inc(emptied[b], 1)

                for h in range(N_SB):
                    logs(h)
                    softmax_rows(h)
                    n = NUMBER["sb", h]
                    for i in range(NT):
                        b = wait_job(l, "sacc", h, i)
                        act.activation(probs[:, n % 2, KEY_AT[i]:KEY_AT[i] + S - i * P], bank[b][:, 0:S - i * P],
                                       ACT.Exp).then_inc(emptied[b], 1)
                rsqrt(l, 3, NT * (N_SB + N_FOX))
                turned(l, "m", "g_merged")
                for t in range(NT):
                    b, _, _, free = JOBS["out", t, 1]
                    act.wait_ge(emptied[b], CREDIT + l * FREES[b] + free)
                    square(t)
                rsqrt(l, 4, NT)
                turned(l, "g", "g_ffn")
                for k in range(2):
                    act.wait_ge(route_arg, l * 2 + k + 1)
                    arg = probs[:, 0, 144 + 16 * k:144 + 16 * k + (NG * NT if k == 0 else NT)]
                    act.activation(arg, arg, ACT.Exp).then_inc(route_exp, 1)
                rows_out(main, l * NE)
                with act.Fori(0, NE // UNROLL - 1) as i:
                    for u in range(UNROLL):
                        e = i * UNROLL + u
                        block_steps(main, l * NE + e, u, 32 * (l * (NE // UNROLL) + i), ahead=True)
                        store(main, e * CAP, u)
                for u in range(UNROLL):
                    e = NE - UNROLL + u
                    block_steps(main, l * NE + e, u, 32 * (l * (NE // UNROLL) + NE // UNROLL - 1), ahead=u < UNROLL - 1)
                    store(main, e * CAP, u)
                act.wait_ge(over_ready, l + 1)
                n_over = over_count(act)
                with act.If(n_over > 0):
                    act.wait_ge(main.y_stored[0], CREDIT + 32 * (l + 1) * (NE // 2))
                    with act.Fori(0, N_OVER) as j:
                        rows_out(over, l * N_OVER + j)
                        block_steps(over, l * N_OVER + j, 0, 32 * (l * N_OVER + j))
                        store(over, (NE + j) * CAP, 0)
                with act.Else():
                    act.sem_inc(over.xs_ready, N_OVER)
                    act.sem_inc(over.exp_done, N_OVER)
                    act.sem_inc(over.y_ready, N_OVER)
                    act.sem_inc(over.y_stored[0], 32 * N_OVER)
            for t in range(NT):
                act.wait_ge(combined, CREDIT + DEPTH * NT)
                square(t)
            rsqrt(DEPTH, 1, NT)

        @block.tensor
        def _(pe):
            def begin(l, *key):
                b, _, free, _ = JOBS[key]
                pe.wait_ge(emptied[b], CREDIT + l * FREES[b] + free)
                return b

            def after(l, *key):
                b, _, _, free = JOBS[key]
                pe.wait_ge(emptied[b], CREDIT + l * FREES[b] + free)

            def all_read(l, *keys, job=None):
                last = {}
                for key in keys:
                    b, _, _, free = JOBS[key]
                    last[b] = max(last.get(b, 0), free)
                if job:
                    b, _, free, _ = JOBS[job]
                    last[b] = max(last.get(b, 0), free)
                for b, free in last.items():
                    pe.wait_ge(emptied[b], CREDIT + l * FREES[b] + free)

            def arrived(l, n):
                s, before, k = FRONT[n]
                pe.wait_ge(landed[s], 16 * (l * DMAS[s] + before + k))
                return s

            def transposes(l, name):
                for t in range(NT):
                    for hh in range(2):
                        b = begin(l, name, t, hh)
                        for j in range(4):
                            k = 4 * hh + j
                            ins = pe.transpose(bank[b][:, j * P:(j + 1) * P], nat[:, t, k * P:(k + 1) * P], c["ident"])
                        ins.then_inc(filled[b], 1)

            def wait_turned(l, name):
                all_read(l, *((name, t, hh) for t in range(NT) for hh in range(2)))

            def tile_T(l, n, j, col):
                s = arrived(l, n)
                b = begin(l, "T", j)
                for k in range(KD):
                    ins = pe.matmul(bank[b][:, :], piece(s)[:, k, col:col + P], trn[:, k, :], start=k == 0, stop=k == KD - 1)
                ins.then_inc(filled[b], 1)

            def tile_N(l, n, name, width, bank_cols=0):
                s = arrived(l, n)
                for t in range(NT):
                    b = begin(l, name, t)
                    for k in range(KD):
                        ins = pe.matmul(bank[b][:, 0:width], trn[:, k, t * P:(t + 1) * P], piece(s, width)[:, k, :],
                                        start=k == 0, stop=k == KD - 1)
                    ins.then_inc(filled[b], 1)

            def rotate(l, j):
                after(l, "T", j)
                b = begin(l, "rot", j)
                pe.matmul(bank[b][:, :], c["perm"], qk[:, j, :], start=True, stop=True).then_inc(filled[b], 1)

            def scores_T(l, kind, h, job):
                q, k, odd = qk_place(kind, h)
                part = slice(odd * HD, (odd + 1) * HD)
                for i in range(NT):
                    b = begin(l, job, h, i)
                    pe.matmul(bank[b][:, 0:S - i * P], qk[part, k, i * P:(i + 1) * P], qk[part, q, i * P:S],
                              start=True, stop=True).then_inc(filled[b], 1)

            def sum_values(l, kind, h):
                n = NUMBER[kind, h]
                made_by = {"ret": "rs", "sb": "sacc", "fox": "ft"}[kind]
                all_read(l, *((made_by, h, i) for i in range(3 if kind == "fox" else NT)), job=("o", kind, h))
                b = JOBS["o", kind, h][0]
                for t in range(NT):
                    dst = bank[b][:, t * HD:(t + 1) * HD]
                    for i in range(t + 1):
                        at = QUERY_AT[t] + i * P if kind == "fox" else KEY_AT[i] + (t - i) * P
                        ins = pe.matmul(dst, probs[:, n % 2, at:at + P], values[kind][:, i, h * HD:(h + 1) * HD],
                                        start=i == 0, stop=i == t)
                ins.then_inc(filled[b], 1)

            def fox_scores(l, h, n):
                q, k, odd = qk_place("fox", h)
                part = slice(odd * HD, (odd + 1) * HD)
                b = begin(l, "fs", h, n)
                for t, at in FOX_JOBS[n]:
                    keys = (t + 1) * P
                    dst = bank[b][:, at:at + keys]
                    pe.matmul(dst, qk[part, q, t * P:(t + 1) * P], qk[part, k, 0:keys], start=True, stop=False)
                    pe.matmul(dst, c["ident"][0:N_FOX, h:h + 1].to_broadcast([N_FOX, P]), neg_f[:, 0:keys],
                              start=False, stop=False)
                    ins = pe.matmul(dst[:, t * P:keys], c["ident"], c["causal_add"], start=False, stop=True)
                ins.then_inc(filled[b], 1)

            def fox_turn(l, h, n):
                all_read(l, ("fs", h, n), job=("ft", h, n))
                b = JOBS["ft", h, n][0]
                for t, at in FOX_JOBS[n]:
                    for i in range(t + 1):
                        ins = pe.transpose(bank[b][:, at + i * P:at + (i + 1) * P],
                                           wide[:, QUERY_AT[t] + i * P:QUERY_AT[t] + (i + 1) * P], c["ident"])
                ins.then_inc(filled[b], 1)

            def sb_sum(l, h, i):
                b = JOBS["sacc", h, i][0]
                for j in range(i, NT):
                    if i == 0:
                        pe.wait_ge(log1m_ready, l * N_SB * NT + h * NT + j + 1)
                    lhs = c["neg_from"] if j == i else c["neg_ones"]
                    pe.matmul(bank[b][:, (j - i) * P:S - i * P], lhs, log1m[:, KEY_AT[j]:KEY_AT[j] + S - j * P],
                              start=False, stop=False, skip_group_check=True)
                pe.matmul(bank[b][:, 0:P], c["ident"], c["strict_add"], start=False, stop=True,
                          skip_group_check=True).then_inc(filled[b], 1)

            def pick_rows(E, n):
                pe.wait_ge(E.hot_ready, n + 1)
                for t in range(NT):
                    for half in range(2):
                        ins = pe.matmul(bank[2][half * CAP:(half + 1) * CAP, :], hot[:, 0, t, :],
                                        nat[:, t, half * 512:(half + 1) * 512], start=t == 0, stop=t == NT - 1)
                ins.then_inc(E.xs_summed, 1)

            def turn_rows(E, n):
                pe.wait_ge(E.xs_ready, n + 1)
                for j in range(4):
                    src = xs.rearrange("p (m c) -> p c m", c=4)[:, j, :]
                    ins = pe.transpose(bank[0][:, j * P:(j + 1) * P], src, c["ident"])
                ins.then_inc(E.xs_turned, 1)

            def expert_block(E, n, gate_at, up_at, down_at, ahead=False):
                pe.wait_ge(E.xt_ready, n + 1)
                for (wait, s), dst, done in ((gate_at, bank[1], E.gate_done), (up_at, bank[3], E.up_done)):
                    pe.wait_ge(*wait)
                    w = ring[:, s, :].rearrange("p (h c n) -> p h c n", h=2, c=4)
                    for k in range(8):
                        h, j = divmod(k, 4)
                        for half in range(2):
                            ins = pe.matmul(dst[half * CAP:(half + 1) * CAP, 0:256],
                                            xt[:, j * P + h * CAP:j * P + (h + 1) * CAP],
                                            w[:, h, j, half * 256:(half + 1) * 256], start=k == 0, stop=k == 7)
                    ins.then_inc(done, 1)
                if ahead:
                    pick_rows(E, n + 1)
                pe.wait_ge(E.hid_ready, n + 1)
                for j in range(2):
                    src = hid.rearrange("p (m c) -> p c m", c=2)[:, j, :]
                    ins = pe.transpose(bank[5][:, j * P:(j + 1) * P], src, c["ident"])
                ins.then_inc(E.hid_turned, 1)
                if ahead:
                    turn_rows(E, n + 1)
                pe.wait_ge(E.hidt_ready, n + 1)
                pe.wait_ge(E.y_ready, CREDIT + n)
                wait, s = down_at
                pe.wait_ge(*wait)
                w = ring[:, s, :].rearrange("p (h c n) -> p h c n", h=2, c=2)
                for k in range(4):
                    h, j = divmod(k, 2)
                    for half in range(2):
                        ins = pe.matmul(bank[6][half * CAP:(half + 1) * CAP, :],
                                        hidt[:, j * P + h * CAP:j * P + (h + 1) * CAP],
                                        w[:, h, j, half * 512:(half + 1) * 512], start=k == 0, stop=k == 3)
                ins.then_inc(E.down_done, 1)

            pe.wait_ge(const_loaded, 16)
            with pe.Fori(0, DEPTH) as l:
                pe.wait_ge(nat_ready, l * 2 * NT + NT)
                transposes(l, "h")
                wait_turned(l, "h")
                for j in range(8):
                    tile_T(l, PQ0 if j < 4 else PQ1, j, (j % 4) * P)
                    if j >= 2:
                        rotate(l, j - 2)
                tile_N(l, PVR, "vr", W_RET)
                all_read(l, *(("rot", j) for j in range(6)), *(("vr", t) for t in range(NT)))
                for h in range(N_RET):
                    scores_T(l, "ret", h, "rs")
                    if h:
                        sum_values(l, "ret", h - 1)
                sum_values(l, "ret", N_RET - 1)
                tile_N(l, PGATE, "gate", W_RET)
                for j in range(8, 16):
                    tile_T(l, PQ2 if j < 12 else PQ3, j, (j % 4) * P)
                tile_N(l, PVF, "vf", W_FOX + N_FOX)
                tile_N(l, PVS, "vs", W_SB)
                pe.wait_ge(logf_ready, l + 1)
                b = begin(l, "F")
                for q in range(NT):
                    for t in range(q + 1):
                        ins = pe.matmul(bank[b][0:N_FOX, q * P:(q + 1) * P], logf[:, 0, t * N_FOX:(t + 1) * N_FOX],
                                        c["neg_upto"] if t == q else c["neg_ones"], start=t == 0, stop=t == q)
                ins.then_inc(filled[b], 1)
                all_read(l, *(("T", j) for j in range(6, 16)), *(("vf", t) for t in range(NT)),
                         *(("vs", t) for t in range(NT)), ("F",))
                for h in range(N_SB):
                    scores_T(l, "sb", h, "sz")
                    for n in range(3):
                        fox_scores(l, h, n)
                    if h:
                        sum_values(l, "sb", h - 1)
                    sb_sum(l, h, 0)
                    sb_sum(l, h, 1)
                    for n in range(3):
                        fox_turn(l, h, n)
                    sb_sum(l, h, 2)
                    sb_sum(l, h, 3)
                    sum_values(l, "fox", h)
                sum_values(l, "sb", N_SB - 1)
                pe.wait_ge(merged, l + 1)
                transposes(l, "m")
                wait_turned(l, "m")
                slots = [arrived(l, PO0), arrived(l, PO1)]
                for t in range(NT):
                    for half in range(2):
                        b = begin(l, "out", t, half)
                        for k in range(KD):
                            ins = pe.matmul(bank[b][:, :], trn[:, k, t * P:(t + 1) * P], piece(slots[half])[:, k, :],
                                            start=k == 0, stop=k == KD - 1)
                        ins.then_inc(filled[b], 1)
                pe.wait_ge(nat_ready, l * 2 * NT + 2 * NT)
                transposes(l, "g")
                wait_turned(l, "g")
                pe.wait_ge(route_loaded, 16 * (l + 1))
                b = begin(l, "route")
                for t in range(NT):
                    for k in range(KD):
                        ins = pe.matmul(bank[b][:, t * 36:(t + 1) * 36], trn[:, k, t * P:(t + 1) * P], wr[:, k, :],
                                        start=k == 0, stop=k == KD - 1)
                ins.then_inc(filled[b], 1)
                pe.wait_ge(assigned, l + 1)
                b = begin(l, "pos")
                pos_in = probs[:, 1, 0:2 * NT * NE].rearrange("p (a t e) -> p a t e", a=2, t=NT)
                for q in range(NT + 1):
                    for t in range(min(q, NT - 1) + 1):
                        own = t == q
                        ins = pe.matmul(bank[b][:, q * NE:(q + 1) * NE], c["strict"] if own else c["neg_ones"],
                                        pos_in[:, 0 if own else 1, t, :], start=t == 0, stop=t == min(q, NT - 1))
                ins.then_inc(filled[b], 1)

                def main_block(i, u, ahead):
                    at = []
                    for kind in range(3):
                        s = slot_of(u, kind)
                        at.append(((landed[s], 16 * (l * DMAS[s] + DMAS0[s] + i + 1)), s))
                    expert_block(main, l * NE + i * UNROLL + u, *at, ahead=ahead)

                pick_rows(main, l * NE)
                turn_rows(main, l * NE)
                with pe.Fori(0, NE // UNROLL - 1) as i:
                    for u in range(UNROLL):
                        main_block(i, u, True)
                for u in range(UNROLL):
                    main_block(NE // UNROLL - 1, u, u < UNROLL - 1)
                pe.wait_ge(over_ready, l + 1)
                n_over = over_count(pe)
                with pe.If(n_over > 0):
                    with pe.Fori(0, N_OVER) as j:
                        n = l * N_OVER + j
                        at = [((over_landed, 48 * (n + 1)), slot_of(0, kind)) for kind in range(3)]
                        pe.wait_ge(main.y_ready, CREDIT + (l + 1) * NE)
                        pick_rows(over, n)
                        turn_rows(over, n)
                        expert_block(over, n, *at)
                with pe.Else():
                    for s in (over.xs_summed, over.xs_turned, over.gate_done, over.up_done, over.hid_turned, over.down_done):
                        pe.sem_inc(s, N_OVER)

        @block.vector
        def _(v):
            base, count = [0], [0]

            def step(ins):
                count[0] += 1
                ins.then_inc(v_step, 1)
                v.wait_ge(v_step, base[0] + count[0])

            def wait_job(l, *key):
                b, fill, _, _ = JOBS[key]
                v.wait_ge(filled[b], l * FILLS[b] + fill)
                return b

            def wait_read(l, *key):
                b, _, _, free = JOBS[key]
                v.wait_ge(emptied[b], CREDIT + l * FREES[b] + free)

            def tt(out, a, b, op):
                return v.tensor_tensor(out, a, b, op)

            def magnitude(out, a):
                return v.tensor_scalar(out.bitcast(I32), a.bitcast(I32), 0x7FFFFFFF, None, ALU.bitwise_and)

            def newton(n):
                m, y, a = st[:, 0, 0:n], st[:, 1, 0:n], st[:, 2, 0:n]
                step(tt(a, y, y, ALU.mult))
                step(tt(a, a, m, ALU.mult))
                step(v.tensor_scalar(a, a, -0.5, 1.5, ALU.mult, ALU.add))
                step(tt(y, y, a, ALU.mult))

            def mean_rsqrt(l, stage, n, width):
                v.tensor_scalar(st[:, 0, 0:n], st[:, 2, 0:n], 1.0 / width, EPS, ALU.mult, ALU.add).then_inc(rms_ready, 1)
                v.wait_ge(rms_ready, l * RMS_STAGES + stage)
                v.wait_ge(log_ready, l * RMS_STAGES + stage)
                newton(n)

            def normalise(l, stage, count_before):
                v.wait_ge(squared, count_before + NT)
                mean_rsqrt(l, stage, NT, D)
                for t in range(NT):
                    v.tensor_scalar(nat[:, t, :], x[:, t, :], st[:, 1, t:t + 1], None, ALU.mult).then_inc(nat_ready, 1)

            def turned(l, name, gain):
                for t in range(NT):
                    b = wait_job(l, name, t, 0)
                    tt(trn[:, 0:4, t * P:(t + 1) * P], bank[b][:, :].rearrange("p (j n) -> p j n", j=4),
                       g[gain][:, 0:4].unsqueeze(2).to_broadcast([P, 4, P]), ALU.mult).then_inc(emptied[b], 1)

            def head_out(l, kind, h):
                b = wait_job(l, "o", kind, h)
                src = bank[b][:, 0:NT * HD].rearrange("p (t d) -> p t d", d=HD)
                col = {"ret": 0, "sb": W_RET, "fox": W_RET + W_SB}[kind] + h * HD
                dst = nat[:, :, col:col + HD]
                if kind == "sb":
                    v.tensor_copy(dst, src).then_inc(emptied[b], 1)
                    return
                if kind == "ret":
                    q = RETC["query_decay"].start + h * NT
                    by = ret_t[:, q:q + NT]
                else:
                    by = fox_stat[:, 1, h * NT:(h + 1) * NT]
                    step(v.reciprocal(by, by))
                tt(dst, src, by.unsqueeze(2).to_broadcast([P, NT, HD]), ALU.mult).then_inc(emptied[b], 1)

            def group_norm_ret(l):
                wait_read(l, "o", "ret", N_RET - 1)
                for t in range(NT):
                    ins = v.tensor_reduce(st[:, 2, t * N_RET:(t + 1) * N_RET], heads(nat[:, t, 0:W_RET]), AXX, ALU.add)
                step(ins)
                step(v.tensor_scalar(st[:, 1, 0:NT * N_RET], st[:, 2, 0:NT * N_RET], 1.0 / HD, None, ALU.mult))
                for t in range(NT):
                    o = heads(nat[:, t, 0:W_RET])
                    ins = tt(o, o, st[:, 1, t * N_RET:(t + 1) * N_RET].unsqueeze(2).to_broadcast([P, N_RET, HD]), ALU.subtract)
                step(ins)
                flat = probs[:, :, :].rearrange("p b n -> p (b n)")
                for t in range(NT):
                    o = nat[:, t, 0:W_RET]
                    ins = tt(flat[:, t * W_RET:(t + 1) * W_RET], o, o, ALU.mult)
                step(ins)
                for t in range(NT):
                    ins = v.tensor_reduce(st[:, 2, t * N_RET:(t + 1) * N_RET], heads(flat[:, t * W_RET:(t + 1) * W_RET]), AXX, ALU.add)
                step(ins)
                mean_rsqrt(l, 2, NT * N_RET, HD)
                for t in range(NT):
                    o = heads(nat[:, t, 0:W_RET])
                    ins = tt(o, o, st[:, 1, t * N_RET:(t + 1) * N_RET].unsqueeze(2).to_broadcast([P, N_RET, HD]), ALU.mult)
                step(ins)

            def gate_ret(l):
                for t in range(NT):
                    e = pair[:, t % 2, 0:W_RET]
                    b = JOBS["gate", t][0]
                    v.wait_ge(gate_exp, l * NT + t + 1)
                    step(v.tensor_scalar(e, e, 1.0, None, ALU.add))
                    step(v.reciprocal(e, e))
                    tt(e, bank[b][:, 0:W_RET], e, ALU.mult).then_inc(emptied[b], 1)
                    v.wait_ge(emptied[b], CREDIT + l * FREES[b] + JOBS["gate", t][3])
                    o = nat[:, t, 0:W_RET]
                    tt(o, o, e, ALU.mult).then_inc(gate_used, 1)

            def rms_heads(l):
                wait_read(l, "o", "sb", N_SB - 1)
                wid, nh = W_SB + W_FOX, N_SB + N_FOX
                flat = probs[:, :, :].rearrange("p b n -> p (b n)")
                for t in range(NT):
                    o = nat[:, t, W_RET:D]
                    ins = tt(flat[:, t * wid:(t + 1) * wid], o, o, ALU.mult)
                step(ins)
                for t in range(NT):
                    ins = v.tensor_reduce(st[:, 2, t * nh:(t + 1) * nh], heads(flat[:, t * wid:(t + 1) * wid]), AXX, ALU.add)
                step(ins)
                mean_rsqrt(l, 3, NT * nh, HD)
                for t in range(NT):
                    o = heads(nat[:, t, W_RET:D])
                    ins = tt(o, o, st[:, 1, t * nh:(t + 1) * nh].unsqueeze(2).to_broadcast([P, nh, HD]), ALU.mult)
                ins.then_inc(merged, 1)

            def forget_gates(l):
                for t in range(NT):
                    b = wait_job(l, "vf", t)
                    tt(logf[:, 0, t * N_FOX:(t + 1) * N_FOX], bank[b][:, W_FOX:W_FOX + N_FOX], g["b_forget"],
                       ALU.add).then_inc(emptied[b], 1)
                for t in range(NT):
                    b, _, free, _ = JOBS["vf", t]
                    v.wait_ge(emptied[b], CREDIT + l * FREES[b] + free + 1)
                magnitude(logf[:, 1, :], logf[:, 0, :]).then_inc(f_ready, 1)
                v.wait_ge(f_done, l * 2 + 2)
                v.scalar_tensor_tensor(out=logf[:, 0, :], in0=logf[:, 0, :], scalar=0.0, in1=logf[:, 1, :],
                                       op0=ALU.min, op1=ALU.subtract).then_inc(logf_ready, 1)
                b = wait_job(l, "F")
                v.tensor_copy(neg_f[:, :], bank[b][0:N_FOX, :]).then_inc(emptied[b], 1)

            def sb_abs(l, h, i):
                b = wait_job(l, "sz", h, i)
                magnitude(absz[:, KEY_AT[i]:KEY_AT[i] + S - i * P], bank[b][:, 0:S - i * P]).then_inc(abs_ready, 1)

            def sb_log1m(l, h, i):
                v.wait_ge(log_done, (l * N_SB + h) * 2 + (1 if i == 0 else 2))
                b, part = JOBS["sz", h, i][0], slice(KEY_AT[i], KEY_AT[i] + S - i * P)
                at = log1m[:, part]
                step(v.scalar_tensor_tensor(out=at, in0=bank[b][:, 0:S - i * P], scalar=0.0, in1=absz[:, part],
                                            op0=ALU.max, op1=ALU.add))
                tt(at[:, 0:P], at[:, 0:P], c["strict"], ALU.mult).then_inc(log1m_ready, 1)

            def fox_max(l, h, n):
                b = wait_job(l, "fs", h, n)
                for t, at in FOX_JOBS[n]:
                    k = h * NT + t
                    ins = v.tensor_reduce(fox_stat[:, 0, k:k + 1], bank[b][:, at:at + (t + 1) * P], AXX, ALU.max, negate=True)
                ins.then_inc(max_ready, 1)

            def fox_turned(l, h, n):
                b = wait_job(l, "ft", h, n)
                t, cols = FOX_JOBS[n][0][0], sum((t + 1) * P for t, _ in FOX_JOBS[n])
                v.tensor_copy(probs[:, NUMBER["fox", h] % 2, QUERY_AT[t]:QUERY_AT[t] + cols],
                              bank[b][:, 0:cols]).then_inc(emptied[b], 1)

            def argmax(o, src, mx, ties, rank, n):
                wide_of = lambda a: a.unsqueeze(2).to_broadcast([P, NT, n])
                step(v.tensor_reduce(mx, src, AXX, ALU.max))
                step(tt(o, src, wide_of(mx), ALU.is_equal))
                step(tt(o, o, rank.unsqueeze(1).to_broadcast([P, NT, n]), ALU.mult))
                step(v.tensor_reduce(ties, o, AXX, ALU.max))
                step(tt(o, o, wide_of(ties), ALU.is_equal))

            def route(l):
                top, flat = [0], probs[:, :, :].rearrange("p b n -> p (b n)")

                def take(n, at=None):
                    if at is None:
                        at = top[0]
                        top[0] += n
                    return flat[:, at:at + n]
                logits = take(NT * (NG + NE)).rearrange("p (t n) -> p t n", t=NT)
                e_group = take(NT * NG).rearrange("p (t n) -> p t n", t=NT)
                e_top = take(NT)
                top[0] = 192
                small = [take(NT) for _ in range(6)]
                onehot_g = take(NT * NG).rearrange("p (t n) -> p t n", t=NT)
                three = lambda a: a.rearrange("p (t n) -> p t n", t=NT)
                el, o1, o2, tmp = (three(take(NT * NE)) for _ in range(4))
                pos_in = probs[:, 1, 0:2 * NT * NE].rearrange("p (a t e) -> p a t e", a=2, t=NT)
                top[0] = BLOCKS + 2 * NT * NE
                where = three(take(NT * NE))
                counts, nblocks, before, shift = (take(NE) for _ in range(4))
                cmp7 = take(NE * 7).rearrange("p (e m) -> p e m", m=7)
                cmp15 = take(N_OVER * NE).rearrange("p (j e) -> p j e", e=NE)
                owner = take(16)
                m_g, s_g, p_g, m_1, m_2, r = small
                bc = lambda a, n: a.unsqueeze(2).to_broadcast([P, NT, n])

                b = wait_job(l, "route")
                bias = par[:, PARAM["b_group"].start:PARAM["b_router"].stop]
                tt(logits, bank[b][:, 0:NT * 36].rearrange("p (t n) -> p t n", t=NT),
                   bias.unsqueeze(1).to_broadcast([P, NT, NG + NE]), ALU.add).then_inc(emptied[b], 1)
                v.wait_ge(emptied[b], CREDIT + l * FREES[b] + JOBS["route",][3])
                argmax(onehot_g, logits[:, :, 0:NG], m_g, r, c["rank4"], NG)
                tt(e_group, logits[:, :, 0:NG], bc(m_g, NG), ALU.subtract).then_inc(route_arg, 1)
                step(v.tensor_scalar(onehot_g, onehot_g, BIG, -BIG, ALU.mult, ALU.add))
                for q in range(NG):
                    part = slice(q * EPG, (q + 1) * EPG)
                    ins = tt(el[:, :, part], logits[:, :, NG + q * EPG:NG + (q + 1) * EPG],
                             onehot_g[:, :, q:q + 1].to_broadcast([P, NT, EPG]), ALU.add)
                step(ins)
                argmax(o1, el, m_1, r, c["rank32"], NE)
                step(v.scalar_tensor_tensor(out=el, in0=o1, scalar=-3.0 * BIG, in1=el, op0=ALU.mult, op1=ALU.add))
                argmax(o2, el, m_2, r, c["rank32"], NE)
                tt(e_top, m_2, m_1, ALU.subtract).then_inc(route_arg, 1)
                step(tt(pos_in[:, 0, :, :], o1, o2, ALU.add))
                v.tensor_scalar(pos_in[:, 1, :, :], pos_in[:, 0, :, :], -1.0, None, ALU.mult).then_inc(assigned, 1)
                v.wait_ge(route_exp, 2 * l + 1)
                step(v.tensor_reduce(s_g, e_group, AXX, ALU.add))
                step(v.reciprocal(p_g, s_g))
                v.wait_ge(route_exp, 2 * l + 2)
                step(v.tensor_scalar(r, e_top, 1.0, None, ALU.add))
                step(v.reciprocal(r, r))
                step(tt(gates[:, 0, :], r, p_g, ALU.mult))
                step(tt(gates[:, 1, :], e_top, gates[:, 0, :], ALU.mult))
                b = wait_job(l, "pos")
                v.tensor_copy(where, bank[b][:, 0:NT * NE].rearrange("p (t n) -> p t n", t=NT))
                v.tensor_copy(counts, bank[b][:, NT * NE:(NT + 1) * NE]).then_inc(emptied[b], 1)
                v.wait_ge(emptied[b], CREDIT + l * FREES[b] + JOBS["pos",][3])
                step(tt(cmp7, counts.unsqueeze(2).to_broadcast([P, NE, 7]),
                        c["thresholds"].unsqueeze(1).to_broadcast([P, NE, 7]), ALU.is_gt))
                step(v.tensor_reduce(nblocks, cmp7, AXX, ALU.add))
                a, z, other = nblocks, shift, before
                for d in (1, 2, 4, 8, 16):
                    v.tensor_copy(z[:, 0:d], a[:, 0:d])
                    step(tt(z[:, d:NE], a[:, d:NE], a[:, 0:NE - d], ALU.add))
                    a, z, other = z, other, z
                step(tt(z, a, nblocks, ALU.subtract))
                step(v.scalar_tensor_tensor(out=z, in0=z, scalar=float(CAP), in1=c["over_base"], op0=ALU.mult, op1=ALU.add))
                step(v.tensor_scalar(tmp, where, float(CAP), None, ALU.is_ge))
                step(tt(tmp, tmp, z.unsqueeze(1).to_broadcast([P, NT, NE]), ALU.mult))
                step(tt(where, where, c["e64"].unsqueeze(1).to_broadcast([P, NT, NE]), ALU.add))
                step(tt(where, where, tmp, ALU.add))
                tt(o1, o1, where, ALU.mult)
                step(tt(o2, o2, where, ALU.mult))
                v.tensor_reduce(rel[:, 0:NT], o1, AXX, ALU.add)
                step(v.tensor_reduce(rel[:, NT:2 * NT], o2, AXX, ALU.add))

                def rest():
                    v.tensor_copy(dest[:, :, :].rearrange("p a t -> p (a t)"), rel).then_inc(dest_ready, 1)
                    step(tt(cmp15, a.unsqueeze(1).to_broadcast([P, N_OVER, NE]),
                            c["block_no"].unsqueeze(2).to_broadcast([P, N_OVER, NE]), ALU.is_le))
                    step(v.tensor_reduce(owner[:, 0:N_OVER], cmp15, AXX, ALU.add))
                    step(v.tensor_scalar(owner[:, 0:N_OVER], owner[:, 0:N_OVER], float(NE - 1), None, ALU.min))
                    step(v.tensor_copy(owner[:, N_OVER:16], a[:, NE - 1:NE]))
                    v.tensor_copy(over_tab[:, :], owner[0:1, :]).then_inc(over_ready, 1)
                return rest

            def mark_rows(E, n):
                v.wait_ge(E.xs_summed, CREDIT + n)
                v.tensor_scalar(rel, rel, -float(CAP), None, ALU.add).then_inc(E.hot_step, 1)
                v.wait_ge(E.hot_step, 2 * n + 1)
                tt(hot[:, :, :, :].rearrange("p a t s -> p (a t) s"), rel.unsqueeze(2).to_broadcast([P, 2 * NT, CAP]),
                   c["row_no"].unsqueeze(1).to_broadcast([P, 2 * NT, CAP]), ALU.is_equal).then_inc(E.hot_step, 1)
                v.wait_ge(E.hot_step, 2 * n + 2)
                tt(hot[:, 0, :, :], hot[:, 0, :, :], hot[:, 1, :, :], ALU.add).then_inc(E.hot_ready, 1)

            def rows_turned(E, n):
                v.wait_ge(E.xs_turned, n + 1)
                tt(xt.rearrange("p (f s) -> p f s", s=CAP), bank[0][:, :].rearrange("p (f s) -> p f s", s=CAP),
                   g["g_expert"].unsqueeze(2).to_broadcast([P, KD, CAP]), ALU.mult).then_inc(E.xt_ready, 1)

            def expert_block(E, n, ahead=False):
                if ahead:
                    mark_rows(E, n + 1)
                v.wait_ge(E.exp_done, n + 1)
                v.tensor_scalar(sg, sg, 1.0, None, ALU.add).then_inc(E.sig_step, 1)
                v.wait_ge(E.sig_step, 4 * n + 1)
                v.reciprocal(sg, sg).then_inc(E.sig_step, 1)
                v.wait_ge(E.sig_step, 4 * n + 2)
                tt(sg, bank[1][:, 0:256], sg, ALU.mult).then_inc(E.sig_step, 1)
                v.wait_ge(E.sig_step, 4 * n + 3)
                v.wait_ge(E.up_done, CREDIT + n + 1)
                tt(hid, bank[3][:, 0:256], sg, ALU.mult).then_inc(E.hid_ready, 1)
                v.wait_ge(E.hid_turned, n + 1)
                v.tensor_copy(hidt, bank[5][:, 0:256]).then_inc(E.hidt_ready, 1)
                v.sem_inc(E.sig_step, 1)
                if ahead:
                    rows_turned(E, n + 1)

            v.memset(zeros[:, :], 0.0).then_inc(zero_set, 1)
            v.wait_ge(const_loaded, 16)
            v.wait_ge(param_loaded, 16 * 4 * DEPTH)
            v.wait_ge(x_loaded, 16 * NT)
            with v.Fori(0, DEPTH) as l:
                base[0], count[0] = l * V_STEPS, 0
                v.tensor_copy(par[:, :], par_all[:, bass.ds(l, 1), :].rearrange("p a n -> p (a n)")).then_inc(par_ready, 1)
                v.wait_ge(par_ready, l + 1)
                normalise(l, 1, l * 2 * NT)
                turned(l, "h", "g_mix")
                v.wait_ge(rope_loaded, 16 * (l + 1))
                for j in range(6):
                    b = wait_job(l, "rot", j)
                    v.tensor_tensor(pair[:, j % 2, :], bank[b][:, :], sin_t, ALU.mult)
                    step(v.tensor_tensor(qk[:, j, :], qk[:, j, :], cos_t, ALU.mult))
                    tt(qk[:, j, :], qk[:, j, :], pair[:, j % 2, :], ALU.add).then_inc(emptied[b], 1)
                v.wait_ge(ret_loaded, 16 * (l + 1))
                for h in range(N_RET):
                    n = NUMBER["ret", h]
                    for i in range(NT):
                        b = wait_job(l, "rs", h, i)
                        v.scalar_tensor_tensor(out=probs[:, n % 2, KEY_AT[i]:KEY_AT[i] + P], in0=bank[b][:, 0:P],
                                               scalar=gamma_tile[h] ** i, in1=ret_t[:, h * P:(h + 1) * P],
                                               op0=ALU.mult, op1=ALU.mult).then_inc(emptied[b], 1)
                    if h:
                        head_out(l, "ret", h - 1)
                head_out(l, "ret", N_RET - 1)
                group_norm_ret(l)
                gate_ret(l)
                forget_gates(l)
                for h in range(N_SB):
                    for i in range(NT):
                        sb_abs(l, h, i)
                    fox_max(l, h, 0)
                    fox_max(l, h, 1)
                    sb_log1m(l, h, 0)
                    fox_max(l, h, 2)
                    for i in range(1, NT):
                        sb_log1m(l, h, i)
                    if h:
                        head_out(l, "sb", h - 1)
                    for n in range(3):
                        fox_turned(l, h, n)
                    head_out(l, "fox", h)
                head_out(l, "sb", N_SB - 1)
                rms_heads(l)
                turned(l, "m", "g_merged")
                for t in range(NT):
                    for half in range(2):
                        b = wait_job(l, "out", t, half)
                        cols = x[:, t, half * 512:(half + 1) * 512]
                        tt(cols, bank[b][:, :], cols, ALU.add).then_inc(emptied[b], 1)
                normalise(l, 4, l * 2 * NT + NT)
                turned(l, "g", "g_ffn")
                rest_of_route = route(l)
                mark_rows(main, l * NE)
                rest_of_route()
                rows_turned(main, l * NE)
                with v.Fori(0, NE - 1) as e:
                    expert_block(main, l * NE + e, ahead=True)
                expert_block(main, l * NE + NE - 1)
                v.wait_ge(over_ready, l + 1)
                n_over = over_count(v)
                with v.If(n_over > 0):
                    with v.Fori(0, N_OVER) as j:
                        mark_rows(over, l * N_OVER + j)
                        rows_turned(over, l * N_OVER + j)
                        expert_block(over, l * N_OVER + j)
                with v.Else():
                    v.sem_inc(over.hot_step, 2 * N_OVER)
                    for s in (over.hot_ready, over.xt_ready, over.hid_ready, over.hidt_ready):
                        v.sem_inc(s, N_OVER)
                    v.sem_inc(over.sig_step, 4 * N_OVER)
                for t in range(NT):
                    v.wait_ge(gathered[t % 2], 64 * l + 32 * (t // 2 + 1))
                    step(v.scalar_tensor_tensor(out=x[:, t, :], in0=got[:, t % 2, 0, :], scalar=gates[:, 0, t:t + 1],
                                                in1=x[:, t, :], op0=ALU.mult, op1=ALU.add))
                    v.scalar_tensor_tensor(out=x[:, t, :], in0=got[:, t % 2, 1, :], scalar=gates[:, 1, t:t + 1],
                                           in1=x[:, t, :], op0=ALU.mult, op1=ALU.add).then_inc(combined, 1)
            assert count[0] == V_STEPS, count[0]
            base[0], count[0] = DEPTH * V_STEPS, 0
            v.wait_ge(combined, CREDIT + DEPTH * NT)
            v.wait_ge(squared, DEPTH * 2 * NT + NT)
            mean_rsqrt(DEPTH, 1, NT, D)
            v.wait_ge(gain_loaded, 16)
            for t in range(NT):
                step(v.tensor_scalar(nat[:, t, :], x[:, t, :], st[:, 1, t:t + 1], None, ALU.mult))
                tt(nat[:, t, :], nat[:, t, :], trn[:, 0:2, :].rearrange("p a s -> p (a s)"), ALU.mult).then_inc(final_ready, 1)


def kernel(x, norm_mix, w_in, b_forget, g_ret, g_sb, g_fox, w_out, norm_ffn, w_group, b_group, w_router,
           b_router, w_gate, w_up, w_down, norm_final):
    from concourse import bacc
    from concourse.bass_utils import run_bass_kernel_spmd

    by_chunk = lambda a: np.asarray(a).reshape(DEPTH, KD, P).transpose(0, 2, 1)
    merged = np.concatenate([np.asarray(g_ret), np.asarray(g_sb), np.asarray(g_fox)], axis=1)
    by_expert = np.asarray(norm_ffn).reshape(DEPTH, 2, P, 4).transpose(0, 2, 3, 1).reshape(DEPTH, P, KD)
    const, rope, ret, gamma_tile = shape_constants()
    arrays = {
        "x_in": x, "w_in": w_in, "w_out": w_out,
        "w_route": np.concatenate([np.asarray(w_group), np.asarray(w_router)], axis=2),
        "w_gate": np.asarray(w_gate).reshape(DEPTH * NE, D, DE), "w_up": np.asarray(w_up).reshape(DEPTH * NE, D, DE),
        "w_down": np.asarray(w_down).reshape(DEPTH * NE, DE, D),
        "gains": np.concatenate([by_chunk(norm_mix), by_chunk(merged), by_chunk(norm_ffn), by_expert], axis=2),
        "b_forget": b_forget, "b_group": b_group, "b_router": b_router, "norm_final": norm_final,
        "const": const, "rope": rope, "ret_tables": ret,
    }
    arrays = {k: np.ascontiguousarray(v) for k, v in arrays.items()}
    nc = bacc.Bacc("TRN2", target_bir_lowering=False, num_devices=1)
    args = {k: nc.dram_tensor(k, a.shape, mybir.dt.from_np(a.dtype), kind="ExternalInput").ap() for k, a in arrays.items()}
    out = nc.dram_tensor("out", (1, S, D), F32, kind="ExternalOutput").ap()
    trunk(nc, out=out, gamma_tile=gamma_tile, **args)
    result = run_bass_kernel_spmd(nc, [arrays], core_ids=[0])
    return result.results[0]["out"]
```

```python
from contextlib import ExitStack

import concourse.bass as bass
from concourse import mybir
import numpy as np

F32 = mybir.dt.float32
F32R = mybir.dt.float32r
BF16 = mybir.dt.bfloat16
U32 = mybir.dt.uint32
I32 = mybir.dt.int32
ALU = mybir.AluOpType
ACT = mybir.ActivationFunctionType
AXX = mybir.AxisListType.X

P = 128
D = 1024
S = 512
DEPTH = 2
KD = D // P
NT = S // P
HD = 64
N_RET, N_SB, N_FOX = 6, 5, 5
W_RET, W_SB, W_FOX = N_RET * HD, N_SB * HD, N_FOX * HD
CHUNK = 64
EPS = 1e-6
NG, EPG = 4, 8
NE = NG * EPG
DE = 512
CAP = 64
N_OVER = 15
ROWS = (NE + N_OVER) * CAP
BIG = 1e30

C_QR, C_KR, C_VR, C_GATE = 0, W_RET, 2 * W_RET, 3 * W_RET
C_QS = 4 * W_RET
C_KS, C_VS = C_QS + W_SB, C_QS + 2 * W_SB
C_QF = C_QS + 3 * W_SB
C_KF, C_VF = C_QF + W_FOX, C_QF + 2 * W_FOX

PIECES = [
    [(C_QR, 512)],
    [(C_QR + 512, 256), (C_QS, 256)],
    [(C_VR, W_RET)],
    [(C_QS + 256, 64), (C_QF, 320), (C_KS, 128)],
    [(C_KS + 128, 192), (C_KF, 320)],
    [(C_GATE, W_RET)],
    [(C_VF - 1, 1 + W_FOX + N_FOX)],
    [(C_VS, W_SB)],
]
PQ0, PQ1, PVR, PQ2, PQ3, PGATE, PVF, PVS, PO0, PO1 = range(10)
N_FRONT = 10
RING = 4
PIECE = 8 * 512
SLOT_REST, SLOT_UPPER, SLOT_V, SLOT_QK, SLOT_TRN = range(RING, RING + 5)
EXPERT_SLOTS = [(2, 3, SLOT_QK), (SLOT_UPPER, 0, SLOT_REST), (SLOT_V, 1, SLOT_TRN)]
UNROLL = len(EXPERT_SLOTS)
ROUNDS, LEFT = divmod(NE, UNROLL)

KEY_AT = [0, 512, 896, 1152]
QUERY_AT = [0, 128, 384, 768]
BLOCKS = 1280


OUT_ORDER = [("m", 0), ("m", 1), ("out", 0), ("m", 2), ("out", 1), ("m", 3), ("g", 0), ("out", 2), ("g", 1),
             ("route", 0), ("out", 3), ("g", 2), ("route", 1), ("g", 3), ("route", 2), ("route", 3)]


def mixer_jobs():
    work, plan, fills, frees = [4, 5, 6, 7], {}, [0] * 8, [0] * 8
    turn = [0]

    def job(*key, bank=None, releases=1):
        if bank is None:
            bank = work[turn[0] % len(work)]
            turn[0] += 1
        fills[bank] += 1
        plan[key] = (bank, fills[bank], frees[bank], frees[bank] + releases)
        frees[bank] += releases

    def turned(name):
        for t in range(NT):
            for hh in range(2):
                job(name, t, hh)

    turned("h")
    for j in range(8):
        job("T", j)
        if j >= 2:
            job("rot", j - 2)
    for t in range(NT):
        job("vr", t, bank=t)
    for h in range(N_RET):
        for i in range(NT):
            job("rs", h, i, bank=i, releases=2 if i < NT - 1 else 1)
        if h:
            job("o", "ret", h - 1)
        job("T", 8 + h)
    job("o", "ret", N_RET - 1)
    for j in range(8 + N_RET, 16):
        job("T", j)
    for t in range(NT):
        job("gate", t, bank=t)
    for t in range(NT):
        job("vf", t, bank=4 + t, releases=2)
    for t in range(NT):
        job("vs", t, bank=t)
    job("F")
    for h in range(N_SB + 1):
        if h < N_SB:
            for i in range(NT):
                job("sz", h, i, bank=i, releases=0)
        if h:
            for n in range(3):
                job("ft", h - 1, n, bank=4 + n)
            job("o", "sb", h - 1, bank=7)
            job("o", "fox", h - 1, bank=4)
        if h < N_SB:
            for n in range(3):
                job("fs", h, n, bank=5 + n)
            for i in range(NT):
                job("sacc", h, i, bank=i)
    for kind, t in OUT_ORDER:
        for half in range(2):
            if kind != "route":
                job(kind, t, half)
    job("route", bank=3)
    job("pos", bank=2)
    return plan, fills, frees


JOBS, FILLS, FREES = mixer_jobs()
LAST_USE = [("T", 3), ("T", 7), ("vr", 3), ("T", 11), ("T", 15), ("gate", 3), ("vf", 3), ("vs", 3),
            ("out", 3, 0), ("out", 3, 1)]


def ring_plan():
    dmas = [0] * RING
    front = []
    for n in range(N_FRONT):
        s = n % RING
        k = len(PIECES[n]) if n < len(PIECES) else 1
        front.append((s, dmas[s], k))
        dmas[s] += k
    dmas += [0] * (len(EXPERT_SLOTS) * 3 - RING)
    after = list(dmas)
    for u, slots in enumerate(EXPERT_SLOTS):
        for s in slots:
            after[s] += of_turn(u)
    return front, dmas, after


def of_turn(u):
    return ROUNDS + (u < LEFT)


def split_units():
    units = []
    for n, name in ((PQ0, None), (PQ1, None), (PVR, "vr"), (PQ2, None), (PQ3, None), (PGATE, "gate"),
                    (PVF, "vf"), (PVS, "vs")):
        units += [(n, u, name) for u in range(4)]
    return units


UNITS = split_units()


def last_use(s):
    if s == SLOT_TRN:
        return "route",
    if s == SLOT_QK:
        return "o", "fox", N_FOX - 1
    if s in (SLOT_UPPER, SLOT_REST, SLOT_V):
        return "out", NT - 1, 0 if s == SLOT_UPPER else 1
    return LAST_USE[max(n for n in range(N_FRONT) if n % RING == s)]


FRONT, DMAS0, DMAS = ring_plan()

HEADS = [("ret", h) for h in range(N_RET)] + [x for h in range(N_SB) for x in (("sb", h), ("fox", h))]
NUMBER = {kh: n for n, kh in enumerate(HEADS)}

FOX_JOBS = [[(0, 0), (1, P)], [(2, 0)], [(3, 0)]]

V_STEPS = 120
ZERO_COLS = 128
RMS_STAGES = 3 + NT
CREDIT = 1


def qk_place(kind, h):
    if kind == "ret":
        return h // 2, 3 + h // 2, h % 2
    q, k, odd = (6 + h // 2, 11 + h // 2, h % 2) if kind == "sb" else \
        (8, 13, 1) if h == 0 else (9 + (h - 1) // 2, 14 + (h - 1) // 2, (h - 1) % 2)
    return tile_buffer(q), tile_buffer(k), odd


def tile_buffer(j):
    return j if j < 10 else (0, 3, 1, 4, 2, 5)[j - 10]


def columns(*sizes):
    at, out = 0, {}
    for name, n in sizes:
        out[name] = slice(at, at + n)
        at += n
    return out, at


CONST, N_CONST = columns(("perm", P), ("ident", P), ("neg_upto", P), ("neg_ones", P), ("strict", P), ("rank4", NG),
                         ("rank32", NE), ("e64", NE), ("over_base", NE), ("thresholds", 7),
                         ("block_no", N_OVER), ("row_no", CAP))
STAGED, N_STAGED = columns(("neg_from", P), ("strict_add", P), ("causal_add", P))
PARAM, N_PARAM = columns(("g_mix", KD), ("g_merged", KD), ("g_ffn", KD), ("g_expert", KD),
                         ("b_forget", N_FOX), ("b_group", NG), ("b_router", NE))
RETC, N_RETC = columns(("diag", N_RET * P), ("key_decay", N_RET * NT), ("query_decay", N_RET * NT))


def shape_constants():
    k, q = np.arange(P)[:, None], np.arange(P)[None, :]
    c, staged = np.zeros((P, N_CONST), np.float64), np.zeros((P, N_STAGED), np.float64)
    perm = np.zeros((P, P))
    for r in range(P):
        half = r % HD
        perm[r + 32 if half < 32 else r - 32, r] = -1.0 if half < 32 else 1.0
    c[:, CONST["perm"]] = perm
    c[:, CONST["ident"]] = np.eye(P)
    staged[:, STAGED["neg_from"]] = -(k >= q).astype(float)
    c[:, CONST["neg_upto"]] = -(k <= q).astype(float)
    c[:, CONST["neg_ones"]] = -1.0
    staged[:, STAGED["strict_add"]] = -BIG * (k >= q)
    c[:, CONST["strict"]] = k < q
    staged[:, STAGED["causal_add"]] = -BIG * (k < q)
    c[:, CONST["rank4"]] = NG - np.arange(NG)
    c[:, CONST["rank32"]] = NE - np.arange(NE)
    c[:, CONST["e64"]] = CAP * (1 + np.arange(NE))
    c[:, CONST["over_base"]] = CAP * NE - CAP - CAP * np.arange(NE)
    c[:, CONST["thresholds"]] = CAP * (1 + np.arange(7))
    c[:, CONST["block_no"]] = np.arange(N_OVER)
    c[:, CONST["row_no"]] = np.arange(CAP)
    half = HD // 2
    inv = (1.0 / (np.float32(10000.0) ** (np.arange(half, dtype=np.float32) / np.float32(half)))).astype(np.float32)
    ang = (np.arange(S, dtype=np.float32)[None, :] * inv[:, None]).astype(np.float64)
    rope = np.concatenate([np.tile(np.cos(ang), (4, 1)), np.tile(np.sin(ang), (4, 1))], axis=1)
    log_g = np.log(1.0 - 2.0 ** (-5.0 - np.arange(N_RET)))
    ret = np.zeros((P, N_RETC), np.float64)
    for h in range(N_RET):
        same = (k // CHUNK) == (q // CHUNK)
        decay = np.exp(log_g[h] * (np.abs(q - k) - q)) * (same | (q > k))
        ret[:, h * P:(h + 1) * P] = decay
        for t in range(NT):
            pos = P * t + np.arange(P)
            ret[:, RETC["key_decay"].start + h * NT + t] = np.exp(-log_g[h] * pos)
            ret[:, RETC["query_decay"].start + h * NT + t] = np.exp(log_g[h] * pos)
    f = lambda a: np.ascontiguousarray(a.astype(np.float32))
    return f(np.concatenate([c, staged], axis=1)), f(rope), f(ret), [float(np.exp(-g * P)) for g in log_g]


def trunk(nc, x_in, w_in, w_out, w_route, w_gate, w_up, w_down, gains, b_forget, b_group, b_router,
          norm_final, const, rope, ret_tables, out, gamma_tile):
    ybuf = nc.dram_tensor("ybuf", (ROWS, D), F32, kind="Internal").ap()
    over_rows = ybuf[NE * CAP:, :].rearrange("(p r) (a n) -> p (r a) n", p=CAP, n=ZERO_COLS)

    with ExitStack() as ctx:
        def sb(name, shape, dt=F32):
            return ctx.enter_context(nc.sbuf_tensor(name, shape, dt))

        def sb_split(name, shape):
            at = -(-nc.sbuf_base // 32) * 32
            plain = sb(name, shape)
            return plain, nc.alloc_sbuf_tensor_at(f"{name}_r", shape, F32R, offset=at)

        def sem(name):
            return ctx.enter_context(nc.semaphore(name))

        ring, ring_r = sb_split("ring", [P, SLOT_UPPER + 1, PIECE])
        x = sb("x", [P, NT, D])
        nat = sb("nat", [P, NT, D])
        trn, trn_r = sb_split("trn", [P, KD, S])
        region_qk = sb("region_qk", [P, 10, S])
        v_log, v_log_r = sb_split("v_log", [P, PIECE])
        work = sb("work", [P, 2 * BLOCKS + 4 * S])
        count_mats = sb("count_mats", [P, 2 * P], BF16)
        mask_mats = sb("mask_mats", [P, 3 * P], BF16)
        ident_b, strict_b, causal_b = (mask_mats[:, n * P:(n + 1) * P] for n in range(3))
        sum_mats = sb("sum_mats", [P, 2 * P], F32R)
        neg_from_r, neg_ones_r = sum_mats[:, 0:P], sum_mats[:, P:2 * P]
        pick_f = sb("pick_f", [P, N_FOX], F32R)
        assigned_to = sb("assigned_to", [P, 2, NT, NE], BF16)
        zeros = sb("zeros", [P, ZERO_COLS])
        cst = sb("cst", [P, N_CONST])
        par_all = sb("par_all", [P, DEPTH, N_PARAM])
        par = sb("par", [P, N_PARAM])
        wr = sb("wr", [P, KD, NG + NE])
        st = sb("st", [P, 3, 48])
        head_sum = st[:, 2, 0:NT * (N_SB + N_FOX)].rearrange("p (t n) -> p t n", t=NT)
        fox_stat = sb("fox_stat", [P, 2, N_FOX * NT])
        logf = sb("logf", [P, 2, NT * N_FOX])
        gates = sb("gates", [P, 2, NT])
        rel = sb("rel", [P, 2 * NT])[:, :]
        dest = sb("dest", [P, 2, NT], U32)
        over_tab = sb("over_tab", [1, 16], I32)
        bank = [ctx.enter_context(nc.psum_tensor(f"bank{i}", [P, S], F32)) for i in range(8)]

        c = {k: cst[:, v] for k, v in CONST.items()}
        g = {k: par[:, v] for k, v in PARAM.items()}
        staged = {k: work[:, v] for k, v in STAGED.items()}
        qk = region_qk
        v_ret = v_log[:, 0:NT * W_RET].rearrange("p (t n) -> p t n", t=NT)
        v_sb = v_log[:, 0:NT * W_SB].rearrange("p (t n) -> p t n", t=NT)
        v_fox = v_log[:, NT * W_RET:NT * (W_RET + W_FOX)].rearrange("p (t n) -> p t n", t=NT)
        log1m_r = v_log_r[:, PIECE - BLOCKS:PIECE]
        probs = work[:, 0:2 * BLOCKS].rearrange("p (b n) -> p b n", b=2)
        pair = work[:, 2 * BLOCKS:2 * BLOCKS + 2 * S].rearrange("p (a s) -> p a s", a=2)
        gate_copy = work[:, 0:NT * W_RET].rearrange("p (t n) -> p t n", t=NT)
        cos_sin = work[:, 2 * BLOCKS + 2 * S:2 * BLOCKS + 4 * S]
        values = {"ret": v_ret, "sb": v_sb, "fox": v_fox}
        cos_t, sin_t = cos_sin[:, 0:S], cos_sin[:, S:2 * S]
        trn_flat = trn[:, :, :].rearrange("p j s -> p (j s)")
        absz, wide = trn_flat[:, 0:BLOCKS], trn_flat[:, BLOCKS:2 * BLOCKS]
        trn_flat_r = trn_r[:, :, :].rearrange("p j s -> p (j s)")
        absz_r, neg_f_r = trn_flat_r[:, 0:BLOCKS], trn_flat_r[:, 2 * BLOCKS:2 * BLOCKS + S]
        ret_t = v_log[:, PIECE - BLOCKS:PIECE - BLOCKS + N_RETC]
        xs, hot = pair[:, 0, :], pair[:, 1, :].rearrange("p (a t s) -> p a t s", a=2, t=NT)
        xt, sg, hid, hidt = work[:, 0:512], work[:, 512:768], work[:, 768:1024], work[:, 1024:1280]
        ys = [cos_sin[:, 0:S], cos_sin[:, S:2 * S], work[:, 1280:1792]]
        nat_flat = nat[:, :, :].rearrange("p t d -> p (t d)")
        got = [buf[:, (2 * b + a) * D:(2 * b + a + 1) * D] for buf in (trn_flat, nat_flat) for b in range(2) for a in range(2)]

        slots = [ring[:, i, :] for i in range(SLOT_UPPER + 1)] + [
            v_log[:, :], region_qk[:, 0:PIECE // S, :].rearrange("p j s -> p (j s)"), trn_flat]
        landed = [sem(f"landed{i}") for i in range(len(slots))]
        filled = [sem(f"filled{i}") for i in range(8)]
        emptied = [sem(f"emptied{i}") for i in range(8)]
        x_loaded = [sem(f"x_loaded{t}") for t in range(NT)]
        const_loaded, staged_loaded, param_loaded = sem("const_loaded"), sem("staged_loaded"), sem("param_loaded")
        rope_loaded, ret_loaded, route_loaded = sem("rope_loaded"), sem("ret_loaded"), sem("route_loaded")
        zero_set, zeros_written = sem("zero_set"), sem("zeros_written")
        v_step, s_step, par_ready = sem("v_step"), sem("s_step"), sem("par_ready")
        squared, rms_ready, log_ready, nat_ready = sem("squared"), sem("rms_ready"), sem("log_ready"), sem("nat_ready")
        gate_exp, gate_used, merged = sem("gate_exp"), sem("gate_used"), sem("merged")
        f_ready, f_done, logf_ready = sem("f_ready"), sem("f_done"), sem("logf_ready")
        abs_ready, exp_done, log_done, log1m_ready = sem("abs_ready"), sem("exp_done"), sem("log_done"), sem("log1m_ready")
        max_ready = sem("max_ready")
        route_arg, route_exp, assigned = sem("route_arg"), sem("route_exp"), sem("assigned")
        dest_ready, over_ready = sem("dest_ready"), sem("over_ready")
        gathered, combined = [sem(f"gathered{t}") for t in range(NT)], sem("combined")
        gain_loaded, final_ready, stored = sem("gain_loaded"), sem("final_ready"), sem("stored")

        heads_squared = sem("heads_squared")
        m_upper_ready, m_split = sem("m_upper_ready"), sem("m_split")
        out_upper_ready, out_split = sem("out_upper_ready"), sem("out_split")
        unit_done = sem("unit_done")
        x_upper_ready, x_split = sem("x_upper_ready"), sem("x_split")
        w_upper_ready, w_split = sem("w_upper_ready"), sem("w_split")
        x_rest, x_rest_r = (a[:, SLOT_REST, :].rearrange("p (k s) -> p k s", k=KD) for a in (ring, ring_r))
        m_rest, m_rest_r = (a[:, :].rearrange("p (k s) -> p k s", k=KD) for a in (v_log, v_log_r))
        out_upper_r = [ring_r[:, s, :].rearrange("p (k n) -> p k n", k=KD) for s in (SLOT_UPPER, SLOT_REST)]
        w_upper, w_upper_r = (a[:, SLOT_UPPER, :].rearrange("p (u n) -> p u n", u=4) for a in (ring, ring_r))

        class Blocks:
            def __init__(self, tag):
                self.hot_step = sem(f"{tag}_hot_step")
                self.hot_ready = sem(f"{tag}_hot_ready")
                self.xs_summed = sem(f"{tag}_xs_summed")
                self.xs_ready = sem(f"{tag}_xs_ready")
                self.xs_turned = sem(f"{tag}_xs_turned")
                self.xt_ready = sem(f"{tag}_xt_ready")
                self.gate_done = sem(f"{tag}_gate_done")
                self.up_done = sem(f"{tag}_up_done")
                self.exp_done = sem(f"{tag}_exp_done")
                self.sig_step = sem(f"{tag}_sig_step")
                self.hid_ready = sem(f"{tag}_hid_ready")
                self.hid_turned = sem(f"{tag}_hid_turned")
                self.hidt_ready = sem(f"{tag}_hidt_ready")
                self.down_done = sem(f"{tag}_down_done")
                self.y_ready = sem(f"{tag}_y_ready")
                self.y_stored = [sem(f"{tag}_y_stored{b}") for b in range(UNROLL)]

        main, over = Blocks("main"), Blocks("over")
        over_landed, waits_passed = sem("over_landed"), sem("waits_passed")
        block = ctx.enter_context(nc.Block())

        def weights(expert, kind):
            return (w_gate, w_up, w_down)[kind][expert, :, :].rearrange("(h p c) n -> p h (c n)", h=2, p=P)

        def piece(s, width=512):
            return slots[s][:, 0:KD * width].rearrange("p (k n) -> p k n", n=width)

        def unit_parts(n, of=ring, upper_of=w_upper):
            p, u, name = UNITS[n]
            width = sum(w for _, w in PIECES[p])
            whole = of[:, FRONT[p][0], 0:KD * width].rearrange("p (k n) -> p k n", n=width)
            if name is None:
                whole, width = whole[:, :, u * P:(u + 1) * P], P
            else:
                whole = whole[:, 2 * u:2 * u + 2, :]
            return whole, upper_of[:, n % 4, 0:whole.shape[1] * width].rearrange("p (k n) -> p k n", n=width)

        def out_part(n, of=ring):
            half, u = divmod(n, 4)
            return of[:, FRONT[PO0 + half][0], :].rearrange("p (k n) -> p k n", k=KD)[:, 2 * u:2 * u + 2, :]

        def wait_unit(eng, l, n):
            p, u, name = UNITS[n]
            if name and u < 3:
                eng.wait_ge(unit_done, l * 12 + 3 * sum(m % 4 == 3 and UNITS[m][2] is not None for m in range(n)) + u + 1)
            else:
                key = ("T", sum(UNITS[m][2] is None for m in range(n))) if name is None else (name, NT - 1)
                b, fill, _, _ = JOBS[key]
                eng.wait_ge(filled[b], l * FILLS[b] + fill)

        def halves(s):
            return slots[s].rearrange("p (h m) -> p h m", h=2)

        def heads(ap):
            return ap.rearrange("p (h d) -> p h d", d=HD)

        def passed(eng):
            eng.sem_inc(waits_passed, 1)

        def over_count(eng):
            passed(eng)
            return eng.value_load(over_tab[0:1, N_OVER:N_OVER + 1], min_val=0, max_val=N_OVER)

        @block.sync
        def _(sp):
            for t in range(NT):
                sp.dma_start(x[:, t, :], x_in[0, t * P:(t + 1) * P, :]).then_inc(x_loaded[t], 16)
            sp.dma_start(cst[:, :], const[:, 0:N_CONST]).then_inc(const_loaded, 16)
            sp.dma_start(work[:, 0:N_STAGED], const[:, N_CONST:]).then_inc(staged_loaded, 16)
            for l in range(DEPTH):
                sp.dma_start(par_all[:, l, 0:4 * KD], gains[l, :, :]).then_inc(param_loaded, 16)
                for name, src in (("b_forget", b_forget), ("b_group", b_group), ("b_router", b_router)):
                    sp.dma_start(par_all[:, l, PARAM[name]], src[l, :].partition_broadcast(P)).then_inc(param_loaded, 16)

            def load_expert(l, e, u, kind):
                s = EXPERT_SLOTS[u][kind]
                sp.dma_start(halves(s), weights(l * NE + e, kind)).then_inc(landed[s], 16)

            with sp.Fori(0, DEPTH) as l:
                sp.wait_ge(combined, NT + l * NT - 1)
                passed(sp)
                for n in range(N_FRONT):
                    s, _, _ = FRONT[n]
                    if n >= RING:
                        b, fill, _, _ = JOBS[LAST_USE[n - RING]]
                        sp.wait_ge(filled[b], l * FILLS[b] + fill)
                    if n < len(PIECES):
                        width, at = sum(w for _, w in PIECES[n]), 0
                        for col, w in PIECES[n]:
                            src = w_in[l, :, col:col + w].rearrange("(k p) n -> p k n", p=P)
                            sp.dma_start(piece(s, width)[:, :, at:at + w], src).then_inc(landed[s], 16)
                            at += w
                    else:
                        half = n - len(PIECES)
                        src = w_out[l, :, half * 512:(half + 1) * 512].rearrange("(k p) n -> p k n", p=P)
                        sp.dma_start(piece(s), src).then_inc(landed[s], 16)
                    if n == 1:
                        sp.wait_ge(combined, NT + l * NT)
                        sp.dma_start(cos_sin[:, :], rope).then_inc(rope_loaded, 16)
                        sp.dma_start(ret_t, ret_tables).then_inc(ret_loaded, 16)
                        sp.dma_start(wr[:, :, :], w_route[l, :, :].rearrange("(k p) n -> p k n", p=P)).then_inc(route_loaded, 16)
                for u in range(UNROLL):
                    for kind in range(3):
                        b, fill, _, _ = JOBS[last_use(EXPERT_SLOTS[u][kind])]
                        sp.wait_ge(filled[b], l * FILLS[b] + fill)
                        load_expert(l, u, u, kind)
                passed(sp)

                def next_expert(i, u):
                    before = l * NE + (i - 1) * UNROLL + u + 1
                    for kind, used in enumerate((main.gate_done, main.up_done, main.down_done)):
                        sp.wait_ge(used, CREDIT + before)
                        passed(sp)
                        load_expert(l, i * UNROLL + u, u, kind)

                with sp.Fori(1, ROUNDS) as i:
                    for u in range(UNROLL):
                        next_expert(i, u)
                for u in range(LEFT):
                    next_expert(ROUNDS, u)
                sp.wait_ge(over_ready, l + 1)
                n_over = over_count(sp)
                with sp.If(n_over > 0):
                    sp.wait_ge(main.down_done, CREDIT + (l + 1) * NE)
                    passed(sp)
                    with sp.Fori(0, N_OVER) as j:
                        sp.wait_ge(over.down_done, CREDIT + l * N_OVER + j)
                        passed(sp)
                        e = sp.value_load(over_tab[0:1, bass.ds(j, 1)], min_val=0, max_val=NE - 1)
                        for kind in range(3):
                            sp.dma_start(halves(EXPERT_SLOTS[0][kind]), weights(l * NE + e, kind)).then_inc(over_landed, 16)
                with sp.Else():
                    sp.sem_inc(over_landed, 16 * 3 * N_OVER)
            sp.wait_ge(combined, NT + DEPTH * NT)
            sp.dma_start(trn[:, 0:2, :].rearrange("p a s -> p (a s)"), norm_final.partition_broadcast(P)).then_inc(gain_loaded, 16)
            for t in range(NT):
                sp.wait_ge(final_ready, t + 1)
                sp.dma_start(out[0, t * P:(t + 1) * P, :], nat[:, t, :]).then_inc(stored, 16)
            sp.wait_ge(stored, 16 * NT)

        @block.gpsimd
        def _(pool):
            pool.sem_inc(combined, NT)
            for count in (main.down_done, over.down_done, *emptied, main.gate_done, over.gate_done,
                          main.up_done, over.up_done, main.xs_summed, over.xs_summed, main.y_ready, over.y_ready, 
                          *main.y_stored, over.y_stored[0]):
                pool.sem_inc(count, CREDIT)
            pool.wait_ge(zero_set, 1)
            for n in range(RING):
                pool.wait_ge(landed[n], 16 * FRONT[n][2])
            pool.dma_start(over_rows, zeros[0:CAP, :].unsqueeze(1).to_broadcast([CAP, over_rows.shape[1], ZERO_COLS])).then_inc(zeros_written, 16)
            pool.wait_ge(zeros_written, 16)
            with pool.Fori(0, DEPTH) as l:
                b, fill, _, _ = JOBS["vs", NT - 1]
                pool.wait_ge(filled[b], l * FILLS[b] + fill)
                passed(pool)
                for n in range(8):
                    if n % 4 == 0:
                        s, before, k = FRONT[PO0 + n // 4]
                        pool.wait_ge(landed[s], 16 * (l * DMAS[s] + before + k))
                        passed(pool)
                    upper = out_upper_r[n // 4][:, 2 * (n % 4):2 * (n % 4) + 2, :]
                    pool.tensor_copy(upper, out_part(n)).then_inc(out_upper_ready, 1)
                    pool.wait_ge(out_upper_ready, l * 8 + n + 1)
                    passed(pool)
                    pool.tensor_tensor(out_part(n, ring_r), out_part(n), upper.bitcast(F32), ALU.subtract).then_inc(out_split, 1)
                pool.wait_ge(dest_ready, l + 1)
                passed(pool)
                for u in range(UNROLL):
                    pool.wait_ge(main.y_stored[u], CREDIT + (l + 1) * 32 * of_turn(u))
                pool.wait_ge(over.y_stored[0], CREDIT + (l + 1) * 32 * N_OVER)
                passed(pool)
                for t in range(NT):
                    for a in range(2):
                        pool.indirect_dma_start(
                            got[2 * t + a], None, ybuf,
                            bass.IndirectOffsetOnAxis(ap=dest[:, a, t:t + 1], axis=0),
                            bounds_check=ROWS - 1).then_inc(gathered[t], 16)

        @block.scalar
        def _(act):
            def rsqrt(l, stage, n, at=0):
                mean, root = st[:, 0, at:at + n], st[:, 1, at:at + n]
                act.wait_ge(rms_ready, l * RMS_STAGES + stage)
                act.activation(root, mean, ACT.Ln).then_inc(s_step, 1)
                act.wait_ge(s_step, l * RMS_STAGES + stage)
                act.activation(root, root, ACT.Exp, scale=-0.5).then_inc(log_ready, 1)

            def square(t, before):
                if t:
                    act.wait_ge(squared, before + t)
                act.activation(pair, x[:, t, :].rearrange("p (a s) -> p a s", a=2), ACT.Square, accum_out=st[:, 2, t:t + 1]).then_inc(squared, 1)

            def wait_job(l, *key):
                b, fill, _, _ = JOBS[key]
                act.wait_ge(filled[b], l * FILLS[b] + fill)
                return b

            def turned(l, name, gain, t, out=trn):
                b = wait_job(l, name, t, 1)
                for j in range(4):
                    ins = act.activation(out[:, 4 + j, t * P:(t + 1) * P], bank[b][:, j * P:(j + 1) * P],
                                         ACT.Copy, scale=g[gain][:, 4 + j:5 + j])
                ins.then_inc(emptied[b], 1)

            def upper_part(l, n):
                p = UNITS[n][0]
                s, before, k = FRONT[p]
                act.wait_ge(landed[s], 16 * (l * DMAS[s] + before + k))
                if n >= 4:
                    wait_unit(act, l, n - 4)
                whole, upper = unit_parts(n, upper_of=w_upper_r)
                act.activation(upper, whole, ACT.Copy).then_inc(w_upper_ready, 1)

            def merged_tile(l, t):
                turned(l, "m", "g_merged", t, out=m_rest)
                for half in range(2):
                    b, _, _, free = JOBS["m", t, half]
                    act.wait_ge(emptied[b], CREDIT + l * FREES[b] + free)
                cols = slice(t * P, (t + 1) * P)
                act.activation(trn_r[:, :, cols], m_rest[:, :, cols], ACT.Copy).then_inc(m_upper_ready, 1)

            def projected(l, j):
                b = wait_job(l, "T", j)
                scale = HD ** -0.5 if j in (0, 1, 2, 6, 7, 8, 9, 10) else 1.0
                act.activation(qk[:, tile_buffer(j), :], bank[b][:, :], ACT.Copy, scale=scale).then_inc(emptied[b], 1)

            def rows_out(E, n):
                act.wait_ge(E.xs_summed, CREDIT + n + 1)
                act.activation(xs, bank[2][:, :], ACT.Copy).then_inc(E.xs_ready, 1)

            def block_steps(E, n, b, stored_before, ahead=False):
                act.wait_ge(E.gate_done, CREDIT + n + 1)
                act.activation(sg, bank[1][:, 0:256], ACT.Exp, scale=-1.0).then_inc(E.exp_done, 1)
                if ahead:
                    rows_out(E, n + 1)
                act.wait_ge(E.down_done, CREDIT + n + 1)
                act.wait_ge(E.y_stored[b], CREDIT + stored_before)
                act.activation(ys[b], bank[6][:, :], ACT.Copy).then_inc(E.y_ready, 1)
                act.wait_ge(E.y_ready, CREDIT + n + 1)

            def store(E, row, b):
                for h in range(2):
                    act.dma_start(ybuf[bass.ds(row, CAP), h * 512:(h + 1) * 512],
                                  ys[b][h * CAP:(h + 1) * CAP, :]).then_inc(E.y_stored[b], 16)

            with act.Fori(0, DEPTH) as l:
                for t in range(NT):
                    act.wait_ge(x_loaded[t], 16)
                    act.wait_ge(combined, l * NT + t + 1)
                    square(t, l * 2 * NT)
                rsqrt(l, 1, NT)
                act.wait_ge(par_ready, l + 1)
                for t in range(NT):
                    turned(l, "h", "g_mix", t, out=x_rest)
                    b, _, _, free = JOBS["h", t, 0]
                    act.wait_ge(emptied[b], CREDIT + l * FREES[b] + free)
                    b, _, _, free = JOBS["h", t, 1]
                    act.wait_ge(emptied[b], CREDIT + l * FREES[b] + free)
                    cols = slice(t * P, (t + 1) * P)
                    act.activation(trn_r[:, :, cols], x_rest[:, :, cols], ACT.Copy).then_inc(x_upper_ready, 1)
                for n in range(4):
                    upper_part(l, n)
                for j in range(8):
                    projected(l, j)
                    upper_part(l, j + 4)
                for n in range(8, 12):
                    upper_part(l, n + 4)
                for t in range(NT):
                    b = wait_job(l, "vr", t)
                    act.activation(v_ret[:, t, :], bank[b][:, 0:W_RET], ACT.Copy).then_inc(emptied[b], 1)
                act.wait_ge(ret_loaded, 16 * (l + 1))
                for h in range(N_RET):
                    n = NUMBER["ret", h]
                    for i in range(NT - 1):
                        b, _, free, _ = JOBS["rs", h, i]
                        act.wait_ge(emptied[b], CREDIT + l * FREES[b] + free + 1)
                        key = RETC["key_decay"].start + h * NT + i
                        act.activation(probs[:, n % 2, KEY_AT[i] + P:KEY_AT[i] + S - i * P], bank[b][:, P:S - i * P],
                                       ACT.Copy, scale=ret_t[:, key:key + 1]).then_inc(emptied[b], 1)
                    projected(l, 8 + h)
                    upper_part(l, 16 + h)
                for j in range(8 + N_RET, 16):
                    projected(l, j)
                    upper_part(l, j + 8)
                rsqrt(l, 2, NT * N_RET)
                for n in range(20, 24):
                    upper_part(l, n + 4)

                def exp_gate(t):
                    b, _, _, free = JOBS["gate", t]
                    act.wait_ge(emptied[b], CREDIT + l * FREES[b] + free)
                    if t >= 2:
                        act.wait_ge(gate_used, l * NT + t - 1)
                    act.activation(pair[:, t % 2, 0:W_RET], gate_copy[:, t, :], ACT.Exp, scale=-1.0).then_inc(gate_exp, 1)

                for t in range(NT):
                    b = wait_job(l, "gate", t)
                    act.activation(gate_copy[:, t, :], bank[b][:, 0:W_RET], ACT.Copy).then_inc(emptied[b], 1)
                exp_gate(0)
                exp_gate(1)
                for n in range(28, 32):
                    upper_part(l, n)
                for t in range(NT):
                    b, _, free, _ = JOBS["vf", t]
                    act.wait_ge(emptied[b], CREDIT + l * FREES[b] + free + 1)
                    act.activation(v_fox[:, t, :], bank[b][:, 1:1 + W_FOX], ACT.Copy).then_inc(emptied[b], 1)
                act.wait_ge(f_ready, l + 1)
                act.activation(logf[:, 1, :], logf[:, 1, :], ACT.Exp, scale=-1.0).then_inc(f_done, 1)
                act.wait_ge(f_done, l * 2 + 1)
                act.activation(logf[:, 1, :], logf[:, 1, :], ACT.Ln, bias=1.0).then_inc(f_done, 1)
                exp_gate(2)
                exp_gate(3)
                for t in range(NT):
                    b = wait_job(l, "vs", t)
                    act.activation(v_sb[:, t, :], bank[b][:, 0:W_SB], ACT.Copy).then_inc(emptied[b], 1)

                def logs(h):
                    k = l * N_SB + h
                    for n, (tiles, at, end) in enumerate(((1, 0, S), (NT, S, BLOCKS))):
                        act.wait_ge(abs_ready, k * NT + tiles)
                        act.activation(absz[:, at:end], absz[:, at:end], ACT.Exp, scale=-1.0).then_inc(exp_done, 1)
                    for n, (at, end) in enumerate(((0, S), (S, BLOCKS))):
                        act.wait_ge(exp_done, 2 * k + n + 1)
                        act.activation(absz[:, at:end], absz[:, at:end], ACT.Ln, bias=1.0).then_inc(log_done, 1)

                def softmax_rows(h, n):
                    b = JOBS["fs", h, n][0]
                    act.wait_ge(max_ready, (l * N_FOX + h) * len(FOX_JOBS) + n + 1)
                    for t, at in FOX_JOBS[n]:
                        k = h * NT + t
                        ins = act.activation(wide[:, QUERY_AT[t]:QUERY_AT[t] + (t + 1) * P], bank[b][:, at:at + (t + 1) * P],
                                             ACT.Exp, bias=fox_stat[:, 0, k:k + 1], accum_out=fox_stat[:, 1, k:k + 1])
                    ins.then_inc(emptied[b], 1)

                def square_head(kind, h):
                    b, _, _, free = JOBS["o", kind, h]
                    act.wait_ge(emptied[b], CREDIT + l * FREES[b] + free)
                    first, n = (W_RET, h) if kind == "sb" else (W_RET + W_SB, N_SB + h)
                    for t in range(NT):
                        ins = act.activation(pair[:, int(kind == "fox"), t * HD:(t + 1) * HD],
                                             nat[:, t, first + h * HD:first + (h + 1) * HD],
                                             ACT.Square, accum_out=head_sum[:, t, n:n + 1])
                    return ins

                for h in range(N_SB):
                    logs(h)
                    if h == 1:
                        act.wait_ge(gate_used, (l + 1) * NT)
                    if h > 1:
                        act.wait_ge(heads_squared, l * (N_SB - 1) + h - 1)
                    if h:
                        ins = square_head("sb", h - 1)
                        if h > 1:
                            ins = square_head("fox", h - 2)
                        ins.then_inc(heads_squared, 1)
                    n = NUMBER["sb", h]
                    for i in range(NT):
                        b = wait_job(l, "sacc", h, i)
                        act.activation(probs[:, n % 2, KEY_AT[i]:KEY_AT[i] + S - i * P], bank[b][:, 0:S - i * P],
                                       ACT.Exp).then_inc(emptied[b], 1)
                        if i >= 1:
                            softmax_rows(h, i - 1)
                rsqrt(l, 3, NT * (N_SB + N_FOX))
                merged_tile(l, 0)
                merged_tile(l, 1)
                for t in range(NT):
                    b, _, _, free = JOBS["out", t, 1]
                    act.wait_ge(emptied[b], CREDIT + l * FREES[b] + free)
                    square(t, l * 2 * NT + NT)
                    rsqrt(l, 4 + t, 1, at=t)
                    if t + 2 < NT:
                        merged_tile(l, t + 2)
                    if t:
                        turned(l, "g", "g_ffn", t - 1)
                turned(l, "g", "g_ffn", NT - 1)
                for k in range(2):
                    act.wait_ge(route_arg, l * 2 + k + 1)
                    arg = probs[:, 0, 144 + 16 * k:144 + 16 * k + (NG * NT if k == 0 else NT)]
                    act.activation(arg, arg, ACT.Exp).then_inc(route_exp, 1)
                rows_out(main, l * NE)

                def main_block(i, u, ahead):
                    e = i * UNROLL + u
                    block_steps(main, l * NE + e, u, 32 * (l * of_turn(u) + i), ahead=ahead)
                    store(main, e * CAP, u)

                with act.Fori(0, ROUNDS) as i:
                    for u in range(UNROLL):
                        main_block(i, u, True)
                for u in range(LEFT):
                    main_block(ROUNDS, u, u < LEFT - 1)
                act.wait_ge(over_ready, l + 1)
                n_over = over_count(act)
                with act.If(n_over > 0):
                    act.wait_ge(main.y_stored[0], CREDIT + 32 * (l + 1) * of_turn(0))
                    act.wait_ge(zeros_written, 16)
                    with act.Fori(0, N_OVER) as j:
                        rows_out(over, l * N_OVER + j)
                        block_steps(over, l * N_OVER + j, 0, 32 * (l * N_OVER + j))
                        store(over, (NE + j) * CAP, 0)
                with act.Else():
                    act.sem_inc(over.xs_ready, N_OVER)
                    act.sem_inc(over.exp_done, N_OVER)
                    act.sem_inc(over.y_ready, N_OVER)
                    act.sem_inc(over.y_stored[0], 32 * N_OVER)
            for t in range(NT):
                act.wait_ge(combined, DEPTH * NT + t + 1)
                square(t, DEPTH * 2 * NT)
            rsqrt(DEPTH, 1, NT)

        @block.tensor
        def _(pe):
            def begin(l, *key):
                b, _, free, _ = JOBS[key]
                pe.wait_ge(emptied[b], CREDIT + l * FREES[b] + free)
                return b

            def after(l, *key):
                b, _, _, free = JOBS[key]
                pe.wait_ge(emptied[b], CREDIT + l * FREES[b] + free)

            def all_read(l, *keys, job=None):
                last = {}
                for key in keys:
                    b, _, _, free = JOBS[key]
                    last[b] = max(last.get(b, 0), free)
                if job:
                    b, _, free, _ = JOBS[job]
                    last[b] = max(last.get(b, 0), free)
                for b, free in last.items():
                    pe.wait_ge(emptied[b], CREDIT + l * FREES[b] + free)

            def transposes(l, name, t):
                for hh in range(2):
                    b = begin(l, name, t, hh)
                    for j in range(4):
                        k = 4 * hh + j
                        ins = pe.transpose(bank[b][:, j * P:(j + 1) * P], nat[:, t, k * P:(k + 1) * P], c["ident"])
                    ins.then_inc(filled[b], 1)

            def three(dst, x_first, w, x, start, stop):
                for n, (a, b) in enumerate(((0, 0), (0, 1), (1, 0))):
                    lhs, rhs = (x[a], w[b]) if x_first else (w[a], x[b])
                    ins = pe.matmul(dst, lhs, rhs, start=start and n == 0, stop=stop and n == 2)
                return ins

            def tile_T(l, n, j):
                pe.wait_ge(w_split, l * len(UNITS) + n + 1)
                rest, upper = unit_parts(n, ring_r, w_upper_r)
                b = begin(l, "T", j)
                for k in range(KD):
                    ins = three(bank[b][:, :], False, (upper[:, k, :], rest[:, k, :]), (trn_r[:, k, :], x_rest_r[:, k, :]),
                                k == 0, k == KD - 1)
                ins.then_inc(filled[b], 1)

            def tiles_N(l, n0, name):
                banks = [begin(l, name, t) for t in range(NT)]
                for u in range(4):
                    pe.wait_ge(w_split, l * len(UNITS) + n0 + u + 1)
                    rest, upper = unit_parts(n0 + u, ring_r, w_upper_r)
                    width = rest.shape[2]
                    for k in (2 * u, 2 * u + 1):
                        for t in range(NT):
                            cols = slice(t * P, (t + 1) * P)
                            ins = three(bank[banks[t]][:, 0:width], True, (upper[:, k % 2, :], rest[:, k % 2, :]),
                                        (trn_r[:, k, cols], x_rest_r[:, k, cols]), k == 0, k == KD - 1)
                            if k == KD - 1:
                                ins.then_inc(filled[banks[t]], 1)
                    if u < 3:
                        ins.then_inc(unit_done, 1)

            def rotate(l, j):
                after(l, "T", j)
                b = begin(l, "rot", j)
                pe.matmul(bank[b][:, :], c["perm"], qk[:, j, :], start=True, stop=True).then_inc(filled[b], 1)

            def scores_T(l, kind, h, job):
                q, k, odd = qk_place(kind, h)
                part = slice(odd * HD, (odd + 1) * HD)
                for i in range(NT):
                    b = begin(l, job, h, i)
                    pe.matmul(bank[b][:, 0:S - i * P], qk[part, k, i * P:(i + 1) * P], qk[part, q, i * P:S],
                              start=True, stop=True).then_inc(filled[b], 1)

            def sum_values(l, kind, h):
                n = NUMBER[kind, h]
                made_by = {"ret": "rs", "sb": "sacc", "fox": "ft"}[kind]
                all_read(l, *((made_by, h, i) for i in range(3 if kind == "fox" else NT)), job=("o", kind, h))
                b = JOBS["o", kind, h][0]
                for t in range(NT):
                    dst = bank[b][:, t * HD:(t + 1) * HD]
                    for i in range(t + 1):
                        at = QUERY_AT[t] + i * P if kind == "fox" else KEY_AT[i] + (t - i) * P
                        ins = pe.matmul(dst, probs[:, n % 2, at:at + P], values[kind][:, i, h * HD:(h + 1) * HD],
                                        start=i == 0, stop=i == t)
                ins.then_inc(filled[b], 1)

            def fox_scores(l, h, n):
                q, k, odd = qk_place("fox", h)
                part = slice(odd * HD, (odd + 1) * HD)
                b = begin(l, "fs", h, n)
                for t, at in FOX_JOBS[n]:
                    keys = (t + 1) * P
                    dst = bank[b][:, at:at + keys]
                    pe.matmul(dst, qk[part, q, t * P:(t + 1) * P], qk[part, k, 0:keys], start=True, stop=False)
                    pe.matmul(dst, pick_f[:, h:h + 1].to_broadcast([P, P]), neg_f_r[:, 0:keys],
                              start=False, stop=False)
                    ins = pe.matmul(dst[:, t * P:keys], ident_b, causal_b, start=False, stop=True)
                ins.then_inc(filled[b], 1)

            def fox_turn(l, h, n):
                all_read(l, ("fs", h, n), job=("ft", h, n))
                b = JOBS["ft", h, n][0]
                for t, at in FOX_JOBS[n]:
                    for i in range(t + 1):
                        ins = pe.transpose(bank[b][:, at + i * P:at + (i + 1) * P],
                                           wide[:, QUERY_AT[t] + i * P:QUERY_AT[t] + (i + 1) * P], c["ident"])
                ins.then_inc(filled[b], 1)

            def sb_sum(l, h, i):
                b = JOBS["sacc", h, i][0]
                for j in range(i, NT):
                    if i == 0 and j < 2:
                        pe.wait_ge(log1m_ready, (l * N_SB + h) * 2 + j + 1)
                    lhs = neg_from_r if j == i else neg_ones_r
                    for part in (log1m_r, absz_r):
                        pe.matmul(bank[b][:, (j - i) * P:S - i * P], lhs,
                                  part[:, KEY_AT[j]:KEY_AT[j] + S - j * P],
                                  start=False, stop=False, skip_group_check=True)
                pe.matmul(bank[b][:, 0:P], ident_b, strict_b, start=False, stop=True,
                          skip_group_check=True).then_inc(filled[b], 1)

            def pick_rows(E, n):
                pe.wait_ge(E.hot_ready, n + 1)
                for t in range(NT):
                    for half in range(2):
                        ins = pe.matmul(bank[2][half * CAP:(half + 1) * CAP, :], hot[:, 0, t, :],
                                        nat[:, t, half * 512:(half + 1) * 512], start=t == 0, stop=t == NT - 1)
                ins.then_inc(E.xs_summed, 1)

            def turn_rows(E, n):
                pe.wait_ge(E.xs_ready, n + 1)
                for j in range(4):
                    src = xs.rearrange("p (m c) -> p c m", c=4)[:, j, :]
                    ins = pe.transpose(bank[0][:, j * P:(j + 1) * P], src, c["ident"])
                ins.then_inc(E.xs_turned, 1)

            def expert_block(E, n, gate_at, up_at, down_at, ahead=False):
                pe.wait_ge(E.xt_ready, n + 1)
                for (wait, s), dst, done in ((gate_at, bank[1], E.gate_done), (up_at, bank[3], E.up_done)):
                    pe.wait_ge(*wait)
                    w = slots[s].rearrange("p (h c n) -> p h c n", h=2, c=4)
                    for k in range(8):
                        h, j = divmod(k, 4)
                        for half in range(2):
                            ins = pe.matmul(dst[half * CAP:(half + 1) * CAP, 0:256],
                                            xt[:, j * P + h * CAP:j * P + (h + 1) * CAP],
                                            w[:, h, j, half * 256:(half + 1) * 256], start=k == 0, stop=k == 7)
                    ins.then_inc(done, 1)
                if ahead:
                    pick_rows(E, n + 1)
                pe.wait_ge(E.hid_ready, n + 1)
                for j in range(2):
                    src = hid.rearrange("p (m c) -> p c m", c=2)[:, j, :]
                    ins = pe.transpose(bank[5][:, j * P:(j + 1) * P], src, c["ident"])
                ins.then_inc(E.hid_turned, 1)
                if ahead:
                    turn_rows(E, n + 1)
                pe.wait_ge(E.hidt_ready, n + 1)
                pe.wait_ge(E.y_ready, CREDIT + n)
                wait, s = down_at
                pe.wait_ge(*wait)
                w = slots[s].rearrange("p (h c n) -> p h c n", h=2, c=2)
                for k in range(4):
                    h, j = divmod(k, 2)
                    for half in range(2):
                        ins = pe.matmul(bank[6][half * CAP:(half + 1) * CAP, :],
                                        hidt[:, j * P + h * CAP:j * P + (h + 1) * CAP],
                                        w[:, h, j, half * 512:(half + 1) * 512], start=k == 0, stop=k == 3)
                ins.then_inc(E.down_done, 1)

            pe.wait_ge(const_loaded, 16)
            with pe.Fori(0, DEPTH) as l:
                for t in range(NT):
                    pe.wait_ge(nat_ready, l * 2 * NT + t + 1)
                    transposes(l, "h", t)
                pe.wait_ge(x_split, (l + 1) * NT)
                for j in range(8):
                    tile_T(l, j, j)
                    if j >= 2:
                        rotate(l, j - 2)
                tiles_N(l, 8, "vr")
                all_read(l, *(("rot", j) for j in range(6)), *(("vr", t) for t in range(NT)))
                for h in range(N_RET):
                    scores_T(l, "ret", h, "rs")
                    if h:
                        sum_values(l, "ret", h - 1)
                    tile_T(l, 12 + h, 8 + h)
                sum_values(l, "ret", N_RET - 1)
                for j in range(8 + N_RET, 16):
                    tile_T(l, j + 4, j)
                tiles_N(l, 20, "gate")
                tiles_N(l, 24, "vf")
                tiles_N(l, 28, "vs")
                pe.wait_ge(logf_ready, l + 1)
                b = begin(l, "F")
                for q in range(NT):
                    for t in range(q + 1):
                        ins = pe.matmul(bank[b][0:N_FOX, q * P:(q + 1) * P], logf[:, 0, t * N_FOX:(t + 1) * N_FOX],
                                        c["neg_upto"] if t == q else c["neg_ones"], start=t == 0, stop=t == q)
                ins.then_inc(filled[b], 1)
                all_read(l, *(("T", j) for j in range(6, 16)), *(("vf", t) for t in range(NT)),
                         *(("vs", t) for t in range(NT)), ("F",))
                for h in range(N_SB + 1):
                    if h < N_SB:
                        scores_T(l, "sb", h, "sz")
                    if h:
                        for n in range(3):
                            fox_turn(l, h - 1, n)
                        sum_values(l, "sb", h - 1)
                        sum_values(l, "fox", h - 1)
                    if h < N_SB:
                        for n in range(3):
                            fox_scores(l, h, n)
                        for i in range(NT):
                            sb_sum(l, h, i)
                pe.wait_ge(out_split, (l + 1) * 8)
                pe.wait_ge(route_loaded, 16 * (l + 1))
                for kind, t in OUT_ORDER:
                    if kind == "m":
                        pe.wait_ge(merged, l * NT + t + 1)
                        transposes(l, "m", t)
                    elif kind == "g":
                        pe.wait_ge(nat_ready, l * 2 * NT + NT + t + 1)
                        transposes(l, "g", t)
                    elif kind == "out":
                        pe.wait_ge(m_split, l * NT + t + 1)
                        cols = slice(t * P, (t + 1) * P)
                        for half in range(2):
                            b = begin(l, "out", t, half)
                            for k in range(KD):
                                rest = out_part(4 * half + k // 2, ring_r)[:, k % 2, :]
                                ins = three(bank[b][:, :], True, (out_upper_r[half][:, k, :], rest),
                                            (trn_r[:, k, cols], m_rest_r[:, k, cols]), k == 0, k == KD - 1)
                            ins.then_inc(filled[b], 1)
                    else:
                        if t == 0:
                            b = begin(l, "route")
                            passed(pe)
                        b = JOBS["route",][0]
                        all_read(l, ("g", t, 0), ("g", t, 1))
                        for k in range(KD):
                            ins = pe.matmul(bank[b][:, t * 36:(t + 1) * 36], trn[:, k, t * P:(t + 1) * P], wr[:, k, :],
                                            start=k == 0, stop=k == KD - 1)
                        if t == NT - 1:
                            ins.then_inc(filled[b], 1)
                pe.wait_ge(assigned, l + 1)
                b = begin(l, "pos")
                for q in range(NT + 1):
                    for t in range(min(q, NT - 1) + 1):
                        own = t == q
                        ins = pe.matmul(bank[b][:, q * NE:(q + 1) * NE], count_mats[:, 0:P] if own else count_mats[:, P:2 * P],
                                        assigned_to[:, 0 if own else 1, t, :], start=t == 0, stop=t == min(q, NT - 1))
                ins.then_inc(filled[b], 1)

                def main_block(i, u, ahead):
                    at = []
                    for kind in range(3):
                        s = EXPERT_SLOTS[u][kind]
                        at.append(((landed[s], 16 * (l * DMAS[s] + DMAS0[s] + i + 1)), s))
                    expert_block(main, l * NE + i * UNROLL + u, *at, ahead=ahead)

                pick_rows(main, l * NE)
                turn_rows(main, l * NE)
                with pe.Fori(0, ROUNDS) as i:
                    for u in range(UNROLL):
                        main_block(i, u, True)
                for u in range(LEFT):
                    main_block(ROUNDS, u, u < LEFT - 1)
                pe.wait_ge(over_ready, l + 1)
                n_over = over_count(pe)
                with pe.If(n_over > 0):
                    with pe.Fori(0, N_OVER) as j:
                        n = l * N_OVER + j
                        at = [((over_landed, 48 * (n + 1)), EXPERT_SLOTS[0][kind]) for kind in range(3)]
                        pe.wait_ge(main.y_ready, CREDIT + (l + 1) * NE)
                        pick_rows(over, n)
                        turn_rows(over, n)
                        expert_block(over, n, *at)
                with pe.Else():
                    for s in (over.xs_summed, over.xs_turned, over.gate_done, over.up_done, over.hid_turned, over.down_done):
                        pe.sem_inc(s, N_OVER)

        @block.vector
        def _(v):
            base, count = [0], [0]

            def step(ins):
                count[0] += 1
                ins.then_inc(v_step, 1)
                v.wait_ge(v_step, base[0] + count[0])

            def wait_job(l, *key):
                b, fill, _, _ = JOBS[key]
                v.wait_ge(filled[b], l * FILLS[b] + fill)
                return b

            def wait_read(l, *key):
                b, _, _, free = JOBS[key]
                v.wait_ge(emptied[b], CREDIT + l * FREES[b] + free)

            def tt(out, a, b, op):
                return v.tensor_tensor(out, a, b, op)

            def magnitude(out, a):
                return v.tensor_scalar(out.bitcast(I32), a.bitcast(I32), 0x7FFFFFFF, None, ALU.bitwise_and)

            def newton(n, at):
                m, y, a = st[:, 0, at:at + n], st[:, 1, at:at + n], st[:, 2, at:at + n]
                step(tt(a, y, y, ALU.mult))
                step(v.scalar_tensor_tensor(out=a, in0=a, scalar=-0.5, in1=m, op0=ALU.mult, op1=ALU.mult))
                step(v.scalar_tensor_tensor(out=y, in0=a, scalar=1.5, in1=y, op0=ALU.add, op1=ALU.mult))

            def mean(n, width, at=0):
                v.tensor_scalar(st[:, 0, at:at + n], st[:, 2, at:at + n], 1.0 / width, EPS, ALU.mult, ALU.add).then_inc(rms_ready, 1)

            def inverse_root(l, stage, n, at=0):
                v.wait_ge(rms_ready, l * RMS_STAGES + stage)
                v.wait_ge(log_ready, l * RMS_STAGES + stage)
                newton(n, at)

            def mean_rsqrt(l, stage, n, width):
                mean(n, width)
                inverse_root(l, stage, n)

            def normalise(t):
                v.tensor_scalar(nat[:, t, :], x[:, t, :], st[:, 1, t:t + 1], None, ALU.mult).then_inc(nat_ready, 1)

            def rest_of_x(l, t):
                v.wait_ge(x_upper_ready, l * NT + t + 1)
                cols = slice(t * P, (t + 1) * P)
                tt(x_rest_r[:, :, cols], x_rest[:, :, cols], trn_r[:, :, cols].bitcast(F32), ALU.subtract).then_inc(x_split, 1)

            def rest_of_merged(l, t):
                v.wait_ge(m_upper_ready, l * NT + t + 1)
                cols = slice(t * P, (t + 1) * P)
                tt(m_rest_r[:, :, cols], m_rest[:, :, cols], trn_r[:, :, cols].bitcast(F32), ALU.subtract).then_inc(m_split, 1)

            def rest_of_weights(l, n):
                v.wait_ge(w_upper_ready, l * len(UNITS) + n + 1)
                whole, upper = unit_parts(n, upper_of=w_upper_r)
                tt(unit_parts(n, ring_r)[0], whole, upper.bitcast(F32), ALU.subtract).then_inc(w_split, 1)

            def turned(l, name, gain, t, out=trn):
                b = wait_job(l, name, t, 0)
                tt(out[:, 0:4, t * P:(t + 1) * P], bank[b][:, :].rearrange("p (j n) -> p j n", j=4),
                   g[gain][:, 0:4].unsqueeze(2).to_broadcast([P, 4, P]), ALU.mult).then_inc(emptied[b], 1)

            def rotary(l, j):
                b = wait_job(l, "rot", j)
                v.tensor_tensor(pair[:, j % 2, :], bank[b][:, :], sin_t, ALU.mult)
                step(v.tensor_tensor(qk[:, j, :], qk[:, j, :], cos_t, ALU.mult))
                tt(qk[:, j, :], qk[:, j, :], pair[:, j % 2, :], ALU.add).then_inc(emptied[b], 1)

            def head_out(l, kind, h):
                b = wait_job(l, "o", kind, h)
                src = bank[b][:, 0:NT * HD].rearrange("p (t d) -> p t d", d=HD)
                col = {"ret": 0, "sb": W_RET, "fox": W_RET + W_SB}[kind] + h * HD
                dst = nat[:, :, col:col + HD]
                if kind == "sb":
                    v.tensor_copy(dst, src).then_inc(emptied[b], 1)
                    return
                if kind == "ret":
                    q = RETC["query_decay"].start + h * NT
                    by = ret_t[:, q:q + NT]
                else:
                    by = fox_stat[:, 1, h * NT:(h + 1) * NT]
                    step(v.reciprocal(by, by))
                tt(dst, src, by.unsqueeze(2).to_broadcast([P, NT, HD]), ALU.mult).then_inc(emptied[b], 1)

            def group_norm_ret(l):
                wait_read(l, "o", "ret", N_RET - 1)
                for t in range(NT):
                    ins = v.tensor_reduce(st[:, 2, t * N_RET:(t + 1) * N_RET], heads(nat[:, t, 0:W_RET]), AXX, ALU.add)
                step(ins)
                step(v.tensor_scalar(st[:, 1, 0:NT * N_RET], st[:, 2, 0:NT * N_RET], 1.0 / HD, None, ALU.mult))
                for t in range(NT):
                    o = heads(nat[:, t, 0:W_RET])
                    ins = tt(o, o, st[:, 1, t * N_RET:(t + 1) * N_RET].unsqueeze(2).to_broadcast([P, N_RET, HD]), ALU.subtract)
                step(ins)
                flat = probs[:, :, :].rearrange("p b n -> p (b n)")
                for t in range(NT):
                    o = nat[:, t, 0:W_RET]
                    ins = tt(flat[:, t * W_RET:(t + 1) * W_RET], o, o, ALU.mult)
                step(ins)
                for t in range(NT):
                    ins = v.tensor_reduce(st[:, 2, t * N_RET:(t + 1) * N_RET], heads(flat[:, t * W_RET:(t + 1) * W_RET]), AXX, ALU.add)
                step(ins)
                mean_rsqrt(l, 2, NT * N_RET, HD)
                for t in range(NT):
                    o = heads(nat[:, t, 0:W_RET])
                    ins = tt(o, o, st[:, 1, t * N_RET:(t + 1) * N_RET].unsqueeze(2).to_broadcast([P, N_RET, HD]), ALU.mult)
                step(ins)

            def gate_ret(l, t):
                e = pair[:, t % 2, 0:W_RET]
                v.wait_ge(gate_exp, l * NT + t + 1)
                step(v.tensor_scalar(e, e, 1.0, None, ALU.add))
                step(v.reciprocal(e, e))
                step(tt(e, gate_copy[:, t, :], e, ALU.mult))
                o = nat[:, t, 0:W_RET]
                tt(o, o, e, ALU.mult).then_inc(gate_used, 1)

            def head_square_sum(l, kind, h):
                wait_read(l, "o", kind, h)
                col, n = {"sb": W_RET, "fox": W_RET + W_SB}[kind] + h * HD, h if kind == "sb" else N_SB + h
                o = nat[:, :, col:col + HD]
                squares = pair[:, int(kind == "fox"), 0:NT * HD].rearrange("p (t d) -> p t d", d=HD)
                step(tt(squares, o, o, ALU.mult))
                return v.tensor_reduce(head_sum[:, :, n], squares, AXX, ALU.add)

            def rms_heads(l, t):
                nh = N_SB + N_FOX
                o = heads(nat[:, t, W_RET:D])
                tt(o, o, st[:, 1, t * nh:(t + 1) * nh].unsqueeze(2).to_broadcast([P, nh, HD]), ALU.mult).then_inc(merged, 1)

            def forget_gates(l):
                for t in range(NT):
                    b = wait_job(l, "vf", t)
                    tt(logf[:, 0, t * N_FOX:(t + 1) * N_FOX], bank[b][:, 1 + W_FOX:1 + W_FOX + N_FOX], g["b_forget"],
                       ALU.add).then_inc(emptied[b], 1)
                for t in range(NT):
                    b, _, free, _ = JOBS["vf", t]
                    v.wait_ge(emptied[b], CREDIT + l * FREES[b] + free + 1)
                magnitude(logf[:, 1, :], logf[:, 0, :]).then_inc(f_ready, 1)
                v.wait_ge(f_done, l * 2 + 2)
                v.scalar_tensor_tensor(out=logf[:, 0, :], in0=logf[:, 0, :], scalar=0.0, in1=logf[:, 1, :],
                                       op0=ALU.min, op1=ALU.subtract).then_inc(logf_ready, 1)

            def sb_abs(l, h, i):
                b = wait_job(l, "sz", h, i)
                magnitude(absz[:, KEY_AT[i]:KEY_AT[i] + S - i * P], bank[b][:, 0:S - i * P]).then_inc(abs_ready, 1)

            def sb_log1m(l, h):
                for i in range(NT):
                    if i < 2:
                        v.wait_ge(log_done, (l * N_SB + h) * 2 + i + 1)
                    at = absz[:, KEY_AT[i]:KEY_AT[i] + S - i * P]
                    ins = v.scalar_tensor_tensor(out=at, in0=bank[JOBS["sz", h, i][0]][:, 0:S - i * P], scalar=0.0,
                                                 in1=at, op0=ALU.max, op1=ALU.add)
                step(ins)
                for i in range(NT):
                    at = absz[:, KEY_AT[i]:KEY_AT[i] + P]
                    ins = tt(at, at, c["strict"], ALU.mult)
                step(ins)
                parts = slice(0, S), slice(S, BLOCKS)
                for part in parts:
                    ins = v.tensor_copy(log1m_r[:, part], absz[:, part])
                step(ins)
                for part in parts:
                    tt(absz_r[:, part], absz[:, part], log1m_r[:, part].bitcast(F32), ALU.subtract).then_inc(log1m_ready, 1)

            def fox_max(l, h, n):
                b = wait_job(l, "fs", h, n)
                for t, at in FOX_JOBS[n]:
                    k = h * NT + t
                    ins = v.tensor_reduce(fox_stat[:, 0, k:k + 1], bank[b][:, at:at + (t + 1) * P], AXX, ALU.max, negate=True)
                ins.then_inc(max_ready, 1)

            def fox_turned(l, h, n):
                b = wait_job(l, "ft", h, n)
                t, cols = FOX_JOBS[n][0][0], sum((t + 1) * P for t, _ in FOX_JOBS[n])
                v.tensor_copy(probs[:, NUMBER["fox", h] % 2, QUERY_AT[t]:QUERY_AT[t] + cols],
                              bank[b][:, 0:cols]).then_inc(emptied[b], 1)

            def argmax(o, src, mx, ties, rank, n):
                wide_of = lambda a: a.unsqueeze(2).to_broadcast([P, NT, n])
                step(v.tensor_reduce(mx, src, AXX, ALU.max))
                step(tt(o, src, wide_of(mx), ALU.is_equal))
                step(tt(o, o, rank.unsqueeze(1).to_broadcast([P, NT, n]), ALU.mult))
                step(v.tensor_reduce(ties, o, AXX, ALU.max))
                step(tt(o, o, wide_of(ties), ALU.is_equal))

            def route(l):
                top, flat = [0], probs[:, :, :].rearrange("p b n -> p (b n)")

                def take(n, at=None):
                    if at is None:
                        at = top[0]
                        top[0] += n
                    return flat[:, at:at + n]
                logits = take(NT * (NG + NE)).rearrange("p (t n) -> p t n", t=NT)
                e_group = take(NT * NG).rearrange("p (t n) -> p t n", t=NT)
                e_top = take(NT)
                top[0] = 192
                small = [take(NT) for _ in range(6)]
                onehot_g = take(NT * NG).rearrange("p (t n) -> p t n", t=NT)
                three = lambda a: a.rearrange("p (t n) -> p t n", t=NT)
                el, o1, o2, tmp = (three(take(NT * NE)) for _ in range(4))
                top[0] = BLOCKS + 2 * NT * NE
                where = three(take(NT * NE))
                counts, nblocks, before, shift = (take(NE) for _ in range(4))
                cmp7 = take(NE * 7).rearrange("p (e m) -> p e m", m=7)
                cmp15 = take(N_OVER * NE).rearrange("p (j e) -> p j e", e=NE)
                owner = take(16)
                m_g, s_g, p_g, m_1, m_2, r = small
                bc = lambda a, n: a.unsqueeze(2).to_broadcast([P, NT, n])

                b = wait_job(l, "route")
                bias = par[:, PARAM["b_group"].start:PARAM["b_router"].stop]
                tt(logits, bank[b][:, 0:NT * 36].rearrange("p (t n) -> p t n", t=NT),
                   bias.unsqueeze(1).to_broadcast([P, NT, NG + NE]), ALU.add).then_inc(emptied[b], 1)
                v.wait_ge(emptied[b], CREDIT + l * FREES[b] + JOBS["route",][3])
                argmax(onehot_g, logits[:, :, 0:NG], m_g, r, c["rank4"], NG)
                tt(e_group, logits[:, :, 0:NG], bc(m_g, NG), ALU.subtract).then_inc(route_arg, 1)
                step(v.tensor_scalar(onehot_g, onehot_g, BIG, -BIG, ALU.mult, ALU.add))
                for q in range(NG):
                    part = slice(q * EPG, (q + 1) * EPG)
                    ins = tt(el[:, :, part], logits[:, :, NG + q * EPG:NG + (q + 1) * EPG],
                             onehot_g[:, :, q:q + 1].to_broadcast([P, NT, EPG]), ALU.add)
                step(ins)
                argmax(o1, el, m_1, r, c["rank32"], NE)
                step(v.scalar_tensor_tensor(out=el, in0=o1, scalar=-3.0 * BIG, in1=el, op0=ALU.mult, op1=ALU.add))
                argmax(o2, el, m_2, r, c["rank32"], NE)
                tt(e_top, m_2, m_1, ALU.subtract).then_inc(route_arg, 1)
                step(tt(assigned_to[:, 0, :, :], o1, o2, ALU.add))
                v.tensor_scalar(assigned_to[:, 1, :, :], assigned_to[:, 0, :, :], -1.0, None, ALU.mult).then_inc(assigned, 1)
                v.wait_ge(route_exp, 2 * l + 1)
                step(v.tensor_reduce(s_g, e_group, AXX, ALU.add))
                step(v.reciprocal(p_g, s_g))
                v.wait_ge(route_exp, 2 * l + 2)
                step(v.tensor_scalar(r, e_top, 1.0, None, ALU.add))
                step(v.reciprocal(r, r))
                step(tt(gates[:, 0, :], r, p_g, ALU.mult))
                step(tt(gates[:, 1, :], e_top, gates[:, 0, :], ALU.mult))
                b = wait_job(l, "pos")
                v.tensor_copy(where, bank[b][:, 0:NT * NE].rearrange("p (t n) -> p t n", t=NT))
                v.tensor_copy(counts, bank[b][:, NT * NE:(NT + 1) * NE]).then_inc(emptied[b], 1)
                v.wait_ge(emptied[b], CREDIT + l * FREES[b] + JOBS["pos",][3])
                step(tt(cmp7, counts.unsqueeze(2).to_broadcast([P, NE, 7]),
                        c["thresholds"].unsqueeze(1).to_broadcast([P, NE, 7]), ALU.is_gt))
                step(v.tensor_reduce(nblocks, cmp7, AXX, ALU.add))
                a, z, other = nblocks, shift, before
                for d in (1, 2, 4, 8, 16):
                    v.tensor_copy(z[:, 0:d], a[:, 0:d])
                    step(tt(z[:, d:NE], a[:, d:NE], a[:, 0:NE - d], ALU.add))
                    a, z, other = z, other, z
                step(tt(z, a, nblocks, ALU.subtract))
                step(v.scalar_tensor_tensor(out=z, in0=z, scalar=float(CAP), in1=c["over_base"], op0=ALU.mult, op1=ALU.add))
                step(v.tensor_scalar(tmp, where, float(CAP), None, ALU.is_ge))
                step(tt(tmp, tmp, z.unsqueeze(1).to_broadcast([P, NT, NE]), ALU.mult))
                step(tt(where, where, c["e64"].unsqueeze(1).to_broadcast([P, NT, NE]), ALU.add))
                step(tt(where, where, tmp, ALU.add))
                tt(o1, o1, where, ALU.mult)
                step(tt(o2, o2, where, ALU.mult))
                v.tensor_reduce(rel[:, 0:NT], o1, AXX, ALU.add)
                step(v.tensor_reduce(rel[:, NT:2 * NT], o2, AXX, ALU.add))

                def rest():
                    v.tensor_copy(dest[:, :, :].rearrange("p a t -> p (a t)"), rel).then_inc(dest_ready, 1)
                    step(tt(cmp15, a.unsqueeze(1).to_broadcast([P, N_OVER, NE]),
                            c["block_no"].unsqueeze(2).to_broadcast([P, N_OVER, NE]), ALU.is_le))
                    step(v.tensor_reduce(owner[:, 0:N_OVER], cmp15, AXX, ALU.add))
                    step(v.tensor_scalar(owner[:, 0:N_OVER], owner[:, 0:N_OVER], float(NE - 1), None, ALU.min))
                    step(v.tensor_copy(owner[:, N_OVER:16], a[:, NE - 1:NE]))
                    v.tensor_copy(over_tab[:, :], owner[0:1, :]).then_inc(over_ready, 1)
                return rest

            def mark_rows(E, n):
                v.wait_ge(E.xs_summed, CREDIT + n)
                v.tensor_scalar(rel, rel, -float(CAP), None, ALU.add).then_inc(E.hot_step, 1)
                v.wait_ge(E.hot_step, 2 * n + 1)
                tt(hot[:, :, :, :].rearrange("p a t s -> p (a t) s"), rel.unsqueeze(2).to_broadcast([P, 2 * NT, CAP]),
                   c["row_no"].unsqueeze(1).to_broadcast([P, 2 * NT, CAP]), ALU.is_equal).then_inc(E.hot_step, 1)
                v.wait_ge(E.hot_step, 2 * n + 2)
                tt(hot[:, 0, :, :], hot[:, 0, :, :], hot[:, 1, :, :], ALU.add).then_inc(E.hot_ready, 1)

            def rows_turned(E, n):
                v.wait_ge(E.xs_turned, n + 1)
                tt(xt.rearrange("p (f s) -> p f s", s=CAP), bank[0][:, :].rearrange("p (f s) -> p f s", s=CAP),
                   g["g_expert"].unsqueeze(2).to_broadcast([P, KD, CAP]), ALU.mult).then_inc(E.xt_ready, 1)

            def expert_block(E, n, ahead=False):
                if ahead:
                    mark_rows(E, n + 1)
                v.wait_ge(E.exp_done, n + 1)
                v.tensor_scalar(sg, sg, 1.0, None, ALU.add).then_inc(E.sig_step, 1)
                v.wait_ge(E.sig_step, 4 * n + 1)
                v.reciprocal(sg, sg).then_inc(E.sig_step, 1)
                v.wait_ge(E.sig_step, 4 * n + 2)
                tt(sg, bank[1][:, 0:256], sg, ALU.mult).then_inc(E.sig_step, 1)
                v.wait_ge(E.sig_step, 4 * n + 3)
                v.wait_ge(E.up_done, CREDIT + n + 1)
                tt(hid, bank[3][:, 0:256], sg, ALU.mult).then_inc(E.hid_ready, 1)
                v.wait_ge(E.hid_turned, n + 1)
                v.tensor_copy(hidt, bank[5][:, 0:256]).then_inc(E.hidt_ready, 1)
                v.sem_inc(E.sig_step, 1)
                if ahead:
                    rows_turned(E, n + 1)

            v.memset(zeros[:, :], 0.0).then_inc(zero_set, 1)
            v.wait_ge(const_loaded, 16)
            v.wait_ge(staged_loaded, 16)
            v.tensor_copy(ident_b, c["ident"])
            v.tensor_copy(strict_b, staged["strict_add"])
            v.tensor_copy(causal_b, staged["causal_add"])
            v.tensor_copy(neg_from_r, staged["neg_from"])
            v.tensor_copy(neg_ones_r, c["neg_ones"])
            tt(pick_f[:, :], c["ident"][:, 0:N_FOX], c["ident"][:, 32:32 + N_FOX], ALU.add)
            v.tensor_copy(count_mats[:, 0:P], c["strict"])
            v.tensor_copy(count_mats[:, P:2 * P], c["neg_ones"])
            v.wait_ge(param_loaded, 16 * 4 * DEPTH)
            for t in range(NT):
                v.wait_ge(x_loaded[t], 16)
            with v.Fori(0, DEPTH) as l:
                base[0], count[0] = l * V_STEPS, 0
                v.tensor_copy(par[:, :], par_all[:, bass.ds(l, 1), :].rearrange("p a n -> p (a n)")).then_inc(par_ready, 1)
                v.wait_ge(par_ready, l + 1)
                v.wait_ge(squared, l * 2 * NT + NT)
                mean_rsqrt(l, 1, NT, D)
                for t in range(NT):
                    normalise(t)
                for t in range(NT):
                    turned(l, "h", "g_mix", t, out=x_rest)
                    if t:
                        rest_of_x(l, t - 1)
                rest_of_x(l, NT - 1)
                for n in range(4):
                    rest_of_weights(l, n)
                for j in range(8):
                    if j == 2:
                        v.wait_ge(rope_loaded, 16 * (l + 1))
                    if j >= 2:
                        rotary(l, j - 2)
                    rest_of_weights(l, j + 4)
                for n in range(8, 12):
                    rest_of_weights(l, n + 4)
                v.wait_ge(ret_loaded, 16 * (l + 1))
                for h in range(N_RET):
                    n = NUMBER["ret", h]
                    for i in range(NT):
                        b = wait_job(l, "rs", h, i)
                        v.scalar_tensor_tensor(out=probs[:, n % 2, KEY_AT[i]:KEY_AT[i] + P], in0=bank[b][:, 0:P],
                                               scalar=gamma_tile[h] ** i, in1=ret_t[:, h * P:(h + 1) * P],
                                               op0=ALU.mult, op1=ALU.mult).then_inc(emptied[b], 1)
                    if h:
                        head_out(l, "ret", h - 1)
                    rest_of_weights(l, 16 + h)
                head_out(l, "ret", N_RET - 1)
                rest_of_weights(l, 22)
                rest_of_weights(l, 23)
                group_norm_ret(l)
                for n in range(20, 24):
                    rest_of_weights(l, n + 4)
                gate_ret(l, 0)
                rest_of_weights(l, 28)
                gate_ret(l, 1)
                for n in range(29, 32):
                    rest_of_weights(l, n)
                forget_gates(l)
                gate_ret(l, 2)
                gate_ret(l, 3)
                b = wait_job(l, "F")
                for part in range(S // ZERO_COLS):
                    ins = v.tensor_copy(neg_f_r[:, part * ZERO_COLS:(part + 1) * ZERO_COLS], zeros[:, :])
                step(ins)
                step(v.tensor_copy(neg_f_r[0:N_FOX, :], bank[b][0:N_FOX, :]))
                tt(neg_f_r[32:32 + N_FOX, :], bank[b][0:N_FOX, :], neg_f_r[0:N_FOX, :].bitcast(F32),
                   ALU.subtract).then_inc(emptied[b], 1)
                for h in range(N_SB + 1):
                    if h < N_SB:
                        for i in range(NT):
                            sb_abs(l, h, i)
                    else:
                        v.wait_ge(heads_squared, (l + 1) * (N_SB - 1))
                        step(head_square_sum(l, "fox", N_SB - 2))
                    if h:
                        for n in range(3):
                            fox_turned(l, h - 1, n)
                        head_out(l, "sb", h - 1)
                    if h < N_SB:
                        sb_log1m(l, h)
                    else:
                        head_square_sum(l, "sb", N_SB - 1)
                    if h:
                        head_out(l, "fox", h - 1)
                    if h < N_SB:
                        for n in range(3):
                            fox_max(l, h, n)
                step(head_square_sum(l, "fox", N_SB - 1))
                mean_rsqrt(l, 3, NT * (N_SB + N_FOX), HD)
                rms_heads(l, 0)
                rms_heads(l, 1)
                turned(l, "m", "g_merged", 0, out=m_rest)
                rms_heads(l, 2)
                rest_of_merged(l, 0)
                turned(l, "m", "g_merged", 1, out=m_rest)
                rms_heads(l, 3)
                rest_of_merged(l, 1)
                for t in range(NT):
                    for half in range(2):
                        b = wait_job(l, "out", t, half)
                        cols = x[:, t, half * 512:(half + 1) * 512]
                        tt(cols, bank[b][:, :], cols, ALU.add).then_inc(emptied[b], 1)
                    v.wait_ge(squared, l * 2 * NT + NT + t + 1)
                    mean(1, D, at=t)
                    if t + 2 < NT:
                        turned(l, "m", "g_merged", t + 2, out=m_rest)
                    if t:
                        turned(l, "g", "g_ffn", t - 1)
                    inverse_root(l, 4 + t, 1, at=t)
                    normalise(t)
                    if t + 2 < NT:
                        rest_of_merged(l, t + 2)
                turned(l, "g", "g_ffn", NT - 1)
                rest_of_route = route(l)
                mark_rows(main, l * NE)
                rest_of_route()
                rows_turned(main, l * NE)
                with v.Fori(0, NE - 1) as e:
                    expert_block(main, l * NE + e, ahead=True)
                expert_block(main, l * NE + NE - 1)
                v.wait_ge(over_ready, l + 1)
                n_over = over_count(v)
                with v.If(n_over > 0):
                    with v.Fori(0, N_OVER) as j:
                        mark_rows(over, l * N_OVER + j)
                        rows_turned(over, l * N_OVER + j)
                        expert_block(over, l * N_OVER + j)
                with v.Else():
                    v.sem_inc(over.hot_step, 2 * N_OVER)
                    for s in (over.hot_ready, over.xt_ready, over.hid_ready, over.hidt_ready):
                        v.sem_inc(s, N_OVER)
                    v.sem_inc(over.sig_step, 4 * N_OVER)
                for t in range(NT):
                    v.wait_ge(gathered[t], 32 * (l + 1))
                    step(v.scalar_tensor_tensor(out=x[:, t, :], in0=got[2 * t], scalar=gates[:, 0, t:t + 1],
                                                in1=x[:, t, :], op0=ALU.mult, op1=ALU.add))
                    v.scalar_tensor_tensor(out=x[:, t, :], in0=got[2 * t + 1], scalar=gates[:, 1, t:t + 1],
                                           in1=x[:, t, :], op0=ALU.mult, op1=ALU.add).then_inc(combined, 1)
            assert count[0] == V_STEPS, count[0]
            base[0], count[0] = DEPTH * V_STEPS, 0
            v.wait_ge(combined, NT + DEPTH * NT)
            v.wait_ge(squared, DEPTH * 2 * NT + NT)
            mean_rsqrt(DEPTH, 1, NT, D)
            v.wait_ge(gain_loaded, 16)
            for t in range(NT):
                step(v.tensor_scalar(nat[:, t, :], x[:, t, :], st[:, 1, t:t + 1], None, ALU.mult))
                tt(nat[:, t, :], nat[:, t, :], trn[:, 0:2, :].rearrange("p a s -> p (a s)"), ALU.mult).then_inc(final_ready, 1)


def kernel(x, norm_mix, w_in, b_forget, g_ret, g_sb, g_fox, w_out, norm_ffn, w_group, b_group, w_router,
           b_router, w_gate, w_up, w_down, norm_final):
    from concourse import bacc
    from concourse.bass_utils import run_bass_kernel_spmd

    by_chunk = lambda a: np.asarray(a).reshape(DEPTH, KD, P).transpose(0, 2, 1)
    merged = np.concatenate([np.asarray(g_ret), np.asarray(g_sb), np.asarray(g_fox)], axis=1)
    by_expert = np.asarray(norm_ffn).reshape(DEPTH, 2, P, 4).transpose(0, 2, 3, 1).reshape(DEPTH, P, KD)
    const, rope, ret, gamma_tile = shape_constants()
    arrays = {
        "x_in": x, "w_in": w_in, "w_out": w_out,
        "w_route": np.concatenate([np.asarray(w_group), np.asarray(w_router)], axis=2),
        "w_gate": np.asarray(w_gate).reshape(DEPTH * NE, D, DE), "w_up": np.asarray(w_up).reshape(DEPTH * NE, D, DE),
        "w_down": np.asarray(w_down).reshape(DEPTH * NE, DE, D),
        "gains": np.concatenate([by_chunk(norm_mix), by_chunk(merged), by_chunk(norm_ffn), by_expert], axis=2),
        "b_forget": b_forget, "b_group": b_group, "b_router": b_router, "norm_final": norm_final,
        "const": const, "rope": rope, "ret_tables": ret,
    }
    arrays = {k: np.ascontiguousarray(v) for k, v in arrays.items()}
    nc = bacc.Bacc("TRN2", target_bir_lowering=False, num_devices=1)
    args = {k: nc.dram_tensor(k, a.shape, mybir.dt.from_np(a.dtype), kind="ExternalInput").ap() for k, a in arrays.items()}
    out = nc.dram_tensor("out", (1, S, D), F32, kind="ExternalOutput").ap()
    trunk(nc, out=out, gamma_tile=gamma_tile, **args)
    result = run_bass_kernel_spmd(nc, [arrays], core_ids=[0])
    return result.results[0]["out"]
```
